# Optimizing a Trainium2 kernel written in Bass

```python
import jax, jax.numpy as jnp
from jax import lax
import numpy as np

D_MODEL = 2048
BATCH = 1
SEQ = 512
DEPTH = 1
DEC_BATCH = 8
DEC_SEQ = 8
PAST_LEN = 2048
PAGE_SIZE = 128

MLA_HEADS = 8
MLA_NOPE = 128
MLA_ROPE = 64
MLA_QK = MLA_NOPE + MLA_ROPE
MLA_V = 128
MLA_Q_RANK = 512
MLA_KV_RANK = 256
MLA_WIDTH = MLA_HEADS * MLA_V
MLA_SCALE = MLA_QK ** -0.5
ROPE_THETA = 10000.0
Q_BLOCK = 128
GLA_HEADS = 4
GLA_DK = 128
GLA_DV = 256
GLA_KEY = GLA_HEADS * GLA_DK
GLA_WIDTH = GLA_HEADS * GLA_DV
GLA_GATE_RANK = 16
GLA_TAU = 16.0
GLA_CHUNK = 64
MIX_WIDTH = MLA_WIDTH + GLA_WIDTH
IN_SPLITS = (MLA_Q_RANK, MLA_KV_RANK, MLA_ROPE, GLA_KEY, GLA_KEY, GLA_WIDTH, GLA_WIDTH, GLA_GATE_RANK)
IN_COLS = sum(IN_SPLITS)
PEER_HEADS = 8
PEER_N_KEYS = 128
PEER_EXPERTS = PEER_N_KEYS * PEER_N_KEYS
PEER_DKEY = 256
PEER_TOPK = 16
PEER_BLOCK = 64
PLE_DIM = 256
EPS = 1e-6

kernel_name = "hymba_mla_gla_peer_decode_step"

F32 = jnp.float32

def rmsnorm(x, g):
    x32 = x.astype(F32)
    y = x32 * lax.rsqrt(jnp.mean(jnp.square(x32), -1, keepdims=True) + EPS)
    return (y * g.astype(F32)).astype(x.dtype)

def rope(x, pos):
    half = x.shape[-1] // 2
    inv_freq = ROPE_THETA ** (-jnp.arange(half, dtype=F32) / half)
    ang = pos.astype(F32)[:, None] * inv_freq
    ang = ang.reshape((1, pos.shape[0]) + (1,) * (x.ndim - 3) + (half,))
    cos, sin = jnp.cos(ang), jnp.sin(ang)
    x32 = x.astype(F32)
    x1, x2 = x32[..., :half], x32[..., half:]
    return jnp.concatenate([x1 * cos - x2 * sin, x2 * cos + x1 * sin], -1).astype(x.dtype)

def mixer_inputs(x, w):
    xn = rmsnorm(x, w["norm_mix"])
    z = xn @ w["w_in"]
    cuts = [int(c) for c in np.cumsum(IN_SPLITS)[:-1]]
    return jnp.split(z, cuts, axis=-1)

def mla_qkv(cq_raw, ckv_raw, kr_raw, pos, w):
    B, T = cq_raw.shape[:2]
    cq = rmsnorm(cq_raw, w["norm_q_lat"])
    q = rmsnorm((cq @ w["w_uq"]).reshape(B, T, MLA_HEADS, MLA_QK), w["qk_gain_q"])
    q_nope, q_rope = q[..., :MLA_NOPE], rope(q[..., MLA_NOPE:], pos)
    c = rmsnorm(ckv_raw, w["norm_kv_lat"])
    k_nope = jnp.einsum("btr,rhd->bthd", c, w["w_uk"])
    ss = jnp.sum(jnp.square(k_nope.astype(F32)), -1) + jnp.sum(jnp.square(kr_raw.astype(F32)), -1)[..., None]
    inv_rms = lax.rsqrt(ss / MLA_QK + EPS).astype(c.dtype)
    kr = rope(kr_raw * w["qk_gain_k"][MLA_NOPE:], pos)
    return q_nope, q_rope, c, k_nope, kr, inv_rms

def mla_prompt(q_nope, q_rope, c, k_nope, kr, inv_rms, w):
    B, S = c.shape[:2]
    k = jnp.concatenate([k_nope * w["qk_gain_k"][:MLA_NOPE],
                         jnp.broadcast_to(kr[:, :, None], (B, S, MLA_HEADS, MLA_ROPE))], -1) * inv_rms[..., None]
    q = jnp.concatenate([q_nope, q_rope], -1)
    v = jnp.einsum("btr,rhd->bthd", c, w["w_uv"])
    nb = S // Q_BLOCK
    qb = jnp.moveaxis(q.reshape(B, nb, Q_BLOCK, MLA_HEADS, MLA_QK), 1, 0)
    key_pos = jnp.arange(S)

    def block(args):
        qi, bi = args
        s = jnp.einsum("bqhd,bshd->bhqs", qi, k).astype(F32) * MLA_SCALE
        qpos = bi * Q_BLOCK + jnp.arange(Q_BLOCK)
        s = jnp.where(key_pos[None, :] <= qpos[:, None], s, -jnp.inf)
        p = jax.nn.softmax(s, -1).astype(v.dtype)
        return jnp.einsum("bhqs,bshd->bqhd", p, v)

    o = lax.map(block, (qb, jnp.arange(nb)))
    return jnp.moveaxis(o, 0, 1).reshape(B, S, MLA_WIDTH)

def mla_sample(q_nope, q_rope, c, kr, inv_rms, lat_pool, kr_pool, ir_pool, page_table, w):
    B, T = c.shape[:2]
    past = page_table.shape[1] * lat_pool.shape[1]
    lat_p = lat_pool[page_table].reshape(B, past, MLA_KV_RANK)
    kr_p = kr_pool[page_table].reshape(B, past, MLA_ROPE)
    ir_p = ir_pool[page_table].reshape(B, past, MLA_HEADS)
    q_lat = jnp.einsum("bthd,rhd->bthr", q_nope * w["qk_gain_k"][:MLA_NOPE], w["w_uk"])

    def scores(lat, krr, ir):
        s = jnp.einsum("bthr,bsr->bhts", q_lat, lat) + jnp.einsum("bthd,bsd->bhts", q_rope, krr)
        return s.astype(F32) * jnp.transpose(ir, (0, 2, 1))[:, :, None, :].astype(F32) * MLA_SCALE

    causal = jnp.tril(jnp.ones((T, T), bool))
    s_all = jnp.concatenate([scores(lat_p, kr_p, ir_p), jnp.where(causal, scores(c, kr, inv_rms), -jnp.inf)], -1)
    p = jax.nn.softmax(s_all, -1).astype(c.dtype)
    o_lat = jnp.einsum("bhts,bsr->bthr", p[..., :past], lat_p) + jnp.einsum("bhts,bsr->bthr", p[..., past:], c)
    o = jnp.einsum("bthr,rhd->bthd", o_lat, w["w_uv"])
    return o.reshape(B, T, MLA_WIDTH)

def gla_inputs(qg, kg, vg, a_lr, w):
    B, T = qg.shape[:2]
    q = qg.reshape(B, T, GLA_HEADS, GLA_DK).astype(F32) * GLA_DK ** -0.5
    k = kg.reshape(B, T, GLA_HEADS, GLA_DK).astype(F32)
    v = vg.reshape(B, T, GLA_HEADS, GLA_DV).astype(F32)
    g = jax.nn.log_sigmoid((a_lr @ w["w_gla_a"] + w["b_gla_a"]).astype(F32)) / GLA_TAU
    return q, k, v, g.reshape(B, T, GLA_HEADS, GLA_DK)

def gla_chunk(S0, q, k, v, g):
    C = q.shape[1]
    b = jnp.cumsum(g, axis=1)
    b_last = b[:, -1]
    o_inter = jnp.einsum("bthk,bhkv->bthv", q * jnp.exp(b), S0)
    causal = jnp.tril(jnp.ones((C, C), bool))[None, :, :, None, None]
    decay = jnp.exp(jnp.where(causal, b[:, :, None] - b[:, None], -jnp.inf))
    A = jnp.einsum("bthk,bshk,btshk->bhts", q, k, decay)
    o = o_inter + jnp.einsum("bhts,bshv->bthv", A, v)
    S = jnp.exp(b_last)[..., None] * S0 + jnp.einsum("bshk,bshv->bhkv", k * jnp.exp(b_last[:, None] - b), v)
    return S, o

def gla_prompt(q, k, v, g):
    B, S = q.shape[:2]
    nc = S // GLA_CHUNK

    def to_chunks(a):
        return jnp.moveaxis(a.reshape((B, nc, GLA_CHUNK) + a.shape[2:]), 1, 0)

    S0 = jnp.zeros((B, GLA_HEADS, GLA_DK, GLA_DV), F32)
    S_fin, o = lax.scan(lambda s, xs: gla_chunk(s, *xs), S0, (to_chunks(q), to_chunks(k), to_chunks(v), to_chunks(g)))
    return jnp.moveaxis(o, 0, 1).reshape(B, S, GLA_HEADS, GLA_DV), S_fin

def gla_output(o, r, w, dtype):
    B, T = o.shape[:2]
    y = rmsnorm(o, w["norm_gla_out"]) * jax.nn.silu(r.reshape(B, T, GLA_HEADS, GLA_DV).astype(F32))
    return y.reshape(B, T, GLA_WIDTH).astype(dtype)

def peer(xn, w):
    B, T, D = xn.shape
    n = B * T
    nb = -(-n // PEER_BLOCK)
    xf = jnp.pad(xn.reshape(n, D), ((0, nb * PEER_BLOCK - n), (0, 0))).reshape(nb, PEER_BLOCK, D)

    def block(xb):
        q = (xb @ w["peer_w_q"]).reshape(PEER_BLOCK, PEER_HEADS, 2, PEER_DKEY // 2)
        s1 = jnp.einsum("thd,kd->thk", q[:, :, 0], w["peer_keys1"])
        s2 = jnp.einsum("thd,kd->thk", q[:, :, 1], w["peer_keys2"])
        v1, i1 = lax.top_k(s1, PEER_TOPK)
        v2, i2 = lax.top_k(s2, PEER_TOPK)
        cand = (v1[..., :, None] + v2[..., None, :]).reshape(PEER_BLOCK, PEER_HEADS, PEER_TOPK * PEER_TOPK)
        cidx = (i1[..., :, None] * PEER_N_KEYS + i2[..., None, :]).reshape(PEER_BLOCK, PEER_HEADS, PEER_TOPK * PEER_TOPK)
        top_s, sel = lax.top_k(cand, PEER_TOPK)
        e = jnp.take_along_axis(cidx, sel, -1)
        gate = jax.nn.softmax(top_s.astype(F32), -1)
        act = jax.nn.gelu(jnp.einsum("td,thkd->thk", xb, w["peer_u"][e]).astype(F32), approximate=False)
        coef = (gate * act).astype(xb.dtype)
        return jnp.einsum("thk,thkd->td", coef, w["peer_v"][e])

    y = lax.map(block, xf)
    return y.reshape(nb * PEER_BLOCK, D)[:n].reshape(B, T, D)

def finish_layer(x, mla_o, gla_o, p_i, w):
    mix = jnp.concatenate([rmsnorm(mla_o, w["norm_mla_out"]), gla_o], -1) @ w["w_out"]
    h = x + mix
    h = h + peer(rmsnorm(h, w["norm_ffn"]), w)
    gate = jax.nn.sigmoid((rmsnorm(h, w["norm_ple"]) @ w["w_ple_gate"]).astype(F32)).astype(h.dtype)
    return h + gate * (p_i @ w["w_ple_proj"])

def setup_inputs(seed: int = 0) -> dict:
    key = jax.random.key(seed)
    ks = jax.random.split(key, 40)
    n_pages = PAST_LEN // PAGE_SIZE
    n_used = DEC_BATCH * n_pages
    n_pool = n_used + max(1, n_used // 4)

    def nrm(i, shape, scale):
        return scale * jax.random.normal(ks[i], shape, F32)

    def gain(i, shape):
        return 1.0 + 0.02 * jax.random.normal(ks[i], shape, F32)

    page_table = jax.random.permutation(ks[39], n_pool)[:n_used].reshape(DEC_BATCH, n_pages).astype(jnp.int32)
    return {
        "x_prompt": nrm(0, (BATCH, SEQ, D_MODEL), 1.0),
        "x_sample": nrm(1, (DEC_BATCH, DEC_SEQ, D_MODEL), 1.0),
        "cache_kv_latent": nrm(2, (DEPTH, n_pool, PAGE_SIZE, MLA_KV_RANK), 1.0),
        "cache_k_rope": nrm(3, (DEPTH, n_pool, PAGE_SIZE, MLA_ROPE), 1.0),
        "cache_k_inv_rms": jax.random.uniform(ks[4], (DEPTH, n_pool, PAGE_SIZE, MLA_HEADS), F32, 0.5, 1.5),
        "state_gla": nrm(5, (DEPTH, DEC_BATCH, GLA_HEADS, GLA_DK, GLA_DV), 0.5),
        "page_table": page_table,
        "p_prompt": nrm(6, (DEPTH, BATCH, SEQ, PLE_DIM), 1.0),
        "p_sample": nrm(7, (DEPTH, DEC_BATCH, DEC_SEQ, PLE_DIM), 1.0),
        "norm_mix": gain(8, (DEPTH, D_MODEL)),
        "w_in": nrm(9, (DEPTH, D_MODEL, IN_COLS), D_MODEL ** -0.5),
        "norm_q_lat": gain(10, (DEPTH, MLA_Q_RANK)),
        "w_uq": nrm(11, (DEPTH, MLA_Q_RANK, MLA_HEADS * MLA_QK), MLA_Q_RANK ** -0.5),
        "norm_kv_lat": gain(12, (DEPTH, MLA_KV_RANK)),
        "w_uk": nrm(13, (DEPTH, MLA_KV_RANK, MLA_HEADS, MLA_NOPE), MLA_KV_RANK ** -0.5),
        "w_uv": nrm(14, (DEPTH, MLA_KV_RANK, MLA_HEADS, MLA_V), MLA_KV_RANK ** -0.5),
        "qk_gain_q": gain(15, (DEPTH, MLA_QK)),
        "qk_gain_k": gain(16, (DEPTH, MLA_QK)),
        "norm_mla_out": gain(17, (DEPTH, MLA_WIDTH)),
        "w_gla_a": nrm(18, (DEPTH, GLA_GATE_RANK, GLA_KEY), GLA_GATE_RANK ** -0.5),
        "b_gla_a": nrm(19, (DEPTH, GLA_KEY), 0.1),
        "norm_gla_out": gain(20, (DEPTH, GLA_DV)),
        "w_out": nrm(21, (DEPTH, MIX_WIDTH, D_MODEL), MIX_WIDTH ** -0.5),
        "norm_ffn": gain(22, (DEPTH, D_MODEL)),
        "peer_w_q": nrm(23, (DEPTH, D_MODEL, PEER_HEADS * PEER_DKEY), D_MODEL ** -0.5),
        "peer_keys1": nrm(24, (DEPTH, PEER_N_KEYS, PEER_DKEY // 2), (PEER_DKEY // 2) ** -0.5),
        "peer_keys2": nrm(25, (DEPTH, PEER_N_KEYS, PEER_DKEY // 2), (PEER_DKEY // 2) ** -0.5),
        "peer_u": nrm(26, (DEPTH, PEER_EXPERTS, D_MODEL), D_MODEL ** -0.5),
        "peer_v": nrm(27, (DEPTH, PEER_EXPERTS, D_MODEL), 0.3),
        "norm_ple": gain(28, (DEPTH, D_MODEL)),
        "w_ple_gate": nrm(29, (DEPTH, D_MODEL, D_MODEL), D_MODEL ** -0.5),
        "w_ple_proj": nrm(30, (DEPTH, PLE_DIM, D_MODEL), PLE_DIM ** -0.5),
    }

def reference(x_prompt, x_sample, cache_kv_latent, cache_k_rope, cache_k_inv_rms, state_gla, page_table,
              p_prompt, p_sample, norm_mix, w_in, norm_q_lat, w_uq, norm_kv_lat, w_uk, w_uv, qk_gain_q, qk_gain_k,
              norm_mla_out, w_gla_a, b_gla_a, norm_gla_out, w_out, norm_ffn, peer_w_q, peer_keys1, peer_keys2,
              peer_u, peer_v, norm_ple, w_ple_gate, w_ple_proj):
    S = x_prompt.shape[1]
    T = x_sample.shape[1]
    past_len = page_table.shape[1] * cache_kv_latent.shape[2]
    pos_p = jnp.arange(S, dtype=F32)
    pos_s = past_len + jnp.arange(T, dtype=F32)
    hp, hs = x_prompt, x_sample
    lat_p, kr_p, ir_p, gla_p = [], [], [], []
    lat_s, kr_s, ir_s, gla_s = [], [], [], []
    for i in range(DEPTH):
        w = {"norm_mix": norm_mix[i], "w_in": w_in[i], "norm_q_lat": norm_q_lat[i], "w_uq": w_uq[i],
             "norm_kv_lat": norm_kv_lat[i], "w_uk": w_uk[i], "w_uv": w_uv[i], "qk_gain_q": qk_gain_q[i],
             "qk_gain_k": qk_gain_k[i], "norm_mla_out": norm_mla_out[i], "w_gla_a": w_gla_a[i],
             "b_gla_a": b_gla_a[i], "norm_gla_out": norm_gla_out[i], "w_out": w_out[i], "norm_ffn": norm_ffn[i],
             "peer_w_q": peer_w_q[i], "peer_keys1": peer_keys1[i], "peer_keys2": peer_keys2[i],
             "peer_u": peer_u[i], "peer_v": peer_v[i], "norm_ple": norm_ple[i], "w_ple_gate": w_ple_gate[i],
             "w_ple_proj": w_ple_proj[i]}
        cq, ckv, kr_raw, qg, kg, vg, r, a_lr = mixer_inputs(hp, w)
        q_nope, q_rope, c, k_nope, kr, inv_rms = mla_qkv(cq, ckv, kr_raw, pos_p, w)
        mla_o = mla_prompt(q_nope, q_rope, c, k_nope, kr, inv_rms, w)
        gq, gk, gv, gg = gla_inputs(qg, kg, vg, a_lr, w)
        o, s_fin = gla_prompt(gq, gk, gv, gg)
        hp_next = finish_layer(hp, mla_o, gla_output(o, r, w, hp.dtype), p_prompt[i], w)
        lat_p.append(c)
        kr_p.append(kr)
        ir_p.append(inv_rms)
        gla_p.append(s_fin)
        cq, ckv, kr_raw, qg, kg, vg, r, a_lr = mixer_inputs(hs, w)
        q_nope, q_rope, c, k_nope, kr, inv_rms = mla_qkv(cq, ckv, kr_raw, pos_s, w)
        mla_o = mla_sample(q_nope, q_rope, c, kr, inv_rms, cache_kv_latent[i], cache_k_rope[i],
                           cache_k_inv_rms[i], page_table, w)
        gq, gk, gv, gg = gla_inputs(qg, kg, vg, a_lr, w)
        s_new, o = gla_chunk(state_gla[i].astype(F32), gq, gk, gv, gg)
        hs_next = finish_layer(hs, mla_o, gla_output(o, r, w, hs.dtype), p_sample[i], w)
        lat_s.append(c)
        kr_s.append(kr)
        ir_s.append(inv_rms)
        gla_s.append(s_new)
        hp, hs = hp_next, hs_next
    new_lat_p = jnp.stack(lat_p, 0)
    new_kr_p = jnp.stack(kr_p, 0)
    new_ir_p = jnp.stack(ir_p, 0)
    new_gla_p = jnp.stack(gla_p, 0)
    new_lat_s = jnp.stack(lat_s, 0)
    new_kr_s = jnp.stack(kr_s, 0)
    new_ir_s = jnp.stack(ir_s, 0)
    new_gla_s = jnp.stack(gla_s, 0)
    return (hp, hs, new_lat_p, new_kr_p, new_ir_p, new_gla_p, new_lat_s, new_kr_s, new_ir_s, new_gla_s)


_drawn_inputs = setup_inputs


def setup_inputs(seed=0):
    import zlib

    import numpy as np

    out = dict(_drawn_inputs(seed))
    spreads = {}
    factors = {'norm_q_lat': 3.189,
     'norm_kv_lat': 2.771,
     'qk_gain_q': 3.788,
     'qk_gain_k': 2.831,
     'norm_mla_out': 10.348,
     'norm_gla_out': 17.358,
     'norm_ffn': 11.164,
     'norm_ple': 64.0}
    for name, (base, spread) in spreads.items():
        noise = np.random.default_rng([zlib.crc32(name.encode()), seed]).standard_normal(out[name].shape)
        drawn = base * np.exp(spread * noise) if base else spread * noise
        out[name] = __import__('jax').numpy.asarray(drawn.astype(out[name].dtype))
    for name, factor in factors.items():
        out[name] = (out[name] * factor).astype(out[name].dtype)
    return out
```

```python
from contextlib import ExitStack

import numpy as np

import concourse.bass as bass
import concourse.mybir as mybir

ALU = mybir.AluOpType
ACT = mybir.ActivationFunctionType
AX = mybir.AxisListType.X
F32 = mybir.dt.float32
U32 = mybir.dt.uint32
I32 = mybir.dt.int32

P = 128
D = 2048
KD = D // P
SEQ = 512
DEC_B, DEC_T = 8, 8
NS = DEC_B * DEC_T
NTOK = SEQ + NS
PT = SEQ // P
T = PT + 1
ROWS = [P] * PT + [NS]
PAGE = 128
N_PAGES = 16
N_POOL = 160
PAST = PAGE * N_PAGES
H_MLA, NOPE, ROPE, DV = 8, 128, 64, 128
QK = NOPE + ROPE
QR, KVR = 512, 256
SCALE = QK ** -0.5
THETA = 10000.0
H_GLA, GK, GV = 4, 128, 256
GATE_R = 16
TAU = 16.0
IN_SPLITS = (QR, KVR, ROPE, H_GLA * GK, H_GLA * GK, H_GLA * GV, H_GLA * GV, GATE_R)
IN_COLS = sum(IN_SPLITS)
MLA_COLS = QR + KVR + ROPE
GLA_COLS = IN_COLS - MLA_COLS
IN_BLOCKS = 8
IN_NC = IN_COLS // IN_BLOCKS
NC = 512
NBLK = D // NC
PH, NKEY, TOPK = 8, 128, 16
PLE = 256
EPS = 1e-6
NEG = -1e30
LOWEST = -3e38
LEVELS = [64, 32, 16, 8, 4, 2, 1]
NLEV = len(LEVELS) + 1
SAMPLE_LEVEL0 = LEVELS.index(DEC_T // 2)
UNITS = PH * PT + PH // 2
LANDED = {"in": 0, "out": IN_BLOCKS // 2, "peer_q": IN_BLOCKS // 2 + NBLK // 2, "gate": IN_BLOCKS // 2 + NBLK // 2 + PH // 2}
SERVED = {"in": 0, "out": IN_BLOCKS * T, "gate": IN_BLOCKS * T + NBLK * T}
RING = 8


def constants():
    i = np.arange(P)
    c = {"ident": np.eye(P, dtype=np.float32)}
    c["tri"] = (i[:, None] <= i[None, :]).astype(np.float32)
    j = np.arange(NS)
    same = (j[:, None] // DEC_T) == (j[None, :] // DEC_T)
    tri_s = np.zeros((P, NS), np.float32)
    tri_s[:NS] = (j[:, None] <= j[None, :]) & same
    c["tri_s"] = tri_s
    lev = np.zeros((P, NLEV, P), np.float32)
    for n, half in enumerate(LEVELS):
        s, t = i[:, None], i[None, :]
        lev[:, n] = (s // (2 * half) == t // (2 * half)) & (s % (2 * half) < half) & (t % (2 * half) >= half)
    lev[:, NLEV - 1] = np.eye(P)
    c["lev"] = lev
    c["causal"] = np.where(i[None, :] <= i[:, None], 0.0, NEG).astype(np.float32)
    m = np.full((P, DEC_B, DEC_B, DEC_T), NEG, np.float32)
    for b in range(DEC_B):
        for h in range(H_MLA):
            for t in range(DEC_T):
                m[h * DEC_T + t, b, b, :t + 1] = 0.0
    c["smask"] = m.reshape(P, DEC_B * NS)
    bm = np.zeros((P, DEC_B), np.float32)
    bm[j, j // DEC_T] = 1.0
    c["bmask"] = bm
    half = ROPE // 2
    inv = np.float32(THETA) ** (-np.arange(half, dtype=np.float32) / np.float32(half))
    pos = np.zeros((P, T), np.float32)
    for t in range(PT):
        pos[:, t] = t * P + i
    pos[:NS, PT] = PAST + j % DEC_T
    ang = pos[:, :, None] * inv
    cos, sin = np.cos(ang), np.sin(ang)
    c["cos"] = np.concatenate([cos, cos], -1).astype(np.float32)
    c["sin"] = np.concatenate([-sin, sin], -1).astype(np.float32)
    c["iota16"] = np.tile(np.arange(TOPK, dtype=np.float32), (P, 1))
    return c


def build(nc, a, o, c):
    ctx = ExitStack()
    with ctx:
        sems = {}

        def s(name):
            if name not in sems:
                sems[name] = nc.alloc_semaphore(name)
            return sems[name]

        def sb(name, shape, dt=F32):
            return ctx.enter_context(nc.sbuf_tensor(name, shape, dt))

        XT = sb("XT", [P, KD, NTOK])
        work = sb("work", [P, 38912])
        used = [0]

        def carve(*shape):
            n = int(np.prod(shape))
            ap = work[:, used[0]:used[0] + n]
            used[0] += n
            assert used[0] <= 38912, used[0]
            if len(shape) == 2:
                ap = ap.rearrange("p (a b) -> p a b", b=shape[1])
            if len(shape) == 3:
                ap = ap.rearrange("p (a b c) -> p a b c", b=shape[1], c=shape[2])
            return ap

        H = carve(T, D)
        X2 = carve(T, D)
        WRf = carve(2 * KD * 512)
        G = carve(D)
        WR = [WRf[:, p * KD * 512:(p + 1) * KD * 512] for p in range(2)]
        ring = WRf.rearrange("p (b n) -> p b n", b=RING)
        zst = H.rearrange("p a b -> p (a b)")[:, 0:10 * 512].rearrange("p (s n) -> p s n", s=10)
        rt = WRf[:, KD * 512:]
        topv = rt[:, 0:T * 16 * TOPK].rearrange("p (t c k) -> p t c k", t=T, k=TOPK)
        topi = rt[:, T * 256:2 * T * 256].rearrange("p (t c k) -> p t c k", t=T, k=TOPK)
        swork = rt[:, 2560:2560 + T * P].rearrange("p (t k) -> p t k", t=T)
        topu = rt[:, 3200:3200 + T * TOPK].bitcast(U32).rearrange("p (t k) -> p t k", t=T)
        qTm = rt[:, 3280:3280 + 2 * NTOK].rearrange("p (s k) -> p s k", s=2)
        keysT = rt[:, 4432:4432 + 2 * P].rearrange("p (s k) -> p s k", s=2)
        keysR = rt[:, 4688:4688 + 2 * P].rearrange("p (s k) -> p s k", s=2)
        sela = rt[:, 5000:5000 + 128].bitcast(U32)
        selh = rt[:, 5128:5128 + 128].bitcast(U32)
        sell = rt[:, 5256:5256 + 128].bitcast(U32)
        selhf = rt[:, 5384:5384 + 128]
        sellf = rt[:, 5512:5512 + 128]
        e1 = rt[:, 5640:5640 + 128]
        e2 = rt[:, 5768:5768 + 128]
        gsum = rt[:, 5896:5896 + 8]
        gtop = rt[:, 5904:5904 + 128]
        XTf = XT[:, :, :].rearrange("p a b -> p (a b)")
        cand = XTf[:, 0:2048]
        candw = XTf[:, 2048:4096]
        oneh = XTf[:, 4096:6144]
        acc1 = XTf[:, 6144:8192]

        ixs_hi = rt[0:NS, 6100:6100 + 64].bitcast(U32)
        gts_hi = rt[0:NS, 6164:6164 + 64]

        used[0] = 0
        m_z = carve(MLA_COLS)
        w_uq = carve(QR // P, H_MLA * QK)
        w_uk = carve(KVR // P, H_MLA * NOPE)
        w_uv = carve(KVR // P, H_MLA * DV)
        KTn = carve(H_MLA, SEQ)
        KTr = carve(H_MLA // 2, SEQ)
        V = carve(PT, H_MLA * DV)
        cT = carve(KVR // P, NTOK)
        c_smp = carve(KVR)
        g_q, g_kv, g_k, g_qk, g_mla = carve(QR), carve(KVR), carve(QK), carve(QK), carve(H_MLA * DV)
        base = used[0]
        cqn = carve(QR)
        cqT = carve(QR // P, P)
        qrow = carve(H_MLA, QK)
        krow = carve(H_MLA, NOPE)
        sqs = carve(H_MLA * QK)
        qro, kro = carve(H_MLA, ROPE), carve(H_MLA, ROPE)
        rtmp = carve(H_MLA, ROPE)
        kr_g, kr_o = carve(ROPE), carve(ROPE)
        QTn = carve(H_MLA, P)
        QTr = carve(H_MLA // 2, P)
        pr = carve(2, SEQ)
        pT = carve(2, SEQ)
        orow = carve(H_MLA * DV)
        onrm = carve(H_MLA * DV)
        used[0] = MLA_COLS
        latb = carve(N_PAGES, KVR)
        krb = carve(N_PAGES, ROPE)
        irb = carve(N_PAGES, H_MLA)
        assert used[0] <= MLA_COLS + 4 * H_MLA * QK
        used[0] = MLA_COLS + 4 * H_MLA * QK + 4 * 1024
        w_ukT = carve(H_MLA, KVR)
        latT = carve(3, 512)
        irs = pT.rearrange("p a b -> p (a b)")[:, 0:512]
        sc = carve(PAST + NS)
        pTs = carve(N_PAGES + 1, NS)
        q_lat0, q_lat1 = carve(H_MLA, NS), carve(H_MLA, NS)
        q_lat = [q_lat0, q_lat1]
        qrT = carve(H_MLA, NS)
        qgT = carve(H_MLA, NS)
        olr = pr.rearrange("p a b -> p (a b)")[:, 0:KVR]
        oT0, oT1 = carve(H_MLA, NS), carve(H_MLA, NS)
        oT = [oT0, oT1]
        assert used[0] <= MLA_COLS + 4 * 1536 + 4 * 1024 + 4096 + 2048 + 4096, used[0]
        used[0] = 0
        gz = carve(GLA_COLS)
        w_ga = carve(H_GLA * GK)
        b_ga = carve(H_GLA * GK)
        g_go = carve(GV)
        S0 = carve(H_GLA, GV)
        Ss = carve(DEC_B * H_GLA, GV)
        gx, gt1, gt2 = carve(H_GLA * GK), carve(H_GLA * GK), carve(H_GLA * GK)
        alT = carve(P)
        gqT, gkT, gbT = carve(H_GLA * GK), carve(H_GLA * GK), carve(H_GLA * GK)
        Mlev = carve(NLEV, H_GLA * P)
        dlev = carve(2, H_GLA * P)
        am = carve(2, NLEV * P)
        AT = carve(H_GLA, P)
        eb = carve(H_GLA * P)
        qe = carve(H_GLA * P)
        kd = carve(H_GLA * P)
        kdr = carve(H_GLA, GK)
        go = carve(H_GLA * GV)
        gsil = carve(H_GLA * GV)
        gsq = carve(H_GLA * GV)
        qz = carve(DEC_B, NS)
        kz = carve(DEC_B, GK)
        eL = carve(H_GLA * DEC_B)
        used[0] = T * D
        pT_ple = carve(PLE // P, NTOK)
        w_pp = carve(PLE // P, D)
        p_row = carve(T, PLE)
        sg = carve(2, NC)
        assert used[0] <= 2 * T * D

        ident = sb("ident", [P, P])
        tri, tri_s = sb("tri", [P, P]), sb("tri_s", [P, NS])
        lev = sb("lev", [P, NLEV, P])
        causal = sb("causal", [P, P])
        smask = sb("smask", [P, DEC_B, NS])
        bmask = sb("bmask", [P, DEC_B])
        cosT, sinT = sb("cosT", [P, T, ROPE]), sb("sinT", [P, T, ROPE])
        iota16 = sb("iota16", [P, TOPK])
        pages = sb("pages", [1, DEC_B * N_PAGES], I32)
        eps = sb("eps", [P, 1])
        ones = sb("ones", [1, P])
        idx_all = sb("idx_all", [P, UNITS * TOPK], U32)
        gate_all = sb("gate_all", [P, UNITS * TOPK])
        idx_cur = sb("idx_cur", [P, 2, TOPK], U32)
        dots, gel, coef = sb("dots", [P, TOPK]), sb("gel", [P, TOPK]), sb("coef", [P, TOPK])
        st = sb("st", [P, 3 * T + 3 * T + 3 * T])
        ms = sb("ms", [P, 100])

        bank = [ctx.enter_context(nc.psum_tensor(f"bank{i}", [P, 512], F32)) for i in range(8)]

        z_dram = nc.dram_tensor("z_dram", [NTOK, IN_COLS], F32).ap()

        def rows(t):
            return slice(t * P, t * P + ROWS[t])

        def x_rows(t):
            return a["x_prompt"][0, t * P:(t + 1) * P, :] if t < PT else a["x_sample"].rearrange("b t d -> (b t) d")

        def bc(ap, *shape):
            return ap.to_broadcast(list(shape))

        def down(dram_row, n):
            return dram_row.partition_broadcast(n)

        SSQ, RQ, IQ = ms[:, 0:1], ms[:, 1:2], ms[:, 2:3]
        SSC, RC, IC = ms[:, 3:4], ms[:, 4:5], ms[:, 5:6]
        SKR = ms[:, 6:7]
        SQH, RQH, IQH = ms[:, 8:16], ms[:, 16:24], ms[:, 24:32]
        SKH, RKH, IKH = ms[:, 32:40], ms[:, 40:48], ms[:, 48:56]
        MXV, NMX, RSUM, RINV = ms[:, 56:64], ms[:, 64:72], ms[:, 72:80], ms[:, 80:88]
        SSO, RSO, ISO = ms[:, 88:89], ms[:, 89:90], ms[:, 90:91]
        GSS, GRS, GIS = ms[:, 8:12], ms[:, 12:16], ms[:, 16:20]

        def by_batch(ap):
            return ap.rearrange("p b (h t) -> p h b t", h=H_MLA)

        ire = sqs[:, 0:N_PAGES * NS].rearrange("p (g n) -> p g n", n=NS)
        ikx = cqn[:, 0:NS]
        irs_new = rtmp.rearrange("p a b -> p (a b)")[:, 0:NS]

        def heads(ap, R):
            return ap[:, 0:H_GLA * P].rearrange("p (h n) -> p h n", h=H_GLA)[:, :, 0:R]


        def level_count(t, n):
            per = NLEV - 1
            return t * per + n if t < PT else PT * per + n - SAMPLE_LEVEL0


        def sample_attention(e):
            for h in range(H_MLA):
                for k in range(2):
                    j = h * 2 + k
                    if j % 4 == 0 and j >= 4:
                        e.wait_ge(s("sprep_act"), j // 4)
                    mm = e.transpose(bank[0][:, (j % 4) * P:(j % 4 + 1) * P], w_uk[:, k, h * NOPE:(h + 1) * NOPE], ident[:, :])
                    if j % 4 == 3:
                        mm.then_inc(s("sprep_psum"), 1)
            e.wait_ge(s("q_rows_ready"), T)
            for h in range(H_MLA):
                e.transpose(bank[2][:, h * NS:(h + 1) * NS], qrow[:NS, h, 0:NOPE], ident[:NS, :NS])
            for h in range(H_MLA):
                mm = e.transpose(bank[3][0:ROPE, h * NS:(h + 1) * NS], qro[:NS, h, :], ident[:NS, :NS])
            mm.then_inc(s("sprep_psum"), 1)
            e.wait_ge(s("sprep_dve"), 1)
            e.wait_ge(s("sprep_act"), 4)
            for k in range(2):
                for h in range(H_MLA):
                    mm = e.matmul(bank[4 + k][:, h * NS:(h + 1) * NS], w_ukT[:, h, k * P:(k + 1) * P], qgT[:, h, :],
                                  start=True, stop=True)
            mm.then_inc(s("sprep_psum"), 1)
            e.wait_ge(s("k_rows_ready"), T)
            e.transpose(bank[6][0:ROPE, 0:NS], kr_o[:NS, :], ident[:NS, :NS]).then_inc(s("sprep_psum"), 1)
            e.wait_ge(s("sprep_dve"), 2)
            e.wait_ge(s("sprep_act"), 5)

            def qb(q, b):
                return q[:, b, :]

            for b in range(DEC_B):
                e.wait_ge(s("pages_landed"), 16 * 3 * N_PAGES * (b + 1))
                for g in range(4):
                    u = 4 * b + g
                    if u:
                        e.wait_ge(s("latT_sb"), u)
                    for j in range(4):
                        pg = 4 * g + j
                        for k in range(2):
                            e.transpose(bank[k][:, j * P:(j + 1) * P], latb[:, pg, k * P:(k + 1) * P], ident[:, :])
                        mm = e.transpose(bank[2][0:ROPE, j * P:(j + 1) * P], krb[:, pg, :], ident[:, :])
                    mm.then_inc(s("latT_psum"), 1)
                    if u:
                        e.wait_ge(s("ir_sb"), u)
                    if g == 0:
                        e.wait_ge(s("ire_ready"), b + 1)
                    for j in range(4):
                        pg = 4 * g + j
                        mm = e.matmul(bank[3][0:NS, j * P:(j + 1) * P], ire[:, pg, :],
                                      ident[:, :], start=True, stop=True)
                    mm.then_inc(s("ir_psum"), 1)
                    e.wait_ge(s("latT_sb"), u + 1)
                    if u:
                        e.wait_ge(s("scaled"), u)
                    e.matmul(bank[4][0:NS, :], qb(q_lat[0], b), latT[:, 0, :], start=True, stop=False)
                    e.matmul(bank[4][0:NS, :], qb(q_lat[1], b), latT[:, 1, :], start=False, stop=False)
                    e.matmul(bank[4][0:NS, :], qb(qrT[0:ROPE], b), latT[0:ROPE, 2, :], start=False, stop=True)\
                        .then_inc(s("sscore_psum"), 1)
                e.wait_ge(s("ikx_ready"), 1)
                if b:
                    e.wait_ge(s("snew_done"), b)
                e.matmul(bank[5][0:NS, 0:NS], qb(q_lat[0], b), cT[:, 0, SEQ:NTOK], start=True, stop=False)
                e.matmul(bank[5][0:NS, 0:NS], qb(q_lat[1], b), cT[:, 1, SEQ:NTOK], start=False, stop=False)
                e.matmul(bank[5][0:NS, 0:NS], qb(qrT[0:ROPE], b), irs_new[0:ROPE, :], start=False, stop=True)
                e.matmul(bank[5][0:NS, NS:2 * NS], ikx[:NS, :], ident[:NS, :NS],
                         start=True, stop=True).then_inc(s("snew_psum"), 1)
                e.wait_ge(s("sexp_done"), b + 1)
                for q in range(3):
                    v = 3 * b + q
                    if v:
                        e.wait_ge(s("spT_sb"), v)
                    for pg in range(8 * q, min(8 * q + 8, N_PAGES + 1)):
                        w = P if pg < N_PAGES else NS
                        mm = e.transpose(bank[6][:w, (pg % 8) * NS:(pg % 8 + 1) * NS], sc[:NS, pg * P:pg * P + w], ident[:NS, :NS])
                    mm.then_inc(s("spT_psum"), 1)
                e.wait_ge(s("spT_sb"), 3 * b + 3)
                for pg in range(N_PAGES):
                    mm = e.matmul(bank[7][0:NS, 0:KVR], pTs[:, pg, :], latb[:, pg, :], start=(pg == 0), stop=False)
                e.matmul(bank[7][0:NS, 0:KVR], pTs[:NS, N_PAGES, :], c_smp[:NS, :], start=False, stop=True)\
                    .then_inc(s("olat_psum"), 1)
                e.wait_ge(s("olat_sb"), b + 1)
                for k in range(2):
                    mm = e.transpose(bank[7][:, 256 + k * NS:256 + (k + 1) * NS], olr[:NS, k * P:(k + 1) * P], ident[:NS, :NS])
                mm.then_inc(s("olatT_psum"), 1)
                e.wait_ge(s("pages_used"), b + 1)
            for h in range(H_MLA):
                for k in range(2):
                    mm = e.matmul(bank[3 + h // 4][:NS, (h % 4) * DV:(h % 4 + 1) * DV], oT[k][:, h, :],
                                  w_uv[:, k, h * DV:(h + 1) * DV], start=(k == 0), stop=(k == 1))
            mm.then_inc(s("sprep_psum"), 1)


        def sample_act(e, link):
            for j in range(4):
                e.wait_ge(s("sprep_psum"), j + 1)
                e.copy(w_ukT[:, 2 * j:2 * j + 2, :].rearrange("p h n -> p (h n)"), bank[0][:, :]).then_inc(s("sprep_act"), 1)
            e.wait_ge(s("sprep_psum"), 6)
            for k in range(2):
                ins = e.copy(by_batch(q_lat[k]), bank[4 + k][:, :].rearrange("p (h b t) -> p h b t", h=H_MLA, b=DEC_B))
            ins.then_inc(s("sprep_act"), 1)
            for b in range(DEC_B):
                for g in range(4):
                    u = 4 * b + g
                    e.wait_ge(s("latT_psum"), u + 1)
                    if u:
                        e.wait_ge(s("sscore_psum"), u)
                    e.copy(latT[:, 0, :], bank[0][:, :])
                    e.copy(latT[:, 1, :], bank[1][:, :])
                    e.copy(latT[0:ROPE, 2, :], bank[2][0:ROPE, :]).then_inc(s("latT_sb"), 1)
                    e.wait_ge(s("ir_psum"), u + 1)
                    if u:
                        e.wait_ge(s("scaled"), u)
                    e.copy(irs[:NS, :], bank[3][:NS, :]).then_inc(s("ir_sb"), 1)
                e.wait_ge(s("sneg_max"), b + 1)
                e.activation(sc[:NS, :], sc[:NS, :], ACT.Exp, scale=SCALE, bias=NMX[:NS, 0:1], accum_out=RSUM[:NS, 0:1])\
                    .then_inc(s("sexp_done"), 1)
                for q in range(3):
                    v = 3 * b + q
                    n = 8 if q < 2 else 1
                    R = P if q < 2 else NS
                    e.wait_ge(s("spT_psum"), v + 1)
                    if b and q == 0:
                        e.wait_ge(s("olat_psum"), b)
                    e.copy(pTs[:R, 8 * q:8 * q + n, :].rearrange("p a b -> p (a b)"), bank[6][:R, 0:n * NS]).then_inc(s("spT_sb"), 1)
                e.wait_ge(s("olatT_psum"), b + 1)
                for k in range(2):
                    ins = e.copy(oT[k][:, :, b * DEC_T:(b + 1) * DEC_T],
                                 bank[7][:, 256 + k * NS:256 + (k + 1) * NS].rearrange("p (h t) -> p h t", h=H_MLA))
                ins.then_inc(s("pages_used"), 1)


        def sample_state(h):
            e = nc.vector
            for b in range(DEC_B):
                upd = bank[b // 2][:, (b % 2) * GV:(b % 2 + 1) * GV]
                st_ = Ss[:, b * H_GLA + h, :]
                ins = e.scalar_tensor_tensor(out=st_, in0=st_, scalar=eL[:, h * DEC_B + b:h * DEC_B + b + 1], in1=upd,
                                             op0=ALU.mult, op1=ALU.add)
            ins.then_inc(s("sample_state_head"), 1)


        def sample_dve(e, link):
            e.wait_ge(s("sprep_psum"), 5)
            e.tensor_copy(qgT, bank[2][:, :].rearrange("p (h n) -> p h n", h=H_MLA))
            e.tensor_copy(by_batch(qrT[0:ROPE]), bank[3][0:ROPE, :].rearrange("p (h b t) -> p h b t", h=H_MLA, b=DEC_B))\
                .then_inc(s("sprep_dve"), 1)
            e.wait_ge(s("sprep_psum"), 7)
            e.tensor_copy(irs_new[0:ROPE, :], bank[6][0:ROPE, 0:NS]).then_inc(s("sprep_dve"), 1)
            for b in range(DEC_B):
                for g in range(4):
                    u = 4 * b + g
                    e.wait_ge(s("sscore_psum"), u + 1)
                    e.wait_ge(s("ir_sb"), u + 1)
                    if b and g == 0:
                        e.wait_ge(s("spT_psum"), 3 * b)
                    e.tensor_tensor(sc[:NS, g * 512:(g + 1) * 512], bank[4][:NS, :], irs[:NS, :], ALU.mult).then_inc(s("scaled"), 1)
                e.wait_ge(s("snew_psum"), b + 1)
                link(e.tensor_copy(sc[:NS, PAST:PAST + NS], bank[5][:NS, NS:2 * NS]))
                link(e.tensor_tensor(sc[:NS, PAST:PAST + NS], sc[:NS, PAST:PAST + NS], bank[5][:NS, 0:NS], ALU.mult))
                e.tensor_tensor(sc[:NS, PAST:PAST + NS], sc[:NS, PAST:PAST + NS], smask[:NS, b, :], ALU.add).then_inc(s("snew_done"), 1)
                e.wait_ge(s("snew_done"), b + 1)
                e.wait_ge(s("scaled"), 4 * b + 4)
                link(e.tensor_reduce(MXV[:NS, 0:1], sc[:NS, :], AX, ALU.max))
                e.tensor_scalar(NMX[:NS, 0:1], MXV[:NS, 0:1], -SCALE, None, ALU.mult).then_inc(s("sneg_max"), 1)
                e.wait_ge(s("sexp_done"), b + 1)
                link(e.reciprocal(RINV[:NS, 0:1], RSUM[:NS, 0:1]))
                e.wait_ge(s("olat_psum"), b + 1)
                e.tensor_scalar(olr[:NS, :], bank[7][:NS, 0:KVR], RINV[:NS, 0:1], None, ALU.mult).then_inc(s("olat_sb"), 1)
            e.wait_ge(s("sprep_psum"), 8)
            for n in range(2):
                ins = e.tensor_copy(orow[:NS, n * 512:(n + 1) * 512], bank[3 + n][:NS, :])
            ins.then_inc(s("mla_o_rows"), 1)


        block = ctx.enter_context(nc.Block())

        @block.sync
        def _(e):
            for name, dst in (("ident", ident), ("tri", tri), ("tri_s", tri_s), ("lev", lev), ("causal", causal),
                              ("bmask", bmask), ("cos", cosT), ("sin", sinT), ("iota16", iota16)):
                v = dst[:, :] if name not in ("lev", "cos", "sin") else dst[:, :, :]
                e.dma_start(v, c[name]).then_inc(s("consts_loaded"), 16)
            e.dma_start(smask[:, :, :].rearrange("p a b -> p (a b)"), c["smask"]).then_inc(s("consts_loaded"), 16)
            e.dma_start(pages[:, :], a["page_table"].rearrange("b n -> (b n)").rearrange("(o n) -> o n", o=1))\
                .then_inc(s("consts_loaded"), 16)
            for t in range(T):
                e.dma_start(H[:ROWS[t], t, :], x_rows(t)).then_inc(s("x_loaded"), 16)
            e.dma_start(G[:, :], down(a["norm_mix"][0], P)).then_inc(s("gain_loaded"), 16)

            def weight_blocks(name, w, ncol, nblk):
                def load(i, p):
                    e.dma_start(WR[p][:, 0:KD * ncol].rearrange("p (k n) -> p k n", k=KD),
                                w[:, bass.ds((i * 2 + p) * ncol, ncol)].rearrange("(k p) n -> p k n", p=P))\
                        .then_inc(s(f"w_landed{p}"), 16)
                load(0, 0)
                load(0, 1)
                with e.Fori(1, nblk // 2) as i:
                    for p in range(2):
                        e.wait_ge(s("tiles_projected"), (i * 2 + p - 1) * T + SERVED[name])
                        load(i, p)

            weight_blocks("in", a["w_in"][0], IN_NC, IN_BLOCKS)

            e.wait_ge(s("z_written"), 1)
            for dst, src in ((w_uq, a["w_uq"][0].rearrange("(k p) n -> p k n", p=P)),
                             (w_uk, a["w_uk"][0].rearrange("(k p) h d -> p k (h d)", p=P)),
                             (w_uv, a["w_uv"][0].rearrange("(k p) h d -> p k (h d)", p=P)),
                             (g_q, down(a["norm_q_lat"][0], P)), (g_kv, down(a["norm_kv_lat"][0], P)),
                             (g_k, down(a["qk_gain_k"][0], P)), (g_qk, down(a["qk_gain_q"][0], P)),
                             (g_mla, down(a["norm_mla_out"][0], P))):
                e.dma_start(dst, src).then_inc(s("weights_loaded"), 16)
            for t in range(T):
                R = ROWS[t]
                if t:
                    e.wait_ge(s("mla_keys_ready"), t)
                e.dma_start(m_z[:R, :], z_dram[rows(t), 0:MLA_COLS]).then_inc(s("mla_z_loaded"), 16)
                lat = o["lat_p"][0, 0, rows(t), :] if t < PT else o["lat_s"][0].rearrange("b t d -> (b t) d")
                krd = o["kr_p"][0, 0, rows(t), :] if t < PT else o["kr_s"][0].rearrange("b t d -> (b t) d")
                ird = o["ir_p"][0, 0, rows(t), :] if t < PT else o["ir_s"][0].rearrange("b t d -> (b t) d")
                e.wait_ge(s("mla_latents_normed"), t + 1)
                e.dma_start(lat, c_smp[:R, :]).then_inc(s("mla_outputs"), 16)
                e.wait_ge(s("mla_keys_ready"), t + 1)
                e.dma_start(krd, kr_o[:R, :]).then_inc(s("mla_outputs"), 16)
                e.dma_start(ird, IKH[:R, :]).then_inc(s("mla_outputs"), 16)

            e.wait_ge(s("sprep_dve"), 2)
            for b in range(DEC_B):
                if b:
                    e.wait_ge(s("pages_used"), b)
                for g in range(N_PAGES):
                    pg = e.value_load(pages[0:1, b * N_PAGES + g:b * N_PAGES + g + 1], min_val=0, max_val=N_POOL - 1)
                    e.dma_start(latb[:, g, :], a["cache_kv_latent"][0, bass.ds(pg, 1), :, :].rearrange("o p d -> (o p) d"))\
                        .then_inc(s("pages_landed"), 16)
                    e.dma_start(krb[:, g, :], a["cache_k_rope"][0, bass.ds(pg, 1), :, :].rearrange("o p d -> (o p) d"))\
                        .then_inc(s("pages_landed"), 16)
                    e.dma_start(irb[:, g, :], a["cache_k_inv_rms"][0, bass.ds(pg, 1), :, :].rearrange("o p d -> (o p) d"))\
                        .then_inc(s("pages_landed"), 16)

            e.wait_ge(s("mla_done"), T)
            e.wait_ge(s("mla_outputs"), 16 * 3 * T)
            e.dma_start(w_ga[0:GATE_R, :], a["w_gla_a"][0]).then_inc(s("weights_loaded"), 16)
            e.dma_start(b_ga[0:1, :], a["b_gla_a"][0].rearrange("(o n) -> o n", o=1)).then_inc(s("weights_loaded"), 16)
            e.dma_start(g_go[:, :], down(a["norm_gla_out"][0], P)).then_inc(s("weights_loaded"), 16)
            e.dma_start(Ss, a["state_gla"][0].rearrange("b h k v -> k (b h) v")).then_inc(s("weights_loaded"), 16)
            for t in range(T):
                if t:
                    e.wait_ge(s("gla_done"), t)
                e.dma_start(gz[:ROWS[t], :], z_dram[rows(t), MLA_COLS:IN_COLS]).then_inc(s("gla_z_loaded"), 16)
                if t == PT:
                    e.wait_ge(s("gla_state"), H_GLA * PT)
                    e.dma_start(o["gla_p"][0, 0].rearrange("h k v -> k h v"), S0).then_inc(s("state_out"), 16)
            e.wait_ge(s("sample_state_head"), H_GLA)
            e.dma_start(o["gla_s"][0].rearrange("b h k v -> k (b h) v"), Ss).then_inc(s("state_out"), 16)

            e.wait_ge(s("gla_done"), T)
            e.wait_ge(s("state_out"), 32)
            for t in range(T):
                e.dma_start(H[:ROWS[t], t, :], x_rows(t)).then_inc(s("x_loaded"), 16)
            e.dma_start(G[:, :], down(a["norm_ffn"][0], P)).then_inc(s("gain_loaded"), 16)
            weight_blocks("out", a["w_out"][0], NC, NBLK)

            e.wait_ge(s("tiles_projected"), SERVED["gate"])
            e.dma_start(keysR[:, 0, :], a["peer_keys1"][0]).then_inc(s("weights_loaded"), 16)
            e.dma_start(keysR[:, 1, :], a["peer_keys2"][0]).then_inc(s("weights_loaded"), 16)
            for h in range(PH):
                if h >= 2:
                    e.wait_ge(s("q_psum_ready"), 2 * (h - 1))
                e.dma_start(WR[0][:, (h % 2) * KD * 256:(h % 2 + 1) * KD * 256].rearrange("p (k n) -> p k n", k=KD),
                            a["peer_w_q"][0][:, h * 256:(h + 1) * 256].rearrange("(k p) n -> p k n", p=P))\
                    .then_inc(s(f"w_landed{h % 2}"), 16)
            e.wait_ge(s("route_ready"), T)
            lo = slice(8 * PT * TOPK, UNITS * TOPK)
            e.dma_start(idx_all[NS:P, lo], ixs_hi).then_inc(s("sample_spread"), 16)
            e.dma_start(gate_all[NS:P, lo], gts_hi).then_inc(s("sample_spread"), 16)
            e.dma_start(X2[NS:P, PT, :], X2[0:NS, PT, :]).then_inc(s("sample_spread"), 16)

            e.wait_ge(s("sample_halves"), 1)
            e.dma_start(acc1[0:NS, :], H[NS:P, PT, :]).then_inc(s("sample_back"), 16)

            e.wait_ge(s("peer_done"), T)
            e.dma_start(G[:, :], down(a["norm_ple"][0], P)).then_inc(s("gain_loaded"), 16)
            e.wait_ge(s("nt_evacuated"), 4 * T * 3)
            e.dma_start(w_pp, a["w_ple_proj"][0].rearrange("(k p) n -> p k n", p=P)).then_inc(s("weights_loaded"), 16)
            for t in range(T):
                src = a["p_prompt"][0, 0, rows(t), :] if t < PT else a["p_sample"][0].rearrange("b t d -> (b t) d")
                e.dma_start(p_row[:ROWS[t], t, :], src).then_inc(s("weights_loaded"), 16)
            weight_blocks("gate", a["w_ple_gate"][0], NC, NBLK)
            for t in range(T):
                e.wait_ge(s("gate_bank_free"), T + (NBLK - 1) * T + t + 1)
                dst = o["y_p"][0, rows(t), :] if t < PT else o["y_s"].rearrange("b t d -> (b t) d")
                e.dma_start(dst, H[:ROWS[t], t, :]).then_inc(s("y_out"), 16)
            e.wait_ge(s("y_out"), 16 * T)
            e.wait_ge(s("mla_outputs"), 16 * 3 * T)
            e.wait_ge(s("state_out"), 32)

        @block.tensor
        def _(e):
            def norm_transposes(use):
                for t in range(T):
                    R = ROWS[t]
                    n = T * use + t
                    e.wait_ge(s("normed"), n + 1)
                    for q in range(4):
                        m = 4 * n + q
                        if m >= 2:
                            e.wait_ge(s("nt_evacuated"), m - 1)
                        for j in range(4):
                            k = 4 * q + j
                            mm = e.transpose(bank[6 + m % 2][:, j * P:j * P + R], X2[:R, t, k * P:(k + 1) * P], ident[:R, :R])
                        mm.then_inc(s("nt_transposed"), 1)

            def project(name, ncol, nblk, extra=None):
                with e.Fori(0, nblk // 2) as i:
                    for p in range(2):
                        w = WR[p][:, 0:KD * ncol].rearrange("p (k n) -> p k n", k=KD)
                        e.wait_ge(s(f"w_landed{p}"), (i + LANDED[name] + 1) * 16)
                        for t in range(T):
                            R = ROWS[t]
                            e.wait_ge(s(f"{name}_bank_free"), (i * 2 + p) * T + t + 1)
                            if extra:
                                e.wait_ge(s("embed_bank_free"), (i * 2 + p) * T + t + 1)
                            for k in range(KD):
                                mm = e.matmul(bank[t][:R, 0:ncol], XT[:, k, t * P:t * P + R], w[:, k, :],
                                              start=(k == 0), stop=(k == KD - 1))
                            mm.then_inc(s("tiles_projected"), 1)
                            if extra:
                                extra(i, p, t)

            e.wait_ge(s("consts_loaded"), 16 * 11)
            norm_transposes(0)
            e.wait_ge(s("nt_evacuated"), 4 * T)
            project("in", IN_NC, IN_BLOCKS)

            e.wait_ge(s("weights_loaded"), 16 * 8)
            e.wait_ge(s("z_written"), 1)
            for t in range(T):
                R = ROWS[t]
                e.wait_ge(s("mla_latents_normed"), t + 1)
                if t:
                    e.wait_ge(s("mla_done"), t)
                for k in range(4):
                    e.transpose(bank[0][:, k * P:k * P + R], cqn[:R, k * P:(k + 1) * P], ident[:R, :R])
                for k in range(2):
                    mm = e.transpose(bank[1][:, k * P:k * P + R], c_smp[:R, k * P:(k + 1) * P], ident[:R, :R])
                mm.then_inc(s("lat_transposed"), 1)
                e.wait_ge(s("latT_ready"), t + 1)
                for n in range(3):
                    for k in range(4):
                        mm = e.matmul(bank[2 + n][:R, :], cqT[:, k, 0:R], w_uq[:, k, n * 512:(n + 1) * 512],
                                      start=(k == 0), stop=(k == 3))
                mm.then_inc(s("q_ready"), 1)
                for n in range(2):
                    for k in range(2):
                        mm = e.matmul(bank[5 + n][:R, :], cT[:, k, t * P:t * P + R], w_uk[:, k, n * 512:(n + 1) * 512],
                                      start=(k == 0), stop=(k == 1))
                mm.then_inc(s("k_ready"), 1)
                if t < PT:
                    for n in range(2):
                        for k in range(2):
                            mm = e.matmul(bank[(7 + n) % 8][:R, :], cT[:, k, t * P:t * P + R],
                                          w_uv[:, k, n * 512:(n + 1) * 512], start=(k == 0), stop=(k == 1))
                    mm.then_inc(s("v_ready"), 1)
                    e.wait_ge(s("q_rows_ready"), t + 1)
                    for h in range(H_MLA):
                        e.transpose(bank[1 + h // 4][:, (h % 4) * P:(h % 4 + 1) * P], qrow[:, h, 0:NOPE], ident[:, :])
                    for j in range(4):
                        mm = e.transpose(bank[3][:, j * P:(j + 1) * P],
                                         qro[:, 2 * j:2 * j + 2, :].rearrange("p a b -> p (a b)"), ident[:, :])
                    mm.then_inc(s("qT_psum"), 1)
                    e.wait_ge(s("k_rows_ready"), t + 1)
                    for h in range(H_MLA):
                        e.transpose(bank[4 + h // 4][:, (h % 4) * P:(h % 4 + 1) * P], krow[:, h, :], ident[:, :])
                    for j in range(4):
                        mm = e.transpose(bank[6][:, j * P:(j + 1) * P],
                                         kro[:, 2 * j:2 * j + 2, :].rearrange("p a b -> p (a b)"), ident[:, :])
                    mm.then_inc(s("kT_psum"), 1)
                    e.wait_ge(s("qT_sb"), t + 1)
                    e.wait_ge(s("kT_sb"), t + 1)
                    e.wait_ge(s("v_sb"), t + 1)
                    n = (t + 1) * P

                    def scores(h):
                        u = t * H_MLA + h
                        if h >= 2:
                            e.wait_ge(s("exp_done"), u - 1)
                        S = bank[7] if h % 2 else bank[0]
                        r = slice((h % 2) * ROPE, (h % 2 + 1) * ROPE)
                        e.matmul(S[:, 0:n], QTn[:, h, :], KTn[:, h, 0:n], start=True, stop=False)
                        e.matmul(S[:, 0:n], QTr[r, h // 2, :], KTr[r, h // 2, 0:n], start=False, stop=False)
                        e.matmul(S[:, t * P:n], ident[:, :], causal[:, :], start=False, stop=True)\
                            .then_inc(s("scores_ready"), 1)

                    scores(0)
                    for h in range(H_MLA):
                        u = t * H_MLA + h
                        if h + 1 < H_MLA:
                            scores(h + 1)
                        e.wait_ge(s("exp_done"), u + 1)
                        if h >= 2:
                            e.wait_ge(s("pT_sb"), u - 1)
                        for kt in range(t + 1):
                            mm = e.transpose(bank[1 + h % 2][:, kt * P:(kt + 1) * P], pr[:, h % 2, kt * P:(kt + 1) * P], ident[:, :])
                        mm.then_inc(s("pT_psum"), 1)
                        e.wait_ge(s("pT_sb"), u + 1)
                        for kt in range(t + 1):
                            mm = e.matmul(bank[3 + h // 4][:, (h % 4) * DV:(h % 4 + 1) * DV], pT[:, h % 2, kt * P:(kt + 1) * P],
                                          V[:, kt, h * DV:(h + 1) * DV], start=(kt == 0), stop=(kt == t))
                        mm.then_inc(s("pv_done"), 1)
                else:
                    sample_attention(e)
                e.wait_ge(s("mla_o_normed"), t + 1)
                for k in range(8):
                    mm = e.transpose(bank[5 + k // 4][:, (k % 4) * P:(k % 4) * P + R], onrm[:R, k * P:(k + 1) * P], ident[:R, :R])
                mm.then_inc(s("mla_oT"), 1)

            e.wait_ge(s("weights_loaded"), 16 * 12)
            e.wait_ge(s("mla_done"), T)
            for t in range(T):
                R = ROWS[t]
                lv0 = 0 if t < PT else SAMPLE_LEVEL0
                e.wait_ge(s("gla_z_loaded"), 16 * (t + 1))
                if t:
                    e.wait_ge(s("gla_done"), t)
                e.transpose(bank[0][0:GATE_R, 0:R], gz[:R, GLA_COLS - GATE_R:GLA_COLS], ident[:R, :R]).then_inc(s("lrT_psum"), 1)
                for h in range(H_GLA):
                    e.transpose(bank[1][:, h * P:h * P + R], gz[:R, h * GK:(h + 1) * GK], ident[:R, :R])
                for h in range(H_GLA):
                    mm = e.transpose(bank[2][:, h * P:h * P + R], gz[:R, (H_GLA + h) * GK:(H_GLA + h + 1) * GK], ident[:R, :R])
                mm.then_inc(s("gqkT_psum"), 1)
                e.wait_ge(s("lrT_sb"), t + 1)
                e.matmul(bank[3][:R, :], alT[0:GATE_R, 0:R], w_ga[0:GATE_R, :], start=True, stop=False)
                e.matmul(bank[3][:R, :], ones[0:1, 0:R], b_ga[0:1, :], start=False, stop=True).then_inc(s("gate_pre"), 1)
                e.wait_ge(s("gate_log"), t + 1)
                for h in range(H_GLA):
                    mm = e.matmul(bank[4][:, h * P:h * P + R], gx[:R, h * GK:(h + 1) * GK],
                                  tri[:, :] if t < PT else tri_s[0:R, :], start=True, stop=True)
                mm.then_inc(s("cum_psum"), 1)
                e.wait_ge(s("levels_ready"), t + 1)
                for h in range(H_GLA):
                    u = t * H_GLA + h
                    if h >= 2:
                        e.wait_ge(s("levels_masked"), u - 1)
                    for n in range(lv0, NLEV):
                        B = bank[2 * (h % 2) + (n - lv0) // 4]
                        dst = B[:R, ((n - lv0) % 4) * P:((n - lv0) % 4) * P + R]
                        if n < NLEV - 1:
                            mm = e.matmul(dst, Mlev[:, n, h * P:h * P + R], Mlev[:, n, h * P:h * P + R], start=True, stop=True)
                        else:
                            mm = e.matmul(dst, gkT[:, h * P:h * P + R], gqT[:, h * P:h * P + R], start=True, stop=True)
                    mm.then_inc(s("level_products"), 1)
                e.wait_ge(s("kdec_ready"), t + 1)
                for h in range(H_GLA):
                    mm = e.transpose(bank[5][:R, h * GK:(h + 1) * GK], kd[:, h * P:h * P + R], ident[:, :])
                mm.then_inc(s("kdr_psum"), 1)
                e.wait_ge(s("kdr_sb"), t + 1)
                for h in range(H_GLA):
                    u = t * H_GLA + h
                    e.wait_ge(s("AT_ready"), (t + 1) * H_GLA)
                    vg = gz[:R, 2 * H_GLA * GK + h * GV:2 * H_GLA * GK + (h + 1) * GV]
                    ob = bank[6 + h // 2][:R, (h % 2) * GV:(h % 2 + 1) * GV]
                    if t < PT:
                        e.matmul(ob, AT[:R, h, 0:R], vg, start=True, stop=(t == 0))
                        if t:
                            e.matmul(ob, qe[:, h * P:h * P + R], S0[:, h, :], start=False, stop=True)
                        e.matmul(bank[(h % 2) * 4][:, 0:GV], kdr[:R, h, :], vg, start=True, stop=True)\
                            .then_inc(s("gla_out_psum"), 1)
                        e.wait_ge(s("gla_state"), u + 1)
                    else:
                        e.wait_ge(s("qz_ready"), h + 1)
                        e.matmul(ob, AT[:R, h, 0:R], vg, start=True, stop=False)
                        for b in range(DEC_B):
                            mm = e.matmul(ob, qz[:, b, :], Ss[:, b * H_GLA + h, :], start=False, stop=(b == DEC_B - 1))
                        mm.then_inc(s("gla_out_psum"), 1)
                        for j in range(4):
                            for b in (2 * j, 2 * j + 1):
                                mm = e.matmul(bank[j if j < 4 else 0][:, (b % 2) * GV:(b % 2 + 1) * GV], kz[:R, b, :], vg,
                                              start=True, stop=True)
                        mm.then_inc(s("sample_state_psum"), 1)
                        e.wait_ge(s("sample_state_head"), h + 1)
                e.wait_ge(s("gla_o_ready"), t + 1)
                for k in range(8):
                    mm = e.transpose(bank[k // 4][:, (k % 4) * P:(k % 4) * P + R], go[:R, k * P:(k + 1) * P], ident[:R, :R])
                mm.then_inc(s("gla_oT"), 1)

            e.wait_ge(s("gla_done"), T)
            project("out", NC, NBLK)
            norm_transposes(1)
            e.wait_ge(s("weights_loaded"), 16 * 14)
            for side in range(2):
                mm = e.transpose(bank[0][:, side * P:(side + 1) * P], keysR[:, side, :], ident[:, :])
            mm.then_inc(s("keysT_psum"), 1)
            e.wait_ge(s("keysT_sb"), 1)
            e.wait_ge(s("nt_evacuated"), 4 * T * 2)

            def query(n):
                h, side = n // 2, n % 2
                w = WR[0][:, (h % 2) * KD * 256:(h % 2 + 1) * KD * 256].rearrange("p (k n) -> p k n", k=KD)
                e.wait_ge(s(f"w_landed{h % 2}"), 16 * (LANDED["peer_q"] + h // 2 + 1))
                if n >= 2:
                    e.wait_ge(s("qT_evacuated"), n - 1)
                for k in range(KD):
                    lhs = w[:, k, side * P:(side + 1) * P]
                    e.matmul(bank[2 * side][:, :], lhs, XT[:, k, 0:SEQ], start=(k == 0), stop=(k == KD - 1))
                    mm = e.matmul(bank[2 * side + 1][:, 0:NS], lhs, XT[:, k, SEQ:NTOK], start=(k == 0), stop=(k == KD - 1))
                mm.then_inc(s("q_psum_ready"), 1)

            def key_scores(n):
                side = n % 2
                e.wait_ge(s("qT_evacuated"), n + 1)
                if n >= 2:
                    e.wait_ge(s("topk_done"), n - 1)
                for t in range(T):
                    R = ROWS[t]
                    B = bank[4 + 2 * side + t // 4]
                    mm = e.matmul(B[:R, (t % 4) * P:(t % 4 + 1) * P], qTm[:, side, t * P:t * P + R], keysT[:, side, :],
                                  start=True, stop=True)
                mm.then_inc(s("key_scores"), 1)

            for n in range(2 * PH + 1):
                if n < 2 * PH:
                    query(n)
                if n:
                    key_scores(n - 1)

            norm_transposes(2)
            e.wait_ge(s("weights_loaded"), 16 * (14 + T + 1))
            for t in range(T):
                R = ROWS[t]
                if t:
                    e.wait_ge(s("pT_ple_sb"), t)
                for k in range(2):
                    mm = e.transpose(bank[5][:, k * P:k * P + R], p_row[:R, t, k * P:(k + 1) * P], ident[:R, :R])
                mm.then_inc(s("pT_ple_psum"), 1)
            e.wait_ge(s("pT_ple_sb"), T)
            e.wait_ge(s("nt_evacuated"), 4 * T * 3)

            def embed(i, p, t):
                R = ROWS[t]
                u = (p * T + t) % 2
                for k in range(2):
                    mm = e.matmul(bank[6 + u][:R, :], pT_ple[:, k, t * P:t * P + R], w_pp[:, k, bass.ds((i * 2 + p) * NC, NC)],
                                  start=(k == 0), stop=(k == 1))
                mm.then_inc(s("embed_ready"), 1)

            project("gate", NC, NBLK, embed)



        @block.scalar
        def _(e):
            own = [0]

            def link(ins):
                own[0] += 1
                ins.then_inc(s("act_own"), 1)
                e.wait_ge(s("act_own"), own[0])

            def mark(ins):
                own[0] += 1
                ins.then_inc(s("act_own"), 1)

            def norm_squares(use, ready):
                for t in range(T):
                    R = ROWS[t]
                    n = T * use + t
                    ready(t)
                    link(e.activation(X2[:R, t, :], H[:R, t, :], ACT.Square, accum_out=st[:R, n:n + 1]))
                    e.activation(st[:R, 3 * T + n:3 * T + n + 1], st[:R, n:n + 1], ACT.Sqrt, scale=1.0 / D, bias=eps[:R, :])\
                        .then_inc(s("rms_ready"), 1)
                    for q in range(4):
                        if t:
                            evacuate_xt(use, t - 1, q)
                for q in range(4):
                    evacuate_xt(use, T - 1, q)

            def evacuate_xt(use, t, q):
                R = ROWS[t]
                m = 4 * (T * use + t) + q
                e.wait_ge(s("nt_transposed"), m + 1)
                e.copy(XT[:, 4 * q:4 * q + 4, t * P:t * P + R],
                       bank[6 + m % 2][:, :].rearrange("p (j n) -> p j n", j=4)[:, :, 0:R]).then_inc(s("nt_evacuated"), 1)

            e.wait_ge(s("fills_ready"), 2)
            norm_squares(0, lambda t: e.wait_ge(s("x_loaded"), 16 * T))
            e.wait_ge(s("normed"), T)
            e.sem_inc(s("in_bank_free"), T)
            with e.Fori(0, IN_BLOCKS // 2) as i:
                for p in range(2):
                    for t in range(T):
                        R = ROWS[t]
                        u = (i * 2 + p) * T + t
                        e.wait_ge(s("tiles_projected"), u + 1)
                        e.copy(zst[:R, p * T + t, 0:IN_NC], bank[t][:R, 0:IN_NC]).then_inc(s("in_bank_free"), 1)
                        e.wait_ge(s("in_bank_free"), u + T + 1)
                        e.dma_start(z_dram[rows(t), bass.ds((i * 2 + p) * IN_NC, IN_NC)], zst[:R, p * T + t, 0:IN_NC])\
                            .then_inc(s("z_stored"), 16)
                e.wait_ge(s("z_stored"), (i + 1) * (2 * T * 16))
            e.sem_inc(s("z_written"), 1)

            def pT_copy(u):
                t, h = u // H_MLA, u % H_MLA
                e.wait_ge(s("pT_psum"), u + 1)
                if h >= 2:
                    e.wait_ge(s("pv_done"), u - 1)
                e.copy(pT[:, h % 2, 0:(t + 1) * P], bank[1 + h % 2][:, 0:(t + 1) * P]).then_inc(s("pT_sb"), 1)

            def rms(out, ssq, width, R):
                return e.activation(out[:R], ssq[:R], ACT.Sqrt, scale=1.0 / width, bias=eps[:R, :])

            for t in range(T):
                R = ROWS[t]
                e.wait_ge(s("mla_z_loaded"), 16 * (t + 1))
                if t:
                    e.wait_ge(s("mla_done"), t)
                mark(e.activation(sqs[:R, 0:QR], m_z[:R, 0:QR], ACT.Square, accum_out=SSQ[:R]))
                mark(e.activation(sqs[:R, QR:QR + KVR], m_z[:R, QR:QR + KVR], ACT.Square, accum_out=SSC[:R]))
                link(e.activation(sqs[:R, QR + KVR:MLA_COLS], m_z[:R, QR + KVR:MLA_COLS], ACT.Square, accum_out=SKR[:R]))
                rms(RQ, SSQ, QR, R)
                rms(RC, SSC, KVR, R).then_inc(s("lat_rms"), 1)
                e.wait_ge(s("lat_transposed"), t + 1)
                e.copy(cqT[:, :, 0:R], bank[0][:, :].rearrange("p (j n) -> p j n", j=4)[:, :, 0:R])
                e.copy(cT[:, :, t * P:t * P + R], bank[1][:, 0:2 * P].rearrange("p (j n) -> p j n", j=2)[:, :, 0:R])\
                    .then_inc(s("latT_ready"), 1)
                e.wait_ge(s("q_ready"), t + 1)
                for n in range(3):
                    ins = e.activation(sqs[:R, n * 512:(n + 1) * 512], bank[2 + n][:R, :], ACT.Square)
                ins.then_inc(s("q_squares"), 1)
                e.wait_ge(s("q_sumsq"), t + 1)
                e.activation(RQH[:R], SQH[:R], ACT.Sqrt, scale=1.0 / QK, bias=eps[:R, :]).then_inc(s("q_rms"), 1)
                e.wait_ge(s("k_ready"), t + 1)
                for n in range(2):
                    ins = e.activation(sqs[:R, n * 512:(n + 1) * 512], bank[5 + n][:R, :], ACT.Square)
                ins.then_inc(s("k_squares"), 1)
                e.wait_ge(s("k_sumsq"), t + 1)
                e.activation(RKH[:R], SKH[:R], ACT.Sqrt, scale=1.0 / QK, bias=eps[:R, :]).then_inc(s("k_rms"), 1)
                if t < PT:
                    e.wait_ge(s("v_ready"), t + 1)
                    e.copy(V[:, t, 0:512], bank[7][:, :])
                    e.copy(V[:, t, 512:1024], bank[0][:, :]).then_inc(s("v_sb"), 1)
                    e.wait_ge(s("qT_psum"), t + 1)
                    e.copy(QTn[:, 0:4, :], bank[1][:, :].rearrange("p (j n) -> p j n", j=4))
                    e.copy(QTn[:, 4:8, :], bank[2][:, :].rearrange("p (j n) -> p j n", j=4))
                    e.copy(QTr[:, :, :], bank[3][:, :].rearrange("p (j n) -> p j n", j=4)).then_inc(s("qT_sb"), 1)
                    n = (t + 1) * P
                    for h in range(H_MLA):
                        u = t * H_MLA + h
                        S = bank[7] if h % 2 else bank[0]
                        e.wait_ge(s("neg_max"), u + 1)
                        if h >= 2:
                            e.wait_ge(s("pT_psum"), u - 1)
                        e.activation(pr[:, h % 2, 0:n], S[:, 0:n], ACT.Exp, scale=SCALE, bias=NMX[:, h:h + 1],
                                     accum_out=RSUM[:, h:h + 1]).then_inc(s("exp_done"), 1)
                        if h:
                            pT_copy(u - 1)
                    pT_copy(t * H_MLA + H_MLA - 1)
                else:
                    sample_act(e, link)
                e.wait_ge(s("mla_o_rows"), t + 1)
                link(e.activation(sqs[:R, 0:1024], orow[:R, :], ACT.Square, accum_out=SSO[:R]))
                rms(RSO, SSO, H_MLA * DV, R).then_inc(s("o_rms"), 1)
                e.wait_ge(s("mla_oT"), t + 1)
                e.copy(XT[:, 0:4, t * P:t * P + R], bank[5][:, :].rearrange("p (j n) -> p j n", j=4)[:, :, 0:R])
                e.copy(XT[:, 4:8, t * P:t * P + R], bank[6][:, :].rearrange("p (j n) -> p j n", j=4)[:, :, 0:R])\
                    .then_inc(s("mla_done"), 1)

            for t in range(T):
                R = ROWS[t]
                lv0 = 0 if t < PT else SAMPLE_LEVEL0
                e.wait_ge(s("lrT_psum"), t + 1)
                e.copy(alT[0:GATE_R, 0:R], bank[0][0:GATE_R, 0:R]).then_inc(s("lrT_sb"), 1)
                e.wait_ge(s("gqkT_psum"), t + 1)
                e.activation(heads(gqT, R), heads(bank[1], R), ACT.Copy, scale=float(GK) ** -0.5)
                e.copy(heads(gkT, R), heads(bank[2], R)).then_inc(s("gqkT_sb"), 1)
                e.wait_ge(s("gate_pre"), t + 1)
                link(e.activation(gt1[:R, :], bank[3][:R, :], ACT.Abs))
                link(e.activation(gt1[:R, :], gt1[:R, :], ACT.Exp, scale=-1.0))
                e.activation(gt1[:R, :], gt1[:R, :], ACT.Ln, bias=1.0).then_inc(s("gate_ln"), 1)
                for n in range(lv0, NLEV - 1):
                    v = level_count(t, n)
                    e.wait_ge(s("level_diff"), v + 1)
                    if v >= 2:
                        e.wait_ge(s("level_done"), v - 1)
                    e.activation(heads(dlev[:, n % 2, :], R), heads(dlev[:, n % 2, :], R), ACT.Exp).then_inc(s("level_exp"), 1)
                e.wait_ge(s("cum_sb"), t + 1)
                e.activation(heads(eb, R), heads(gbT, R), ACT.Exp).then_inc(s("eb_ready"), 1)
                e.wait_ge(s("kdiff"), t + 1)
                e.activation(heads(kd, R), heads(kd, R), ACT.Exp).then_inc(s("kexp"), 1)
                e.wait_ge(s("kdr_psum"), t + 1)
                e.copy(kdr[:R, :, :], bank[5][:R, :].rearrange("p (h n) -> p h n", h=H_GLA)).then_inc(s("kdr_sb"), 1)
                link(e.activation(gsil[:R, :], gz[:R, 2 * H_GLA * GK + 1024:2 * H_GLA * GK + 2048], ACT.Silu))
                e.wait_ge(s("gla_o_sb"), t + 1)
                for h in range(H_GLA):
                    ins = e.activation(gsq[:R, h * GV:(h + 1) * GV], go[:R, h * GV:(h + 1) * GV], ACT.Square,
                                       accum_out=GSS[:R, h:h + 1])
                link(ins)
                e.activation(GRS[:R], GSS[:R], ACT.Sqrt, scale=1.0 / GV, bias=eps[:R, :]).then_inc(s("gla_rms"), 1)
                e.wait_ge(s("gla_oT"), t + 1)
                e.copy(XT[:, 8:12, t * P:t * P + R], bank[0][:, :].rearrange("p (j n) -> p j n", j=4)[:, :, 0:R])
                e.copy(XT[:, 12:16, t * P:t * P + R], bank[1][:, :].rearrange("p (j n) -> p j n", j=4)[:, :, 0:R])\
                    .then_inc(s("gla_done"), 1)

            norm_squares(1, lambda t: e.wait_ge(s("out_bank_free"), T + (NBLK - 1) * T + t + 1))
            e.wait_ge(s("keysT_psum"), 1)
            e.copy(keysT[:, :, :], bank[0][:, 0:2 * P].rearrange("p (j n) -> p j n", j=2)).then_inc(s("keysT_sb"), 1)
            for n in range(2 * PH):
                side = n % 2
                e.wait_ge(s("q_psum_ready"), n + 1)
                if n >= 2:
                    e.wait_ge(s("key_scores"), n - 1)
                e.copy(qTm[:, side, 0:SEQ], bank[2 * side][:, :])
                e.copy(qTm[:, side, SEQ:NTOK], bank[2 * side + 1][:, 0:NS]).then_inc(s("qT_evacuated"), 1)
            for t in range(T):
                R = ROWS[t]
                e.wait_ge(s("gate_diff"), t + 1)
                e.activation(gtop[:R, :], gtop[:R, :], ACT.Exp).then_inc(s("gate_exp"), 1)
            with e.Fori(0, UNITS) as u:
                e.wait_ge(s("dots_done"), (u + 1) * TOPK)
                e.activation(gel[:, :], dots[:, :], ACT.Gelu).then_inc(s("gelu_ready"), 1)

            norm_squares(2, lambda t: e.wait_ge(s("peer_done"), t + 1))
            for t in range(T):
                e.wait_ge(s("pT_ple_psum"), t + 1)
                e.copy(pT_ple[:, :, t * P:t * P + ROWS[t]],
                       bank[5][:, 0:2 * P].rearrange("p (j n) -> p j n", j=2)[:, :, 0:ROWS[t]]).then_inc(s("pT_ple_sb"), 1)
            e.sem_inc(s("gate_sg_free"), 2)
            with e.Fori(0, NBLK // 2) as i:
                for p in range(2):
                    for t in range(T):
                        R = ROWS[t]
                        u = (i * 2 + p) * T + t
                        e.wait_ge(s("tiles_projected"), u + SERVED["gate"] + 1)
                        e.wait_ge(s("gate_sg_free"), u + 1)
                        e.activation(sg[:R, (p * T + t) % 2, :], bank[t][:R, :], ACT.Sigmoid).then_inc(s("sigmoid_ready"), 1)




        @block.vector
        def _(e):
            own = [0]

            def link(ins):
                own[0] += 1
                ins.then_inc(s("dve_own"), 1)
                e.wait_ge(s("dve_own"), own[0])

            def mark(ins):
                own[0] += 1
                ins.then_inc(s("dve_own"), 1)

            def norm_rows(use):
                for t in range(T):
                    R = ROWS[t]
                    n = T * use + t
                    e.wait_ge(s("rms_ready"), n + 1)
                    link(e.reciprocal(st[:R, 6 * T + n:6 * T + n + 1], st[:R, 3 * T + n:3 * T + n + 1]))
                    if t == 0:
                        e.wait_ge(s("gain_loaded"), 16 * (use + 1))
                    e.scalar_tensor_tensor(out=X2[:R, t, :], in0=H[:R, t, :], scalar=st[:R, 6 * T + n:6 * T + n + 1],
                                           in1=G[:R, :], op0=ALU.mult, op1=ALU.mult).then_inc(s("normed"), 1)

            e.memset(ones[:, :], 1.0).then_inc(s("fills_ready"), 1)
            e.memset(eps[:, :], EPS).then_inc(s("fills_ready"), 1)
            norm_rows(0)

            e.wait_ge(s("consts_loaded"), 16 * 11)
            e.wait_ge(s("weights_loaded"), 16 * 8)
            for t in range(T):
                R = ROWS[t]

                def rotate(out, x, n):
                    cs, sn = cosT[:R, t, :], sinT[:R, t, :]
                    hf = ROPE // 2
                    if n > 1:
                        cb = cs.unsqueeze(1).to_broadcast([R, n, ROPE])
                        s0 = sn[:, 0:hf].unsqueeze(1).to_broadcast([R, n, hf])
                        s1 = sn[:, hf:ROPE].unsqueeze(1).to_broadcast([R, n, hf])
                        tmp = rtmp[:R]
                        xa, xb, ta, tb = x[:, :, hf:ROPE], x[:, :, 0:hf], tmp[:, :, 0:hf], tmp[:, :, hf:ROPE]
                    else:
                        cb, s0, s1 = cs, sn[:, 0:hf], sn[:, hf:ROPE]
                        tmp = rtmp[:R, 0, :]
                        xa, xb, ta, tb = x[:, hf:ROPE], x[:, 0:hf], tmp[:, 0:hf], tmp[:, hf:ROPE]
                    e.tensor_tensor(ta, xa, s0, ALU.mult)
                    e.tensor_tensor(tb, xb, s1, ALU.mult)
                    link(e.tensor_tensor(out, x, cb, ALU.mult))
                    return e.tensor_tensor(out, out, tmp, ALU.add)

                e.wait_ge(s("lat_rms"), t + 1)
                e.reciprocal(IQ[:R], RQ[:R])
                link(e.reciprocal(IC[:R], RC[:R]))
                e.scalar_tensor_tensor(out=cqn[:R, :], in0=m_z[:R, 0:QR], scalar=IQ[:R], in1=g_q[:R, :], op0=ALU.mult, op1=ALU.mult)
                if t:
                    e.wait_ge(s("mla_outputs"), 16 * 3 * t)
                e.scalar_tensor_tensor(out=c_smp[:R, :], in0=m_z[:R, QR:QR + KVR], scalar=IC[:R], in1=g_kv[:R, :],
                                       op0=ALU.mult, op1=ALU.mult).then_inc(s("mla_latents_normed"), 1)
                e.wait_ge(s("mla_latents_normed"), t + 1)
                link(e.tensor_tensor(kr_g[:R, :], m_z[:R, QR + KVR:MLA_COLS], g_k[:R, NOPE:QK], ALU.mult))
                link(rotate(kr_o[:R, :], kr_g[:R, :], 1))
                e.wait_ge(s("q_squares"), t + 1)
                e.tensor_reduce(SQH[:R], sqs[:R, :].rearrange("p (h n) -> p h n", h=H_MLA), AX, ALU.add).then_inc(s("q_sumsq"), 1)
                e.wait_ge(s("q_rms"), t + 1)
                link(e.reciprocal(IQH[:R], RQH[:R]))
                for h in range(H_MLA):
                    lo_, hi_ = h * QK, (h + 1) * QK
                    while lo_ < hi_:
                        nx = min(hi_, (lo_ // 512 + 1) * 512)
                        ins = e.tensor_scalar(qrow[:R, h, lo_ - h * QK:nx - h * QK],
                                              bank[2 + lo_ // 512][:R, lo_ % 512:lo_ % 512 + nx - lo_], IQH[:R, h:h + 1], None, ALU.mult)
                        lo_ = nx
                link(ins)
                link(e.tensor_tensor(qrow[:R], qrow[:R], g_qk[:R, :].unsqueeze(1).to_broadcast([R, H_MLA, QK]), ALU.mult))
                link(rotate(qro[:R], qrow[:R, :, NOPE:QK], H_MLA))
                if t == PT:
                    link(e.tensor_tensor(qrow[:R, :, 0:NOPE], qrow[:R, :, 0:NOPE],
                                         g_k[:R, 0:NOPE].unsqueeze(1).to_broadcast([R, H_MLA, NOPE]), ALU.mult))
                e.sem_inc(s("q_rows_ready"), 1)
                e.wait_ge(s("k_squares"), t + 1)
                link(e.tensor_reduce(SKH[:R], sqs[:R, 0:1024].rearrange("p (h n) -> p h n", h=H_MLA), AX, ALU.add))
                e.tensor_scalar(SKH[:R], SKH[:R], SKR[:R], None, ALU.add).then_inc(s("k_sumsq"), 1)
                e.wait_ge(s("k_rms"), t + 1)
                link(e.reciprocal(IKH[:R], RKH[:R]))
                e.sem_inc(s("mla_keys_ready"), 1)
                if t < PT:
                    for n in range(2):
                        ins = e.tensor_tensor(krow[:, 4 * n:4 * n + 4, :], bank[5 + n][:, :].rearrange("p (h n) -> p h n", h=4),
                                              IKH[:, 4 * n:4 * n + 4].unsqueeze(2).to_broadcast([P, 4, NOPE]), ALU.mult)
                    link(ins)
                    link(e.tensor_tensor(krow[:, :, :], krow[:, :, :], g_k[:, 0:NOPE].unsqueeze(1).to_broadcast([P, H_MLA, NOPE]), ALU.mult))
                    e.tensor_tensor(kro[:, :, :], kr_o[:, :].unsqueeze(1).to_broadcast([P, H_MLA, ROPE]),
                                    IKH[:, :].unsqueeze(2).to_broadcast([P, H_MLA, ROPE]), ALU.mult).then_inc(s("k_rows_ready"), 1)
                    e.wait_ge(s("kT_psum"), t + 1)
                    e.tensor_copy(KTn[:, 0:4, t * P:(t + 1) * P], bank[4][:, :].rearrange("p (j n) -> p j n", j=4))
                    e.tensor_copy(KTn[:, 4:8, t * P:(t + 1) * P], bank[5][:, :].rearrange("p (j n) -> p j n", j=4))
                    e.tensor_copy(KTr[:, :, t * P:(t + 1) * P], bank[6][:, :].rearrange("p (j n) -> p j n", j=4))\
                        .then_inc(s("kT_sb"), 1)
                    for h in range(H_MLA):
                        u = t * H_MLA + h
                        S = bank[7] if h % 2 else bank[0]
                        e.wait_ge(s("scores_ready"), u + 1)
                        link(e.tensor_reduce(MXV[:, h:h + 1], S[:, 0:(t + 1) * P], AX, ALU.max))
                        e.tensor_scalar(NMX[:, h:h + 1], MXV[:, h:h + 1], -SCALE, None, ALU.mult).then_inc(s("neg_max"), 1)
                    e.wait_ge(s("exp_done"), (t + 1) * H_MLA)
                    link(e.reciprocal(RINV[:, :], RSUM[:, :]))
                    e.wait_ge(s("pv_done"), (t + 1) * H_MLA)
                    for n in range(2):
                        ins = e.tensor_tensor(orow[:, n * 512:(n + 1) * 512].rearrange("p (h n) -> p h n", h=4),
                                              bank[3 + n][:, :].rearrange("p (h n) -> p h n", h=4),
                                              RINV[:, 4 * n:4 * n + 4].unsqueeze(2).to_broadcast([P, 4, DV]), ALU.mult)
                    ins.then_inc(s("mla_o_rows"), 1)
                else:
                    e.sem_inc(s("k_rows_ready"), 1)
                    sample_dve(e, link)
                e.wait_ge(s("o_rms"), t + 1)
                link(e.reciprocal(ISO[:R], RSO[:R]))
                e.scalar_tensor_tensor(out=onrm[:R, :], in0=orow[:R, :], scalar=ISO[:R], in1=g_mla[:R, :],
                                       op0=ALU.mult, op1=ALU.mult).then_inc(s("mla_o_normed"), 1)

            e.wait_ge(s("mla_done"), T)
            e.wait_ge(s("weights_loaded"), 16 * 12)
            link(e.memset(qz, 0.0))
            for t in range(T):
                R = ROWS[t]
                lv0 = 0 if t < PT else SAMPLE_LEVEL0
                e.wait_ge(s("gate_pre"), t + 1)
                if t:
                    e.wait_ge(s("gla_done"), t)
                e.wait_ge(s("gate_ln"), t + 1)
                link(e.tensor_scalar(gt2[:R, :], bank[3][:R, :], 0.0, 1.0 / TAU, ALU.min, ALU.mult))
                e.scalar_tensor_tensor(out=gx[:R, :], in0=gt1[:R, :], scalar=-1.0 / TAU, in1=gt2[:R, :],
                                       op0=ALU.mult, op1=ALU.add).then_inc(s("gate_log"), 1)
                e.wait_ge(s("cum_psum"), t + 1)
                e.tensor_copy(heads(gbT, R), heads(bank[4], R)).then_inc(s("cum_sb"), 1)
                e.wait_ge(s("cum_sb"), t + 1)
                e.wait_ge(s("gqkT_sb"), t + 1)

                def halves(ap, n):
                    hf = LEVELS[n]
                    if R == P:
                        v = ap[:, 0:H_GLA * P].rearrange("p (g a b) -> p g a b", a=2, b=hf)
                        return v[:, :, 0, :], v[:, :, 1, :]
                    v = heads(ap, R).rearrange("p h (g a b) -> p h g a b", a=2, b=hf)
                    return v[:, :, :, 0, :], v[:, :, :, 1, :]

                def multiply(n):
                    v = level_count(t, n)
                    e.wait_ge(s("level_exp"), v + 1)
                    dl = dlev[:, n % 2, :]
                    d0, d1 = halves(dl, n)
                    m0, m1 = halves(Mlev[:, n, :], n)
                    k0, _ = halves(gkT, n)
                    _, q1 = halves(gqT, n)
                    e.tensor_tensor(m0, d0, k0, ALU.mult)
                    e.tensor_tensor(m1, d1, q1, ALU.mult).then_inc(s("level_done"), 1)

                for n in range(lv0, NLEV - 1):
                    hf = LEVELS[n]
                    v = level_count(t, n)
                    dl = dlev[:, n % 2, :]
                    if v >= 2:
                        e.wait_ge(s("level_done"), v - 1)
                    b0, b1 = halves(gbT, n)
                    d0, d1 = halves(dl, n)
                    ref = b0[..., hf - 1:hf]
                    rb = ref.to_broadcast(list(b0.shape))
                    e.tensor_tensor(d0, rb, b0, ALU.subtract)
                    e.tensor_tensor(d1, b1, rb, ALU.subtract).then_inc(s("level_diff"), 1)
                    if n > lv0:
                        multiply(n - 1)
                multiply(NLEV - 2)
                e.wait_ge(s("level_done"), level_count(t, NLEV - 2) + 1)
                e.sem_inc(s("levels_ready"), 1)
                seg = P if t < PT else DEC_T
                gseg = heads(gbT, R).rearrange("p h (g n) -> p h g n", n=seg)
                kseg = heads(kd, R).rearrange("p h (g n) -> p h g n", n=seg)
                last = gseg[:, :, :, seg - 1:seg]
                e.tensor_tensor(kseg, last.to_broadcast(list(gseg.shape)), gseg, ALU.subtract).then_inc(s("kdiff"), 1)
                e.wait_ge(s("eb_ready"), t + 1)
                e.tensor_tensor(heads(qe, R), heads(gqT, R), heads(eb, R), ALU.mult)
                ebs = heads(eb, R).rearrange("p h (g n) -> p h g n", n=seg)[:, :, :, seg - 1]
                nseg = R // seg
                link(e.tensor_copy(eL[:, 0:H_GLA * nseg].rearrange("p (h g) -> p h g", h=H_GLA), ebs))
                e.wait_ge(s("kexp"), t + 1)
                e.tensor_tensor(heads(kd, R), heads(kd, R), heads(gkT, R), ALU.mult).then_inc(s("kdec_ready"), 1)
                nl = NLEV - lv0
                for h in range(H_GLA):
                    u = t * H_GLA + h
                    e.wait_ge(s("level_products"), u + 1)
                    A = am[:, h % 2, :].rearrange("p (l n) -> p l n", n=P)
                    ins = None
                    for half in range((nl + 3) // 4):
                        n4 = min(4, nl - 4 * half)
                        ins = e.tensor_tensor(A[:R, 4 * half:4 * half + n4, 0:R],
                                              bank[2 * (h % 2) + half][:R, :].rearrange("p (l n) -> p l n", n=P)[:, 0:n4, 0:R],
                                              lev[:R, lv0 + 4 * half:lv0 + 4 * half + n4, 0:R], ALU.mult)
                    ins.then_inc(s("levels_masked"), 1)
                    e.wait_ge(s("levels_masked"), u + 1)
                    e.tensor_reduce(AT[:R, h, 0:R], A[:R, 0:nl, 0:R].rearrange("p l n -> p n l"), AX, ALU.add).then_inc(s("AT_ready"), 1)
                for h in range(H_GLA):
                    u = t * H_GLA + h
                    if t < PT:
                        e.wait_ge(s("gla_out_psum"), u + 1)
                        upd = bank[(h % 2) * 4][:, 0:GV]
                        if t:
                            e.scalar_tensor_tensor(out=S0[:, h, :], in0=S0[:, h, :], scalar=eL[:, h:h + 1], in1=upd,
                                                   op0=ALU.mult, op1=ALU.add).then_inc(s("gla_state"), 1)
                        else:
                            e.tensor_copy(S0[:, h, :], upd).then_inc(s("gla_state"), 1)
                    else:
                        if h:
                            e.wait_ge(s("sample_state_psum"), h)
                            sample_state(h - 1)
                        for b in range(DEC_B):
                            ins = e.tensor_copy(qz[:, b, b * DEC_T:(b + 1) * DEC_T], qe[:, h * P + b * DEC_T:h * P + (b + 1) * DEC_T])
                        e.wait_ge(s("kdr_sb"), T)
                        e.tensor_tensor(kz[:R, :, :], kdr[:R, h, :].unsqueeze(1).to_broadcast([R, DEC_B, GK]),
                                        bmask[:R, :].unsqueeze(2).to_broadcast([R, DEC_B, GK]), ALU.mult).then_inc(s("qz_ready"), 1)
                if t == PT:
                    e.wait_ge(s("sample_state_psum"), H_GLA)
                    sample_state(H_GLA - 1)
                e.wait_ge(s("gla_out_psum"), (t + 1) * H_GLA)
                e.tensor_copy(go[:R, 0:512], bank[6][:R, :])
                e.tensor_copy(go[:R, 512:1024], bank[7][:R, :]).then_inc(s("gla_o_sb"), 1)
                e.wait_ge(s("gla_rms"), t + 1)
                link(e.reciprocal(GIS[:R], GRS[:R]))
                gv = go[:R, :].rearrange("p (h n) -> p h n", h=H_GLA)
                link(e.tensor_tensor(gv, gv, GIS[:R].unsqueeze(2).to_broadcast([R, H_GLA, GV]), ALU.mult))
                link(e.tensor_tensor(gv, gv, g_go[:R, :].unsqueeze(1).to_broadcast([R, H_GLA, GV]), ALU.mult))
                e.tensor_tensor(go[:R, :], go[:R, :], gsil[:R, :], ALU.mult).then_inc(s("gla_o_ready"), 1)

            e.wait_ge(s("x_loaded"), 16 * 2 * T)
            e.sem_inc(s("out_bank_free"), T)
            with e.Fori(0, NBLK // 2) as i:
                for p in range(2):
                    for t in range(T):
                        R = ROWS[t]
                        u = (i * 2 + p) * T + t
                        hs = H[:R, t, bass.ds((i * 2 + p) * NC, NC)]
                        e.wait_ge(s("tiles_projected"), u + SERVED["out"] + 1)
                        e.tensor_tensor(hs, hs, bank[t][:R, :], ALU.add).then_inc(s("out_bank_free"), 1)
            norm_rows(1)

            for n in range(2 * PH):
                side = n % 2
                e.wait_ge(s("key_scores"), n + 1)

                def sco(t):
                    return bank[4 + 2 * side + t // 4][:ROWS[t], (t % 4) * P:(t % 4 + 1) * P]

                def top(t):
                    return topv[:ROWS[t], t, n, :]

                for t in range(T):
                    ins = e.max(top(t)[:, 0:8], sco(t))
                link(ins)
                for t in range(T):
                    R = ROWS[t]
                    e.max_index(topu[:R, t, 0:8], top(t)[:, 0:8], sco(t))
                    ins = e.match_replace(out=swork[:R, t, :], in_to_replace=top(t)[:, 0:8], in_values=sco(t), imm_value=LOWEST)
                link(ins)
                for t in range(T):
                    ins = e.max(top(t)[:, 8:16], swork[:ROWS[t], t, :])
                link(ins)
                for t in range(T):
                    R = ROWS[t]
                    ins = e.max_index(topu[:R, t, 8:16], top(t)[:, 8:16], swork[:R, t, :])
                link(ins)
                ins = e.tensor_copy(topi[:, 0:PT, n, :], topu[:, 0:PT, :])
                e.tensor_copy(topi[:NS, PT, n, :], topu[:NS, PT, :]).then_inc(s("topk_done"), 1)
            e.wait_ge(s("topk_done"), 2 * PH)
            e.wait_ge(s("q_psum_ready"), 2 * PH)
            for t in range(T):
                R = ROWS[t]
                tv = topv[:R, t, :, :].rearrange("p (h w) k -> p h w k", w=2)
                ti = topi[:R, t, :, :].rearrange("p (h w) k -> p h w k", w=2)
                cv = cand[:R, :].rearrange("p (h i j) -> p h i j", h=PH, i=TOPK)
                link(e.tensor_tensor(cv, tv[:, :, 0, :].unsqueeze(3).to_broadcast([R, PH, TOPK, TOPK]),
                                     tv[:, :, 1, :].unsqueeze(2).to_broadcast([R, PH, TOPK, TOPK]), ALU.add))
                gv = gtop
                for h in range(PH):
                    ins = e.max(gv[:R, h * 16:h * 16 + 8], cand[:R, h * 256:(h + 1) * 256])
                link(ins)
                for h in range(PH):
                    e.max_index(sela[:R, h * 16:h * 16 + 8], gv[:R, h * 16:h * 16 + 8], cand[:R, h * 256:(h + 1) * 256])
                    ins = e.match_replace(out=candw[:R, h * 256:(h + 1) * 256], in_to_replace=gv[:R, h * 16:h * 16 + 8],
                                          in_values=cand[:R, h * 256:(h + 1) * 256], imm_value=LOWEST)
                link(ins)
                for h in range(PH):
                    ins = e.max(gv[:R, h * 16 + 8:h * 16 + 16], candw[:R, h * 256:(h + 1) * 256])
                link(ins)
                for h in range(PH):
                    ins = e.max_index(sela[:R, h * 16 + 8:h * 16 + 16], gv[:R, h * 16 + 8:h * 16 + 16], candw[:R, h * 256:(h + 1) * 256])
                link(ins)
                link(e.tensor_copy(e1[:R, 0:8], gv[:R, :].rearrange("p (h k) -> p h k", h=PH)[:, :, 0]))
                g3 = gv[:R, :].rearrange("p (h k) -> p h k", h=PH)
                e.tensor_tensor(g3, g3, e1[:R, 0:8].unsqueeze(2).to_broadcast([R, PH, TOPK]), ALU.subtract).then_inc(s("gate_diff"), 1)
                e.tensor_single_scalar(selh[:R, :], sela[:R, :], 4, ALU.logical_shift_right)
                link(e.tensor_single_scalar(sell[:R, :], sela[:R, :], 15, ALU.bitwise_and))
                e.tensor_copy(selhf[:R, :], selh[:R, :])
                link(e.tensor_copy(sellf[:R, :], sell[:R, :]))
                for sel, w, out in ((selhf, 0, e1), (sellf, 1, e2)):
                    oh = oneh[:R, :].rearrange("p (h i j) -> p h i j", h=PH, i=TOPK)
                    o3 = oneh[:R, :].rearrange("p (n j) -> p n j", j=TOPK)
                    link(e.tensor_tensor(o3, sel[:R, :].unsqueeze(2).to_broadcast([R, P, TOPK]),
                                         iota16[:R, :].unsqueeze(1).to_broadcast([R, P, TOPK]), ALU.is_equal))
                    link(e.tensor_tensor(oh, oh, ti[:, :, w, :].unsqueeze(2).to_broadcast([R, PH, TOPK, TOPK]), ALU.mult))
                    link(e.tensor_reduce(out[:R, :], o3, AX, ALU.add))
                link(e.scalar_tensor_tensor(out=e1[:R, :], in0=e1[:R, :], scalar=float(NKEY), in1=e2[:R, :], op0=ALU.mult, op1=ALU.add))
                e.wait_ge(s("gate_exp"), t + 1)
                link(e.tensor_reduce(gsum[:R, :], g3, AX, ALU.add))
                link(e.reciprocal(gsum[:R, :], gsum[:R, :]))
                u0 = t * PH * TOPK
                if t < PT:
                    e.tensor_copy(idx_all[:, u0:u0 + 128], e1[:, :])
                    link(e.tensor_tensor(gate_all[:, u0:u0 + 128].rearrange("p (h k) -> p h k", h=PH), g3,
                                         gsum[:, :].unsqueeze(2).to_broadcast([P, PH, TOPK]), ALU.mult))
                else:
                    hh = PH // 2
                    e.tensor_copy(idx_all[:R, u0:u0 + 64], e1[:R, 0:64])
                    e.tensor_copy(ixs_hi, e1[:R, 64:128])
                    e.tensor_tensor(gate_all[:R, u0:u0 + 64].rearrange("p (h k) -> p h k", h=hh), g3[:, 0:hh],
                                    gsum[:R, 0:hh].unsqueeze(2).to_broadcast([R, hh, TOPK]), ALU.mult)
                    link(e.tensor_tensor(gts_hi.rearrange("p (h k) -> p h k", h=hh), g3[:, hh:PH],
                                         gsum[:R, hh:PH].unsqueeze(2).to_broadcast([R, hh, TOPK]), ALU.mult))
                e.sem_inc(s("route_ready"), 1)

            e.memset(H[NS:P, PT, :], 0.0)
            e.wait_ge(s("sample_spread"), 48)
            e.sem_inc(s("buffers_free"), RING)
            e.sem_inc(s("summed"), 1)
            for t in range(T):
                nu = PH if t < PT else PH // 2
                accs = [H[:, t, :], acc1]
                link(e.memset(acc1, 0.0))
                with e.Fori(t * PH, t * PH + nu) as u:
                    for k in range(TOPK):
                        b = k % RING
                        e.wait_ge(s(f"rows_landed{b}"), u * 64 + 16 * (k // RING + 1))
                        e.tensor_tensor_reduce(out=ring[:, b, :], in0=ring[:, b, :], in1=X2[:, t, :], scale=1.0, scalar=0.0,
                                               op0=ALU.mult, op1=ALU.add, accum_out=dots[:, k:k + 1]).then_inc(s("dots_done"), 1)
                        e.wait_ge(s("dots_done"), u * TOPK + k + 1)
                        e.sem_inc(s("buffers_free"), 1)
                    e.wait_ge(s("gelu_ready"), u + 1)
                    e.tensor_tensor(coef[:, :], gel[:, :], gate_all[:, bass.ds(u * TOPK, TOPK)], ALU.mult).then_inc(s("coef_ready"), 1)
                    e.wait_ge(s("coef_ready"), u + 1)
                    for k in range(TOPK):
                        b = k % RING
                        e.wait_ge(s(f"rows_landed{b}"), u * 64 + 16 * ((TOPK + k) // RING + 1))
                        e.wait_ge(s("summed"), u * TOPK + max(k, 1))
                        e.scalar_tensor_tensor(out=accs[k % 2], in0=ring[:, b, :], scalar=coef[:, k:k + 1], in1=accs[k % 2],
                                               op0=ALU.mult, op1=ALU.add).then_inc(s("summed"), 1)
                        e.wait_ge(s("summed"), u * TOPK + k + 2)
                        e.sem_inc(s("buffers_free"), 1)
                R = ROWS[t]
                link(e.tensor_tensor(H[:, t, :], H[:, t, :], acc1, ALU.add))
                if t == PT:
                    e.sem_inc(s("sample_halves"), 1)
                    e.wait_ge(s("sample_back"), 16)
                    link(e.tensor_tensor(H[:R, t, :], H[:R, t, :], acc1[0:R, :], ALU.add))
                e.sem_inc(s("peer_done"), 1)

            norm_rows(2)
            e.sem_inc(s("gate_bank_free"), T)
            e.sem_inc(s("embed_bank_free"), 2)
            e.wait_ge(s("nt_evacuated"), 4 * T * 3)
            with e.Fori(0, NBLK // 2) as i:
                for p in range(2):
                    for t in range(T):
                        R = ROWS[t]
                        u = (i * 2 + p) * T + t
                        v = (p * T + t) % 2
                        e.wait_ge(s("sigmoid_ready"), u + 1)
                        e.wait_ge(s("embed_ready"), u + 1)
                        e.tensor_tensor(sg[:R, v, :], sg[:R, v, :], bank[6 + v][:R, :], ALU.mult).then_inc(s("embed_bank_free"), 1)
                        e.wait_ge(s("embed_bank_free"), u + 3)
                        hs = H[:R, t, bass.ds((i * 2 + p) * NC, NC)]
                        e.tensor_tensor(hs, hs, sg[:R, v, :], ALU.add).then_inc(s("gate_bank_free"), 1)
                        e.wait_ge(s("gate_bank_free"), u + T + 1)
                        e.sem_inc(s("gate_sg_free"), 1)



        @block.gpsimd
        def _(e):
            e.wait_ge(s("sprep_dve"), 2)
            e.tensor_copy(ikx[:NS, :].rearrange("p (h t) -> p h t", t=DEC_T),
                          IKH[:NS, :].unsqueeze(2).to_broadcast([NS, H_MLA, DEC_T])).then_inc(s("ikx_ready"), 1)
            for b in range(DEC_B):
                e.wait_ge(s("pages_landed"), 16 * 3 * N_PAGES * (b + 1))
                if b:
                    e.wait_ge(s("ir_psum"), 4 * b)
                e.tensor_copy(ire.rearrange("p g (h t) -> p (g h) t", t=DEC_T),
                              irb.rearrange("p g h -> p (g h)").unsqueeze(2).to_broadcast([P, N_PAGES * H_MLA, DEC_T]))\
                    .then_inc(s("ire_ready"), 1)

            e.wait_ge(s("route_ready"), T)
            e.wait_ge(s("sample_spread"), 48)
            with e.Fori(0, UNITS // 2) as i:
                for p in range(2):
                    u = i * 2 + p
                    e.wait_ge(s("buffers_free"), u * (2 * TOPK) + 1)
                    e.tensor_copy(idx_cur[:, p, :], idx_all[:, bass.ds(u * TOPK, TOPK)]).then_inc(s("idx_ready"), 1)
                    e.wait_ge(s("idx_ready"), u + 1)
                    for k in range(2 * TOPK):
                        e.wait_ge(s("buffers_free"), u * (2 * TOPK) + k + 1)
                        e.sem_inc(s("slots_granted"), 1)
                        e.indirect_dma_start(out=ring[:, k % RING, :], out_offset=None,
                                             in_=(a["peer_u"] if k < TOPK else a["peer_v"])[0],
                                             in_offset=bass.IndirectOffsetOnAxis(ap=idx_cur[:, p, k % TOPK:k % TOPK + 1], axis=0))\
                            .then_inc(s(f"rows_landed{k % RING}"), 16)


_OUTS = [("y_p", (1, SEQ, D)), ("y_s", (DEC_B, DEC_T, D)), ("lat_p", (1, 1, SEQ, KVR)), ("kr_p", (1, 1, SEQ, ROPE)),
         ("ir_p", (1, 1, SEQ, H_MLA)), ("gla_p", (1, 1, H_GLA, GK, GV)), ("lat_s", (1, DEC_B, DEC_T, KVR)),
         ("kr_s", (1, DEC_B, DEC_T, ROPE)), ("ir_s", (1, DEC_B, DEC_T, H_MLA)), ("gla_s", (1, DEC_B, H_GLA, GK, GV))]


def kernel(**inputs):
    import concourse.bacc as bacc
    from concourse.bass_utils import run_bass_kernel_spmd

    nc = bacc.Bacc("TRN2", target_bir_lowering=False, num_devices=1)
    arrays, a, o, c = {}, {}, {}, {}
    for name, value in inputs.items():
        v = np.ascontiguousarray(value)
        arrays[f"in_{name}"] = v
        a[name] = nc.dram_tensor(f"in_{name}", v.shape, mybir.dt.from_np(v.dtype), kind="ExternalInput").ap()
    for name, v in constants().items():
        arrays[f"const_{name}"] = v
        c[name] = nc.dram_tensor(f"const_{name}", v.shape, F32, kind="ExternalInput").ap()
    for name, shape in _OUTS:
        o[name] = nc.dram_tensor(f"out_{name}", shape, F32, kind="ExternalOutput").ap()
    build(nc, a, o, c)
    r = run_bass_kernel_spmd(nc, [arrays], core_ids=[0])
    return tuple(r.results[0][f"out_{name}"] for name, _ in _OUTS)
```

```python
from contextlib import ExitStack

import numpy as np

import concourse.bass as bass
import concourse.mybir as mybir

ALU = mybir.AluOpType
ACT = mybir.ActivationFunctionType
AX = mybir.AxisListType.X
F32 = mybir.dt.float32
U32 = mybir.dt.uint32
I32 = mybir.dt.int32

P = 128
D = 2048
KD = D // P
SEQ = 512
DEC_B, DEC_T = 8, 8
NS = DEC_B * DEC_T
NTOK = SEQ + NS
PT = SEQ // P
T = PT + 1
ROWS = [P] * PT + [NS]
PAGE = 128
N_PAGES = 16
N_POOL = 160
PAST = PAGE * N_PAGES
H_MLA, NOPE, ROPE, DV = 8, 128, 64, 128
QK = NOPE + ROPE
QR, KVR = 512, 256
SCALE = QK ** -0.5
THETA = 10000.0
H_GLA, GK, GV = 4, 128, 256
GATE_R = 16
TAU = 16.0
IN_SPLITS = (QR, KVR, ROPE, H_GLA * GK, H_GLA * GK, H_GLA * GV, H_GLA * GV, GATE_R)
IN_COLS = sum(IN_SPLITS)
MLA_COLS = QR + KVR + ROPE
GLA_COLS = IN_COLS - MLA_COLS
IN_BLOCKS = 16
IN_NC = IN_COLS // IN_BLOCKS
NC = 256
NBLK = D // NC
GROUPS = [[0, 1], [2, 3, 4]]
PLE_GROUPS = [[0, 1], [2, 3], [4]]
MT = 3
HH = H_MLA // 2
PH, NKEY, TOPK = 8, 128, 16
PLE = 256
EPS = 1e-6
NEG = -1e30
LOWEST = -3e38
LEVELS = [64, 32, 16, 8, 4, 2, 1]
NLEV = len(LEVELS) + 1
SAMPLE_LEVEL0 = LEVELS.index(DEC_T // 2)
UNITS = PH * PT + PH // 2
PASSES = {}
_landed = _served = 0
for _name, _nt, _nb in (("in0", 2, IN_BLOCKS), ("out0", 2, NBLK), ("query0", 2, PH), ("in1", 3, IN_BLOCKS),
                        ("out1", 3, NBLK), ("query1", 2, PH), ("gate0", 2, NBLK), ("gate1", 2, NBLK), ("gate2", 1, NBLK)):
    PASSES[_name] = (_landed, _served)
    _landed += _nb // 2
    _served += _nb * _nt
IN_READ = {"in0": 4, "in1": 4 + 2 * IN_BLOCKS}
ADDED = {"out0": 4, "out1": 4 + 2 * NBLK, "gate0": 4 + 5 * NBLK, "gate1": 4 + 7 * NBLK, "gate2": 4 + 9 * NBLK}
NORMS = {k: n for n, k in enumerate(
    [(use, t) for g in GROUPS for use in ("x", "mix", "ffn") for t in g] + [("ple", t) for t in range(T)])}
HALVES = {k: n for n, k in enumerate([(hh, t) for g in GROUPS for hh in range(2) for t in g])}
PHALVES = {k: n for n, k in enumerate([(hh, t) for g in GROUPS for hh in range(2) for t in g if t < PT])}
GAINS = [(use, g[0]) for g in GROUPS for use in ("x", "mix", "ffn")] + [("ple", g[0]) for g in PLE_GROUPS]
Z_BEFORE = [32, 32 + 16 * 2 * IN_BLOCKS // 2]
Z_STORED = [Z_BEFORE[1], Z_BEFORE[1] + 16 * 3 * IN_BLOCKS // 2]
EMBEDDED = [0, 2 * NBLK, 4 * NBLK]
STEP, SEGMENT = 0, 1
STEPS_PER_SLOT = 2
RING = 8


SEGMENTS = [1, 3, 2, 1, 2, 3, 2, 3, 3, 3, 3, 2, 2, 2, 2, 2] + [1, 1, 0, 1, 1, 1, 1, 1] + [0] * 8 + [0, 2, 2, 1]


def constants():
    i = np.arange(P)
    c = {"ident": np.eye(P, dtype=np.float32)}
    c["tri"] = (i[:, None] <= i[None, :]).astype(np.float32)
    j = np.arange(NS)
    same = (j[:, None] // DEC_T) == (j[None, :] // DEC_T)
    tri_s = np.zeros((P, NS), np.float32)
    tri_s[:NS] = (j[:, None] <= j[None, :]) & same
    c["tri_s"] = tri_s
    lev = np.zeros((P, NLEV, P), np.float32)
    for n, half in enumerate(LEVELS):
        s, t = i[:, None], i[None, :]
        lev[:, n] = (s // (2 * half) == t // (2 * half)) & (s % (2 * half) < half) & (t % (2 * half) >= half)
    lev[:, NLEV - 1] = np.eye(P)
    c["lev"] = lev
    c["causal"] = np.where(i[None, :] <= i[:, None], 0.0, NEG).astype(np.float32)
    m = np.full((P, DEC_B, DEC_B, DEC_T), NEG, np.float32)
    for b in range(DEC_B):
        for h in range(H_MLA):
            for t in range(DEC_T):
                m[h * DEC_T + t, b, b, :t + 1] = 0.0
    c["smask"] = m.reshape(P, DEC_B * NS)
    bm = np.zeros((P, DEC_B), np.float32)
    bm[j, j // DEC_T] = 1.0
    c["bmask"] = bm
    half = ROPE // 2
    inv = np.float32(THETA) ** (-np.arange(half, dtype=np.float32) / np.float32(half))
    pos = np.zeros((P, T), np.float32)
    for t in range(PT):
        pos[:, t] = t * P + i
    pos[:NS, PT] = PAST + j % DEC_T
    ang = pos[:, :, None] * inv
    cos, sin = np.cos(ang), np.sin(ang)
    c["cos"] = np.concatenate([cos, cos], -1).astype(np.float32)
    c["sin"] = np.concatenate([-sin, sin], -1).astype(np.float32)
    c["iota16"] = np.tile(np.arange(TOPK, dtype=np.float32), (P, 1))
    return c


def build(nc, a, o, c):
    ctx = ExitStack()
    with ctx:
        sems = {}

        def s(name):
            if name not in sems:
                sems[name] = nc.alloc_semaphore(name)
            return sems[name]

        def sb(name, shape, dt=F32):
            return ctx.enter_context(nc.sbuf_tensor(name, shape, dt))

        ring = sb("ring", [P, RING, D])
        acc = sb("acc", [P, 2, D])
        xrow = sb("xrow", [P, 2, D])
        ident = sb("ident", [P, P])
        tri, tri_s = sb("tri", [P, P]), sb("tri_s", [P, NS])
        lev = sb("lev", [P, NLEV, P])
        causal = sb("causal", [P, P])
        smask = sb("smask", [P, DEC_B, NS])
        bmask = sb("bmask", [P, DEC_B])
        cosT, sinT = sb("cosT", [P, T, ROPE]), sb("sinT", [P, T, ROPE])
        iota16 = sb("iota16", [P, TOPK])
        pages = sb("pages", [1, DEC_B * N_PAGES], I32)
        eps = sb("eps", [P, 1])
        ones = sb("ones", [1, P])
        idx_all = sb("idx_all", [P, UNITS * TOPK], U32)
        gate_all = sb("gate_all", [P, UNITS * TOPK])
        idx_cur = sb("idx_cur", [P, 2, TOPK], U32)
        dots, gel, coef = sb("dots", [P, TOPK]), sb("gel", [P, TOPK]), sb("coef", [P, TOPK])
        ns = len(NORMS)
        st = sb("st", [P, 3 * ns])
        ms = sb("ms", [P, 112])
        FW = 24304
        front = sb("front", [P, FW])
        used = [0]

        def carve(*shape, at=None):
            if at is not None:
                used[0] = at
            n = int(np.prod(shape))
            ap = front[:, used[0]:used[0] + n]
            used[0] += n
            assert used[0] <= FW, used[0]
            if len(shape) == 2:
                ap = ap.rearrange("p (a b) -> p a b", b=shape[1])
            if len(shape) == 3:
                ap = ap.rearrange("p (a b c) -> p a b c", b=shape[1], c=shape[2])
            return ap

        GT = 2 * P + NS
        XT = carve(KD, GT, at=0)
        W = [carve(KD * NC), carve(KD * NC)]
        h0 = used[0]
        H = carve(MT, D)
        y0 = used[0]
        Y = carve(D)
        G = carve(D)
        zst = carve(2 * MT, NC, at=h0)
        topv, topi = carve(MT, 16, TOPK, at=h0), carve(MT, 16, TOPK)
        swork = carve(MT, P)
        topu = carve(MT, TOPK).bitcast(U32)
        qTm = carve(2, GT)
        keysT, keysR = carve(2, P), carve(2, P)
        sela, selh, sell = [carve(P).bitcast(U32) for _ in range(3)]
        selhf, sellf, e1, e2, gtop = [carve(P) for _ in range(5)]
        gsum = carve(PH)
        ixs_hi, gts_hi = carve(64)[0:NS].bitcast(U32), carve(64)[0:NS]
        assert used[0] <= y0
        cand, candw = Y, G
        oneh = front[:, 0:D]
        pT_ple = carve(PLE // P, 2 * P, at=y0)
        p_row = carve(2, PLE)
        w_pp = [carve(PLE // P, NC), carve(PLE // P, NC)]
        sg = G.rearrange("p (a b) -> p a b", a=8)

        c_rows, cT = carve(KVR, at=0), carve(MT, KVR // P, P)
        kr_o = carve(MT, ROPE)
        qgT, qrT = carve(H_MLA, NS), carve(DEC_B, NS)
        low = used[0]
        m_z, cqn, cqT, kr_g = carve(MLA_COLS), carve(QR), carve(MT, QR // P, P), carve(ROPE)
        g_q, g_kv, g_k, g_qk = carve(QR), carve(KVR), carve(QK), carve(QK)
        half0 = used[0]
        wq, wk, wv = carve(QR // P, HH * QK), carve(KVR // P, HH * NOPE), carve(KVR // P, HH * DV)
        KTn, KTr, V = carve(HH, SEQ), carve(HH // 2, SEQ), carve(PT, HH * DV)
        qrow, krow, sqs = carve(HH, QK), carve(HH, NOPE), carve(HH * QK)
        qro, kro, rtmp = carve(HH, ROPE), carve(HH, ROPE), carve(HH, ROPE)
        QTn, QTr = carve(HH, P), carve(HH // 2, P)
        pr, pT = carve(2, SEQ), carve(2, SEQ)
        orow = carve(HH * DV)
        sc = carve(PAST + NS, at=low)
        latT = carve(3, 512)
        krT, ikx = carve(NS), carve(NS)
        assert used[0] <= half0
        pages_sb = []
        used[0] = half0
        for _ in range(2):
            pages_sb.append((carve(N_PAGES, KVR), carve(N_PAGES, ROPE), carve(N_PAGES, H_MLA)))
        wuv_f = carve(KVR // P, H_MLA * DV)
        pTs = carve(N_PAGES + 1, NS)
        q_lat = [carve(DEC_B, NS), carve(DEC_B, NS)]
        oT = [carve(H_MLA, NS), carve(H_MLA, NS)]
        olr = carve(KVR)
        ire = carve(N_PAGES, NS)
        irs = carve(512)
        wuk_f, w_ukT = carve(KVR // P, H_MLA * NOPE, at=half0), carve(H_MLA, KVR)
        so_rows = carve(H_MLA * DV, at=half0)
        gz = carve(GLA_COLS, at=0)
        w_ga, g_go = carve(H_GLA * GK), carve(GV)
        S0 = carve(H_GLA, GV)
        Ss = [carve(DEC_B, GV), carve(DEC_B, GV)]
        gx, gt1, gt2 = carve(H_GLA * GK), carve(H_GLA * GK), carve(H_GLA * GK)
        alT = carve(P)
        gqT, gkT, gbT = carve(H_GLA * GK), carve(H_GLA * GK), carve(H_GLA * GK)
        Mlev = carve(NLEV - 1, H_GLA * P)
        dlev = carve(2, H_GLA * P)
        am = carve(NLEV, P)
        AT = carve(H_GLA, P)
        eb, qe, kd = carve(H_GLA * P), carve(H_GLA * P), carve(H_GLA * P)
        kdr = carve(H_GLA, GK)
        go, gsil = carve(H_GLA * GV), carve(H_GLA * GV)
        gsq = dlev.rearrange("p a b -> p (a b)")
        qz, kz = carve(DEC_B, NS), carve(DEC_B, GK)
        eL = carve(H_GLA * DEC_B)

        bank = [ctx.enter_context(nc.psum_tensor(f"bank{i}", [P, 512], F32)) for i in range(8)]

        def scratch(name, *shape):
            return nc.dram_tensor(name, list(shape), F32).ap()

        z_dram = scratch("z_dram", NTOK, IN_COLS)
        mix_dram = scratch("mix_dram", NTOK, D)
        h_dram = scratch("h_dram", NTOK, D)
        xn_dram = scratch("xn_dram", NTOK, D)
        h2_dram = scratch("h2_dram", NTOK, D)
        kt_dram = scratch("kt_dram", 2, P, HH, 2 * P)
        ktr_dram = scratch("ktr_dram", 2, P, HH // 2, 2 * P)
        v_dram = scratch("v_dram", 2, P, 2, HH * DV)
        s_dram = scratch("s_dram", P, H_GLA, GV)

        def rows(t):
            return slice(t * P, t * P + ROWS[t])

        def tile_of(prompt, sample, t):
            return prompt[rows(t), :] if t < PT else sample.rearrange("b t d -> (b t) d")

        def x_rows(t):
            return tile_of(a["x_prompt"][0], a["x_sample"], t)

        def down(dram_row, n=P):
            return dram_row.partition_broadcast(n)

        def slot(t):
            return t - (0 if t < 2 else 2)

        def pairs(e, lo, hi, looped):
            if looped:
                with e.Fori(lo, hi) as i:
                    yield i
            else:
                for i in range(lo, hi):
                    yield i

        SSQ, RQ, IQ = ms[:, 0:1], ms[:, 1:2], ms[:, 2:3]
        SSC, RC, IC = ms[:, 3:4], ms[:, 4:5], ms[:, 5:6]
        SQH, RQH, IQH = ms[:, 8:12], ms[:, 12:16], ms[:, 16:20]
        SKH, RKH = ms[:, 20:24], ms[:, 24:28]
        MXV, NMX, RSUM, RINV = ms[:, 28:32], ms[:, 32:36], ms[:, 36:40], ms[:, 40:44]
        GSS, GRS, GIS = ms[:, 44:48], ms[:, 48:52], ms[:, 52:56]

        def SKR(t):
            return ms[:, 56 + slot(t):57 + slot(t)]

        def IKH(t):
            return ms[:, 64 + 8 * slot(t):72 + 8 * slot(t)]

        def heads(ap, R):
            return ap[:, 0:H_GLA * P].rearrange("p (h n) -> p h n", h=H_GLA)[:, :, 0:R]

        def level_count(t, n):
            per = NLEV - 1
            return t * per + n if t < PT else PT * per + n - SAMPLE_LEVEL0

        def by_batch(ap, h0_=0, n=H_MLA):
            return ap.rearrange("p b (h t) -> p h b t", h=H_MLA)[:, h0_:h0_ + n]

        def four(ap, R=P):
            return ap[:, :].rearrange("p (j n) -> p j n", j=4)[:, :, 0:R]

        def out_bank(p, sl):
            return bank[3 * p + sl]

        block = ctx.enter_context(nc.Block())

        @block.sync
        def _(e):
            def weight_blocks(name, w, ncol, nblk, nt, extra=None):
                served = PASSES[name][1]

                def load(i, p):
                    col = bass.ds((i * 2 + p) * ncol, ncol)
                    e.dma_start(W[p][:, 0:KD * ncol].rearrange("p (k n) -> p k n", k=KD),
                                w[:, col].rearrange("(k p) n -> p k n", p=P)).then_inc(s(f"w_landed{p}"), 16)
                    if extra is not None:
                        e.dma_start(w_pp[p], extra[:, col].rearrange("(k p) n -> p k n", p=P))\
                            .then_inc(s(f"embed_w_landed{p}"), 16)
                load(0, 0)
                load(0, 1)
                with e.Fori(1, nblk // 2) as i:
                    for p in range(2):
                        e.wait_ge(s("tiles_projected"), (i * 2 + p - 1) * nt + served)
                        load(i, p)

            for name, dst in (("ident", ident), ("tri", tri), ("tri_s", tri_s), ("lev", lev), ("causal", causal),
                              ("bmask", bmask), ("cos", cosT), ("sin", sinT), ("iota16", iota16)):
                v = dst[:, :] if name not in ("lev", "cos", "sin") else dst[:, :, :]
                e.dma_start(v, c[name]).then_inc(s("consts_loaded"), 16)
            e.dma_start(smask[:, :, :].rearrange("p a b -> p (a b)"), c["smask"]).then_inc(s("consts_loaded"), 16)
            e.dma_start(pages[:, :], a["page_table"].rearrange("b n -> (b n)").rearrange("(o n) -> o n", o=1))\
                .then_inc(s("consts_loaded"), 16)

            def mixer_loads(g):
                tiles = GROUPS[g]
                nt = len(tiles)
                if g:
                    e.wait_ge(s("route_ready"), 2)
                for t in tiles:
                    e.dma_start(H[:ROWS[t], slot(t), :], x_rows(t)).then_inc(s("rows_loaded"), 16)
                e.dma_start(G, down(a["norm_mix"][0])).then_inc(s("gain_loaded"), 16)
                weight_blocks(f"in{g}", a["w_in"][0], IN_NC, IN_BLOCKS, nt)

                e.wait_ge(s("tiles_projected"), PASSES[f"out{g}"][1])
                e.wait_ge(s("z_stored0"), Z_STORED[g])
                e.wait_ge(s("z_stored1"), Z_STORED[g])
                for dst, src in ((g_q, down(a["norm_q_lat"][0])), (g_kv, down(a["norm_kv_lat"][0])),
                                 (g_k, down(a["qk_gain_k"][0])), (g_qk, down(a["qk_gain_q"][0]))):
                    e.dma_start(dst, src).then_inc(s("mla_gains_loaded"), 16)
                for t in tiles:
                    R = ROWS[t]
                    if t:
                        e.wait_ge(s("rope_key_ready"), t)
                    e.dma_start(m_z[:R, :], z_dram[rows(t), 0:MLA_COLS]).then_inc(s("mla_z_loaded"), 16)
                    if t == tiles[0]:
                        half_weights(g, 0)
                    e.wait_ge(s("mla_latents_normed"), t + 1)
                    e.dma_start(tile_of(o["lat_p"][0, 0], o["lat_s"][0], t), c_rows[:R, :]).then_inc(s("lat_stored"), 16)
                    e.wait_ge(s("rope_key_ready"), t + 1)
                    e.dma_start(tile_of(o["kr_p"][0, 0], o["kr_s"][0], t), kr_o[:R, slot(t), :]).then_inc(s("mla_outputs"), 16)
                for hh in range(2):
                    if hh:
                        half_weights(g, hh)
                    for t in tiles:
                        if t < PT:
                            n = PHALVES[hh, t]
                            e.wait_ge(s("mla_o_rows"), n + 1)
                            e.dma_start(mix_dram[rows(t), hh * HH * DV:(hh + 1) * HH * DV], orow).then_inc(s("o_stored"), 16)
                    if g == 0:
                        e.wait_ge(s("kT_sb"), PHALVES[hh, 1] + 1)
                        e.wait_ge(s("v_sb"), PHALVES[hh, 1] + 1)
                        e.dma_start(kt_dram[hh], KTn[:, :, 0:2 * P]).then_inc(s("keys_parked"), 16)
                        e.dma_start(ktr_dram[hh], KTr[:, :, 0:2 * P]).then_inc(s("keys_parked"), 16)
                        e.dma_start(v_dram[hh], V[:, 0:2, :]).then_inc(s("keys_parked"), 16)
                for t in tiles:
                    e.wait_ge(s("ikh_ready"), HALVES[1, t] + 1)
                    e.dma_start(tile_of(o["ir_p"][0, 0], o["ir_s"][0], t), IKH(t)[:ROWS[t], :]).then_inc(s("mla_outputs"), 16)

                if g:
                    e.wait_ge(s("pv_done"), HH * len(PHALVES))
                    e.wait_ge(s("o_stored"), 16 * len(PHALVES))
                    e.wait_ge(s("q_rows_ready"), len(HALVES))
                    e.wait_ge(s("k_rows_ready"), len(HALVES))
                    e.wait_ge(s("sample_qT_psum"), 2)
                    e.dma_start(wuk_f, a["w_uk"][0].rearrange("(k p) h d -> p k (h d)", p=P)).then_inc(s("sample_w_loaded"), 16)
                    e.dma_start(wuv_f, a["w_uv"][0].rearrange("(k p) h d -> p k (h d)", p=P)).then_inc(s("sample_w_loaded"), 16)
                    e.wait_ge(s("sprep_psum"), 6)
                    for b in range(DEC_B):
                        if b >= 2:
                            e.wait_ge(s("olat_psum"), b - 1)
                        for q in range(N_PAGES):
                            i = b * N_PAGES + q
                            pg = e.value_load(pages[0:1, i:i + 1], min_val=0, max_val=N_POOL - 1)
                            for dst, pool in zip(pages_sb[b % 2], ("cache_kv_latent", "cache_k_rope", "cache_k_inv_rms")):
                                e.dma_start(dst[:, q, :], a[pool][0, bass.ds(pg, 1), :, :].rearrange("o p d -> (o p) d"))\
                                    .then_inc(s(f"pages_landed{b % 2}"), 16)
                    e.wait_ge(s("sample_o_rows"), 1)
                    e.dma_start(mix_dram[rows(PT), 0:H_MLA * DV], so_rows[:NS, :]).then_inc(s("o_stored"), 16)

                e.wait_ge(s("o_stored"), 16 * (4 if g == 0 else 9))
                e.wait_ge(s("mla_outputs"), 16 * 2 * (2 if g == 0 else T))
                e.wait_ge(s("lat_stored"), 16 * (tiles[-1] + 1))
                if g == 0:
                    e.wait_ge(s("keys_parked"), 16 * 6)
                e.dma_start(w_ga[0:GATE_R, :], a["w_gla_a"][0]).then_inc(s("gla_w_loaded"), 16)
                e.dma_start(w_ga[GATE_R:GATE_R + 1, :], a["b_gla_a"][0].rearrange("(o n) -> o n", o=1)).then_inc(s("gla_w_loaded"), 16)
                e.dma_start(g_go, down(a["norm_gla_out"][0])).then_inc(s("gla_w_loaded"), 16)
                if g:
                    e.dma_start(S0, s_dram).then_inc(s("gla_w_loaded"), 16)

                def head_state(h):
                    e.dma_start(Ss[h % 2], a["state_gla"][0, :, h].rearrange("b k v -> k b v")).then_inc(s(f"state_loaded{h % 2}"), 16)

                for t in tiles:
                    if t != tiles[0]:
                        e.wait_ge(s("gla_read"), t)
                    e.dma_start(gz[:ROWS[t], :], z_dram[rows(t), MLA_COLS:IN_COLS]).then_inc(s("gla_z_loaded"), 16)
                    if t == PT:
                        head_state(0)
                        head_state(1)
                        for h in range(H_GLA):
                            e.wait_ge(s("sample_state_head"), h + 1)
                            e.dma_start(o["gla_s"][0, :, h].rearrange("b k v -> k b v"), Ss[h % 2]).then_inc(s("state_out"), 16)
                            if h < 2:
                                e.wait_ge(s("state_out"), 16 * (h + 3))
                                head_state(h + 2)
                    e.wait_ge(s("gla_o_ready"), t + 1)
                    e.dma_start(mix_dram[rows(t), H_MLA * DV:D], go[:ROWS[t], :]).then_inc(s("go_stored"), 16)
                    if t == 1:
                        e.wait_ge(s("gla_state"), H_GLA * 2)
                        e.dma_start(s_dram, S0).then_inc(s("state_out"), 16)
                        e.wait_ge(s("state_out"), 16)
                    if t == PT - 1:
                        e.wait_ge(s("gla_state"), H_GLA * PT)
                        e.dma_start(o["gla_p"][0, 0].rearrange("h k v -> k h v"), S0).then_inc(s("state_out"), 16)
                        e.wait_ge(s("state_out"), 32)

                e.wait_ge(s("go_stored"), 16 * (tiles[-1] + 1))
                if g:
                    e.wait_ge(s("state_out"), 16 * 6)
                for t in tiles:
                    e.dma_start(H[:ROWS[t], slot(t), :], mix_dram[rows(t), :]).then_inc(s("rows_loaded"), 16)
                e.dma_start(G[:, 0:H_MLA * DV], down(a["norm_mla_out"][0])).then_inc(s("gain_loaded"), 16)

                def residual_rows():
                    for t in tiles:
                        e.wait_ge(s("nt_transposed"), 4 * (NORMS["mix", t] + 1))
                        e.dma_start(H[:ROWS[t], slot(t), :], x_rows(t)).then_inc(s("rows_loaded"), 16)
                    e.wait_ge(s("normed"), NORMS["mix", tiles[-1]] + 1)
                    e.dma_start(G, down(a["norm_ffn"][0])).then_inc(s("gain_loaded"), 16)

                residual_rows()
                weight_blocks(f"out{g}", a["w_out"][0], NC, NBLK, nt)
                for t in tiles:
                    e.wait_ge(s("rows_added"), ADDED[f"out{g}"] + (NBLK - 1) * nt + slot(t) + 1)
                    e.dma_start(h_dram[rows(t), :], H[:ROWS[t], slot(t), :]).then_inc(s("h_stored"), 16)
                for t in tiles:
                    e.wait_ge(s("normed"), NORMS["ffn", t] + 1)
                    e.dma_start(xn_dram[rows(t), :], Y[:ROWS[t], :]).then_inc(s("xn_stored"), 16)
                weight_blocks(f"query{g}", a["peer_w_q"][0], NC, PH, 2)

            def half_weights(g, hh):
                n = 2 * g + hh
                if hh:
                    e.wait_ge(s("k_ready"), HALVES[1, GROUPS[g][0]])
                    e.wait_ge(s("v_ready"), PHALVES[1, GROUPS[g][0]])
                e.dma_start(wq, a["w_uq"][0][:, hh * HH * QK:(hh + 1) * HH * QK].rearrange("(k p) n -> p k n", p=P))\
                    .then_inc(s("half_w_loaded"), 16)
                e.dma_start(wk, a["w_uk"][0][:, hh * HH:(hh + 1) * HH, :].rearrange("(k p) h d -> p k (h d)", p=P))\
                    .then_inc(s("half_w_loaded"), 16)
                e.dma_start(wv, a["w_uv"][0][:, hh * HH:(hh + 1) * HH, :].rearrange("(k p) h d -> p k (h d)", p=P))\
                    .then_inc(s("half_w_loaded"), 16)
                if g:
                    if hh:
                        e.wait_ge(s("pv_done"), HH * PHALVES[1, 2])
                    e.dma_start(KTn[:, :, 0:2 * P], kt_dram[hh]).then_inc(s("old_keys_loaded"), 16)
                    e.dma_start(KTr[:, :, 0:2 * P], ktr_dram[hh]).then_inc(s("old_keys_loaded"), 16)
                    e.dma_start(V[:, 0:2, :], v_dram[hh]).then_inc(s("old_keys_loaded"), 16)

            def embedding_loads(pg):
                tiles = PLE_GROUPS[pg]
                nt = len(tiles)
                if pg == 0:
                    e.wait_ge(s("route_ready"), T)
                else:
                    e.wait_ge(s("y_out"), 16 * PLE_GROUPS[pg][0])
                for t in tiles:
                    if t < PT:
                        e.wait_ge(s("h2_stored"), 16 * (t + 1))
                        e.dma_start(H[:ROWS[t], t % 2, :], h2_dram[rows(t), :]).then_inc(s("rows_loaded"), 16)
                if pg:
                    e.wait_ge(s("rows_added"), ADDED[f"gate{pg}"])
                e.dma_start(G, down(a["norm_ple"][0])).then_inc(s("gain_loaded"), 16)
                e.wait_ge(s("nt_transposed"), 4 * (NORMS["ple", tiles[-1]] + 1))
                for t in tiles:
                    e.dma_start(p_row[:ROWS[t], t % 2, :], tile_of(a["p_prompt"][0, 0], a["p_sample"][0], t))\
                        .then_inc(s("p_loaded"), 16)
                weight_blocks(f"gate{pg}", a["w_ple_gate"][0], NC, NBLK, nt, extra=a["w_ple_proj"][0])
                for t in tiles:
                    e.wait_ge(s("rows_added"), ADDED[f"gate{pg}"] + (NBLK - 1) * nt + t % 2 + 1)
                    e.dma_start(tile_of(o["y_p"][0], o["y_s"], t), H[:ROWS[t], t % 2, :]).then_inc(s("y_out"), 16)

            mixer_loads(0)
            mixer_loads(1)
            e.wait_ge(s("route_ready"), T)
            lo = slice(PH * PT * TOPK, UNITS * TOPK)
            e.dma_start(idx_all[NS:P, lo], ixs_hi).then_inc(s("sample_spread"), 16)
            e.dma_start(gate_all[NS:P, lo], gts_hi).then_inc(s("sample_spread"), 16)
            e.wait_ge(s("sample_spread"), 32)
            for pg in range(len(PLE_GROUPS)):
                embedding_loads(pg)
            e.wait_ge(s("y_out"), 16 * T)

        @block.tensor
        def _(e):
            def norm_transposes(use, tiles):
                for t in tiles:
                    R = ROWS[t]
                    n = NORMS[use, t]
                    sl = slot(t) if use != "ple" else t % 2
                    e.wait_ge(s("normed"), n + 1)
                    for q in range(4):
                        m = 4 * n + q
                        if m >= 2:
                            e.wait_ge(s("nt_evacuated"), m - 1)
                        for j in range(4):
                            k = 4 * q + j
                            src = H[:R, sl, k * P:(k + 1) * P] if use == "mix" and k >= 8 else Y[:R, k * P:(k + 1) * P]
                            mm = e.transpose(bank[6 + m % 2][:, j * P:j * P + R], src, ident[:R, :R])
                        mm.then_inc(s("nt_transposed"), 1)

            def project(name, tiles, ncol, nblk, free, free0, embed=False):
                nt = len(tiles)
                landed = PASSES[name][0]
                pg = int(name[-1])
                with e.Fori(0, nblk // 2) as i:
                    for p in range(2):
                        w = W[p][:, 0:KD * ncol].rearrange("p (k n) -> p k n", k=KD)
                        e.wait_ge(s(f"w_landed{p}"), (i + landed + 1) * 16)
                        if embed:
                            e.wait_ge(s(f"embed_w_landed{p}"), (i + pg * NBLK // 2 + 1) * 16)
                        for sl, t in enumerate(tiles):
                            R = ROWS[t]
                            u = (i * 2 + p) * nt + sl
                            if embed:
                                x = (p * nt + sl) % 2
                                e.wait_ge(s("embed_read"), u + EMBEDDED[pg] + 1)
                                for k in range(PLE // P):
                                    e.matmul(bank[6 + x][:R, 0:NC], pT_ple[:, k, sl * P:sl * P + R], w_pp[p][:, k, :],
                                             start=(k == 0), stop=(k == 1))
                            e.wait_ge(s(free), u + (free0 - 2 * nt + 1))
                            for k in range(KD):
                                mm = e.matmul(out_bank(p, sl)[:R, 0:ncol], XT[:, k, sl * P:sl * P + R], w[:, k, :],
                                              start=(k == 0), stop=(k == KD - 1))
                            mm.then_inc(s("tiles_projected"), 1)

            def latent_attention(g):
                tiles = GROUPS[g]
                for t in tiles:
                    R = ROWS[t]
                    e.wait_ge(s("mla_latents_normed"), t + 1)
                    if t:
                        e.wait_ge(s("latT_ready"), t)
                    for k in range(4):
                        e.transpose(bank[0][:, k * P:k * P + R], cqn[:R, k * P:(k + 1) * P], ident[:R, :R])
                    for k in range(2):
                        mm = e.transpose(bank[1][:, k * P:k * P + R], c_rows[:R, k * P:(k + 1) * P], ident[:R, :R])
                    mm.then_inc(s("lat_transposed"), 1)
                e.wait_ge(s("latT_ready"), tiles[-1] + 1)
                for hh in range(2):
                    e.wait_ge(s("half_w_loaded"), 48 * (2 * g + hh + 1))
                    for t in tiles:
                        R = ROWS[t]
                        n = HALVES[hh, t]
                        m = PHALVES[hh, t] if t < PT else len(PHALVES)
                        before = sum(1 for k, v in HALVES.items() if v < n and k[1] < PT)
                        if n:
                            e.wait_ge(s("q_rows_ready"), n)
                            e.wait_ge(s("k_rows_ready"), n)
                        if before:
                            e.wait_ge(s("exp_done"), HH * before)
                            e.wait_ge(s("pT_sb"), HH * before)
                            e.wait_ge(s("v_sb"), before)
                        for j in range(2):
                            for k in range(4):
                                mm = e.matmul(bank[j][:R, 0:2 * QK], cqT[:, slot(t), k, 0:R], wq[:, k, j * 2 * QK:(j + 1) * 2 * QK],
                                              start=(k == 0), stop=(k == 3))
                        mm.then_inc(s("q_ready"), 1)
                        for k in range(2):
                            mm = e.matmul(bank[2][:R, :], cT[:, slot(t), k, 0:R], wk[:, k, :], start=(k == 0), stop=(k == 1))
                        mm.then_inc(s("k_ready"), 1)
                        if t < PT:
                            for k in range(2):
                                mm = e.matmul(bank[3][:R, :], cT[:, slot(t), k, 0:R], wv[:, k, :], start=(k == 0), stop=(k == 1))
                            mm.then_inc(s("v_ready"), 1)
                        e.wait_ge(s("q_rows_ready"), n + 1)
                        if t == PT:
                            if before:
                                e.wait_ge(s("mla_o_rows"), before)
                            if hh:
                                e.wait_ge(s("sample_qT_sb"), 1)
                            for h in range(HH):
                                e.transpose(bank[4][:, h * NS:(h + 1) * NS], qrow[:NS, h, 0:NOPE], ident[:NS, :NS])
                            for h in range(HH):
                                mm = e.transpose(bank[5][0:ROPE, h * NS:(h + 1) * NS], qro[:NS, h, :], ident[:NS, :NS])
                            mm.then_inc(s("sample_qT_psum"), 1)
                            continue
                        if before:
                            e.wait_ge(s("mla_o_rows"), before)
                        if hh and g:
                            e.wait_ge(s("sample_qT_sb"), 1)
                        for h in range(HH):
                            e.transpose(bank[4][:, h * P:(h + 1) * P], qrow[:, h, 0:NOPE], ident[:, :])
                        for j in range(2):
                            mm = e.transpose(bank[5][:, j * P:(j + 1) * P],
                                             qro[:, 2 * j:2 * j + 2, :].rearrange("p a b -> p (a b)"), ident[:, :])
                        mm.then_inc(s("qT_psum"), 1)
                        e.wait_ge(s("k_rows_ready"), n + 1)
                        for h in range(HH):
                            e.transpose(bank[6][:, h * P:(h + 1) * P], krow[:, h, :], ident[:, :])
                        for j in range(2):
                            mm = e.transpose(bank[7][:, j * P:(j + 1) * P],
                                             kro[:, 2 * j:2 * j + 2, :].rearrange("p a b -> p (a b)"), ident[:, :])
                        mm.then_inc(s("kT_psum"), 1)
                        e.wait_ge(s("qT_sb"), m + 1)
                        e.wait_ge(s("kT_sb"), m + 1)
                        e.wait_ge(s("v_sb"), m + 1)
                        if g:
                            e.wait_ge(s("old_keys_loaded"), 48 * (hh + 1))
                        nk = (t + 1) * P

                        def scores(h):
                            if h >= 2:
                                e.wait_ge(s("exp_done"), m * HH + h - 1)
                            S = bank[h % 2]
                            r = slice((h % 2) * ROPE, (h % 2 + 1) * ROPE)
                            e.matmul(S[:, 0:nk], QTn[:, h, :], KTn[:, h, 0:nk], start=True, stop=False)
                            e.matmul(S[:, 0:nk], QTr[r, h // 2, :], KTr[r, h // 2, 0:nk], start=False, stop=False)
                            e.matmul(S[:, t * P:nk], ident[:, :], causal[:, :], start=False, stop=True)\
                                .then_inc(s("scores_ready"), 1)

                        scores(0)
                        for h in range(HH):
                            u = m * HH + h
                            if h + 1 < HH:
                                scores(h + 1)
                            e.wait_ge(s("exp_done"), u + 1)
                            if h >= 2:
                                e.wait_ge(s("pT_sb"), u - 1)
                            for kt in range(t + 1):
                                mm = e.transpose(bank[2 + h % 2][:, kt * P:(kt + 1) * P], pr[:, h % 2, kt * P:(kt + 1) * P], ident[:, :])
                            mm.then_inc(s("pT_psum"), 1)
                            e.wait_ge(s("pT_sb"), u + 1)
                            for kt in range(t + 1):
                                mm = e.matmul(bank[4][:, h * DV:(h + 1) * DV], pT[:, h % 2, kt * P:(kt + 1) * P],
                                              V[:, kt, h * DV:(h + 1) * DV], start=(kt == 0), stop=(kt == t))
                            mm.then_inc(s("pv_done"), 1)

            def sample_attention():
                e.wait_ge(s("sample_w_loaded"), 32)
                for h in range(H_MLA):
                    for k in range(2):
                        j = h * 2 + k
                        if j % 4 == 0 and j >= 4:
                            e.wait_ge(s("sprep_act"), j // 4)
                        mm = e.transpose(bank[0][:, (j % 4) * P:(j % 4 + 1) * P], wuk_f[:, k, h * NOPE:(h + 1) * NOPE], ident[:, :])
                        if j % 4 == 3:
                            mm.then_inc(s("sprep_psum"), 1)
                e.wait_ge(s("rope_key_ready"), T)
                e.transpose(bank[1][0:ROPE, 0:NS], kr_o[:NS, slot(PT), :], ident[:NS, :NS]).then_inc(s("sprep_psum"), 1)
                e.wait_ge(s("sample_qT_sb"), 2)
                e.wait_ge(s("sprep_act"), 4)
                e.wait_ge(s("mla_o_rows"), len(PHALVES))
                for k in range(2):
                    for h in range(H_MLA):
                        mm = e.matmul(bank[4 + k][:, h * NS:(h + 1) * NS], w_ukT[:, h, k * P:(k + 1) * P], qgT[:, h, :],
                                      start=True, stop=True)
                mm.then_inc(s("sprep_psum"), 1)
                e.wait_ge(s("sprep_act"), 7)
                for b in range(DEC_B):
                    latb, krb, _ = pages_sb[b % 2]
                    e.wait_ge(s(f"pages_landed{b % 2}"), 16 * 3 * N_PAGES * (b // 2 + 1))
                    for g in range(4):
                        u = 4 * b + g
                        if u:
                            e.wait_ge(s("latT_sb"), u)
                        for j in range(4):
                            pg = 4 * g + j
                            for k in range(2):
                                e.transpose(bank[k][:, j * P:(j + 1) * P], latb[:, pg, k * P:(k + 1) * P], ident[:, :])
                            mm = e.transpose(bank[2][0:ROPE, j * P:(j + 1) * P], krb[:, pg, :], ident[:, :])
                        mm.then_inc(s("latT_psum"), 1)
                        if u:
                            e.wait_ge(s("ir_sb"), u)
                        if g == 0:
                            e.wait_ge(s("ire_ready"), b + 1)
                        for j in range(4):
                            mm = e.matmul(bank[3][0:NS, j * P:(j + 1) * P], ire[:, 4 * g + j, :], ident[:, :], start=True, stop=True)
                        mm.then_inc(s("ir_psum"), 1)
                        e.wait_ge(s("latT_sb"), u + 1)
                        if u:
                            e.wait_ge(s("scaled"), u)
                        e.matmul(bank[4][0:NS, :], q_lat[0][:, b, :], latT[:, 0, :], start=True, stop=False)
                        e.matmul(bank[4][0:NS, :], q_lat[1][:, b, :], latT[:, 1, :], start=False, stop=False)
                        e.matmul(bank[4][0:NS, :], qrT[0:ROPE, b, :], latT[0:ROPE, 2, :], start=False, stop=True)\
                            .then_inc(s("sscore_psum"), 1)
                    if b:
                        e.wait_ge(s("snew_done"), b)
                    cs = cT[:, slot(PT)]
                    e.matmul(bank[5][0:NS, 0:NS], q_lat[0][:, b, :], cs[:, 0, 0:NS], start=True, stop=False)
                    e.matmul(bank[5][0:NS, 0:NS], q_lat[1][:, b, :], cs[:, 1, 0:NS], start=False, stop=False)
                    e.matmul(bank[5][0:NS, 0:NS], qrT[0:ROPE, b, :], krT[0:ROPE, :], start=False, stop=True)
                    e.matmul(bank[5][0:NS, NS:2 * NS], ikx[:NS, :], ident[:NS, :NS], start=True, stop=True).then_inc(s("snew_psum"), 1)
                    e.wait_ge(s("sexp_done"), b + 1)
                    for q in range(3):
                        v = 3 * b + q
                        if v:
                            e.wait_ge(s("spT_sb"), v)
                        for pg in range(8 * q, min(8 * q + 8, N_PAGES + 1)):
                            w = P if pg < N_PAGES else NS
                            mm = e.transpose(bank[6][:w, (pg % 8) * NS:(pg % 8 + 1) * NS], sc[:NS, pg * P:pg * P + w], ident[:NS, :NS])
                        mm.then_inc(s("spT_psum"), 1)
                    e.wait_ge(s("spT_sb"), 3 * b + 3)
                    if b:
                        e.wait_ge(s("olatT_sb"), b)
                    for pg in range(N_PAGES):
                        e.matmul(bank[7][0:NS, 0:KVR], pTs[:, pg, :], latb[:, pg, :], start=(pg == 0), stop=False)
                    e.matmul(bank[7][0:NS, 0:KVR], pTs[:NS, N_PAGES, :], c_rows[:NS, :], start=False, stop=True)\
                        .then_inc(s("olat_psum"), 1)
                    e.wait_ge(s("olat_sb"), b + 1)
                    for k in range(2):
                        mm = e.transpose(bank[7][:, 256 + k * NS:256 + (k + 1) * NS], olr[:NS, k * P:(k + 1) * P], ident[:NS, :NS])
                    mm.then_inc(s("olatT_psum"), 1)
                e.wait_ge(s("olatT_sb"), DEC_B)
                for h in range(H_MLA):
                    for k in range(2):
                        mm = e.matmul(bank[h // 4][:NS, (h % 4) * DV:(h % 4 + 1) * DV], oT[k][:, h, :],
                                      wuv_f[:, k, h * DV:(h + 1) * DV], start=(k == 0), stop=(k == 1))
                mm.then_inc(s("sprep_psum"), 1)

            def linear_attention(g):
                tiles = GROUPS[g]
                e.wait_ge(s("gla_w_loaded"), 48 if g == 0 else 48 + 64)
                for t in tiles:
                    R = ROWS[t]
                    lv0 = 0 if t < PT else SAMPLE_LEVEL0
                    e.wait_ge(s("gla_z_loaded"), 16 * (t + 1))
                    if t:
                        e.wait_ge(s("gla_read"), t)
                    e.transpose(bank[0][0:GATE_R, 0:R], gz[:R, GLA_COLS - GATE_R:GLA_COLS], ident[:R, :R]).then_inc(s("lrT_psum"), 1)
                    for h in range(H_GLA):
                        e.transpose(bank[1][:, h * P:h * P + R], gz[:R, h * GK:(h + 1) * GK], ident[:R, :R])
                    for h in range(H_GLA):
                        mm = e.transpose(bank[2][:, h * P:h * P + R], gz[:R, (H_GLA + h) * GK:(H_GLA + h + 1) * GK], ident[:R, :R])
                    mm.then_inc(s("gqkT_psum"), 1)
                    e.wait_ge(s("lrT_sb"), t + 1)
                    e.matmul(bank[3][:R, :], alT[0:GATE_R + 1, 0:R], w_ga[0:GATE_R + 1, :], start=True, stop=True)\
                        .then_inc(s("gate_pre"), 1)
                    e.wait_ge(s("gate_log"), t + 1)
                    for h in range(H_GLA):
                        mm = e.matmul(bank[4][:, h * P:h * P + R], gx[:R, h * GK:(h + 1) * GK],
                                      tri[:, :] if t < PT else tri_s[0:R, :], start=True, stop=True)
                    mm.then_inc(s("cum_psum"), 1)
                    e.wait_ge(s("levels_ready"), t + 1)
                    for h in range(H_GLA):
                        u = t * H_GLA + h
                        if h >= 2:
                            e.wait_ge(s("levels_masked"), u - 1)
                        for n in range(lv0, NLEV):
                            B = bank[2 * (h % 2) + (n - lv0) // 4]
                            dst = B[:R, ((n - lv0) % 4) * P:((n - lv0) % 4) * P + R]
                            l = Mlev[:, n, h * P:h * P + R] if n < NLEV - 1 else gkT[:, h * P:h * P + R]
                            r = l if n < NLEV - 1 else gqT[:, h * P:h * P + R]
                            mm = e.matmul(dst, l, r, start=True, stop=True)
                        mm.then_inc(s("level_products"), 1)
                    e.wait_ge(s("kdec_ready"), t + 1)
                    for h in range(H_GLA):
                        mm = e.transpose(bank[5][:R, h * GK:(h + 1) * GK], kd[:, h * P:h * P + R], ident[:, :])
                    mm.then_inc(s("kdr_psum"), 1)
                    e.wait_ge(s("kdr_sb"), t + 1)
                    for h in range(H_GLA):
                        u = t * H_GLA + h
                        e.wait_ge(s("AT_ready"), (t + 1) * H_GLA)
                        vg = gz[:R, 2 * H_GLA * GK + h * GV:2 * H_GLA * GK + (h + 1) * GV]
                        ob = bank[6 + h // 2][:R, (h % 2) * GV:(h % 2 + 1) * GV]
                        if t < PT:
                            e.matmul(ob, AT[:R, h, 0:R], vg, start=True, stop=(t == 0))
                            if t:
                                e.matmul(ob, qe[:, h * P:h * P + R], S0[:, h, :], start=False, stop=True)
                            if h >= 2:
                                e.wait_ge(s("gla_state"), u - 1)
                            e.matmul(bank[(h % 2) * 4][:, 0:GV], kdr[:R, h, :], vg, start=True, stop=True)\
                                .then_inc(s("gla_out_psum"), 1)
                        else:
                            e.wait_ge(s("qz_ready"), h + 1)
                            e.wait_ge(s(f"state_loaded{h % 2}"), 16 * (h // 2 + 1))
                            e.matmul(ob, AT[:R, h, 0:R], vg, start=True, stop=False)
                            for b in range(DEC_B):
                                mm = e.matmul(ob, qz[:, b, :], Ss[h % 2][:, b, :], start=False, stop=(b == DEC_B - 1))
                            mm.then_inc(s("gla_out_psum"), 1)
                            for b in range(DEC_B):
                                mm = e.matmul(bank[b // 2][:, (b % 2) * GV:(b % 2 + 1) * GV], kz[:R, b, :], vg,
                                              start=True, stop=True)
                            mm.then_inc(s("sample_state_psum"), 1)
                            e.wait_ge(s("sample_state_head"), h + 1)

            def queries(g):
                tiles = GROUPS[g]
                ntok = sum(ROWS[t] for t in tiles)
                landed = PASSES[f"query{g}"][0]
                e.wait_ge(s("keys_loaded"), 32 * (g + 1))
                for side in range(2):
                    mm = e.transpose(bank[0][:, side * P:(side + 1) * P], keysR[:, side, :], ident[:, :])
                mm.then_inc(s("keysT_psum"), 1)
                e.wait_ge(s("keysT_sb"), g + 1)
                e.wait_ge(s("nt_evacuated"), 4 * (NORMS["ffn", tiles[-1]] + 1))

                def query(n):
                    h, side = n // 2, n % 2
                    m = 2 * PH * g + n
                    w = W[h % 2].rearrange("p (k n) -> p k n", k=KD)
                    e.wait_ge(s(f"w_landed{h % 2}"), 16 * (landed + h // 2 + 1))
                    if n >= 2:
                        e.wait_ge(s("qT_evacuated"), m - 1)
                    for k in range(KD):
                        mm = e.matmul(bank[side][:, 0:ntok], w[:, k, side * P:(side + 1) * P], XT[:, k, 0:ntok],
                                      start=(k == 0), stop=(k == KD - 1))
                    mm.then_inc(s("tiles_projected"), 1)

                def key_scores(n):
                    side = n % 2
                    m = 2 * PH * g + n
                    e.wait_ge(s("qT_evacuated"), m + 1)
                    if n >= 2:
                        e.wait_ge(s("topk_done"), m - 1)
                    for sl, t in enumerate(tiles):
                        R = ROWS[t]
                        mm = e.matmul(bank[2 + side][:R, sl * P:(sl + 1) * P], qTm[:, side, sl * P:sl * P + R], keysT[:, side, :],
                                      start=True, stop=True)
                    mm.then_inc(s("key_scores"), 1)

                for n in range(2 * PH + 1):
                    if n < 2 * PH:
                        query(n)
                    if n:
                        key_scores(n - 1)

            e.wait_ge(s("consts_loaded"), 16 * 11)
            for g, tiles in enumerate(GROUPS):
                norm_transposes("x", tiles)
                e.wait_ge(s("nt_evacuated"), 4 * (NORMS["x", tiles[-1]] + 1))
                if g:
                    e.wait_ge(s("topk_done"), 2 * PH)
                    e.wait_ge(s("qT_evacuated"), 2 * PH)
                project(f"in{g}", tiles, IN_NC, IN_BLOCKS, "z_read", IN_READ[f"in{g}"])
                e.wait_ge(s("z_read"), IN_READ[f"in{g}"] + IN_BLOCKS * len(tiles))
                latent_attention(g)
                if g:
                    sample_attention()
                linear_attention(g)
                norm_transposes("mix", tiles)
                e.wait_ge(s("nt_evacuated"), 4 * (NORMS["mix", tiles[-1]] + 1))
                e.wait_ge(s("gla_o_sb"), tiles[-1] + 1)
                project(f"out{g}", tiles, NC, NBLK, "rows_added", ADDED[f"out{g}"])
                norm_transposes("ffn", tiles)
                queries(g)
            for pg, tiles in enumerate(PLE_GROUPS):
                if pg == 0:
                    e.wait_ge(s("topk_done"), 4 * PH)
                norm_transposes("ple", tiles)
                e.wait_ge(s("p_loaded"), 16 * (tiles[-1] + 1))
                for t in tiles:
                    R = ROWS[t]
                    if t:
                        e.wait_ge(s("pT_ple_sb"), t)
                    for k in range(2):
                        mm = e.transpose(bank[5][:, k * P:k * P + R], p_row[:R, t % 2, k * P:(k + 1) * P], ident[:R, :R])
                    mm.then_inc(s("pT_ple_psum"), 1)
                e.wait_ge(s("pT_ple_sb"), tiles[-1] + 1)
                e.wait_ge(s("nt_evacuated"), 4 * (NORMS["ple", tiles[-1]] + 1))
                project(f"gate{pg}", tiles, NC, NBLK, "rows_added", ADDED[f"gate{pg}"], embed=True)

        @block.scalar
        def _(e):
            own = [0]

            def mark(ins):
                own[0] += 1
                ins.then_inc(s("act_own"), 1)

            def link(ins):
                mark(ins)
                e.wait_ge(s("act_own"), own[0])

            def norm_squares(use, tiles, ready):
                for t in tiles:
                    R = ROWS[t]
                    n = NORMS[use, t]
                    sl = slot(t) if use != "ple" else t % 2
                    width = H_MLA * DV if use == "mix" else D
                    ready(t)
                    if n:
                        e.wait_ge(s("nt_transposed"), 4 * n)
                    if use == "ffn" and t != tiles[0]:
                        e.wait_ge(s("xn_stored"), 16 * t)
                    link(e.activation(Y[:R, 0:width], H[:R, sl, 0:width], ACT.Square, accum_out=st[:R, n:n + 1]))
                    e.activation(st[:R, ns + n:ns + n + 1], st[:R, n:n + 1], ACT.Sqrt, scale=1.0 / width, bias=eps[:R, :])\
                        .then_inc(s("rms_ready"), 1)
                    for q in range(4):
                        m = 4 * n + q
                        e.wait_ge(s("nt_transposed"), m + 1)
                        e.copy(XT[:, 4 * q:4 * q + 4, sl * P:sl * P + R], four(bank[6 + m % 2], R)).then_inc(s("nt_evacuated"), 1)

            def rms(out, ssq, width, R):
                return e.activation(out[:R], ssq[:R], ACT.Sqrt, scale=1.0 / width, bias=eps[:R, :])

            def pT_copy(m, t, h):
                u = m * HH + h
                e.wait_ge(s("pT_psum"), u + 1)
                if h >= 2:
                    e.wait_ge(s("pv_done"), u - 1)
                e.copy(pT[:, h % 2, 0:(t + 1) * P], bank[2 + h % 2][:, 0:(t + 1) * P]).then_inc(s("pT_sb"), 1)

            def mixer(g):
                tiles = GROUPS[g]
                nt = len(tiles)
                loaded = 0 if g == 0 else 3 * 2
                if g:
                    e.wait_ge(s("route_ready"), 2)
                norm_squares("x", tiles, lambda t: e.wait_ge(s("rows_loaded"), 16 * (loaded + nt)))
                e.wait_ge(s("normed"), NORMS["x", tiles[-1]] + 1)
                yield
                per = IN_BLOCKS // 8
                for seg in range(4 if g else 1):
                    lo, hi = (seg * per, seg * per + per) if g else (0, IN_BLOCKS // 2)
                    for i in pairs(e, lo, hi, g == 0):
                        for p in range(2):
                            e.wait_ge(s(f"z_stored{p}"), (i * (16 * nt)) + Z_BEFORE[g])
                            for sl, t in enumerate(tiles):
                                R = ROWS[t]
                                u = (i * 2 + p) * nt + sl
                                e.wait_ge(s("tiles_projected"), u + (PASSES[f"in{g}"][1] + 1))
                                zs = zst[:R, p * MT + sl, 0:IN_NC]
                                e.copy(zs, out_bank(p, sl)[:R, 0:IN_NC]).then_inc(s("z_read"), 1)
                                e.wait_ge(s("z_read"), u + (IN_READ[f"in{g}"] + 1))
                                e.dma_start(z_dram[rows(t), bass.ds((i * 2 + p) * IN_NC, IN_NC)], zs).then_inc(s(f"z_stored{p}"), 16)
                    yield
                for t in tiles:
                    R = ROWS[t]
                    e.wait_ge(s("mla_z_loaded"), 16 * (t + 1))
                    if t != tiles[0]:
                        e.wait_ge(s("rope_key_ready"), t)
                    mark(e.activation(sqs[:R, 0:QR], m_z[:R, 0:QR], ACT.Square, accum_out=SSQ[:R]))
                    mark(e.activation(QTn[:R, 0:2, :].rearrange("p a b -> p (a b)"), m_z[:R, QR:QR + KVR], ACT.Square, accum_out=SSC[:R]))
                    link(e.activation(QTr[:R, 0, 0:ROPE], m_z[:R, QR + KVR:MLA_COLS], ACT.Square, accum_out=SKR(t)[:R]))
                    rms(RQ, SSQ, QR, R)
                    rms(RC, SSC, KVR, R).then_inc(s("lat_rms"), 1)
                    e.wait_ge(s("lat_transposed"), t + 1)
                    e.copy(cqT[:, slot(t), :, 0:R], four(bank[0], R))
                    e.copy(cT[:, slot(t), :, 0:R], four(bank[1], R)[:, 0:2]).then_inc(s("latT_ready"), 1)
                yield
                for hh in range(2):
                    for t in tiles:
                        R = ROWS[t]
                        n = HALVES[hh, t]
                        e.wait_ge(s("q_ready"), n + 1)
                        if n:
                            e.wait_ge(s("ssq_done"), 2 * n)
                        for j in range(2):
                            ins = e.activation(sqs[:R, j * 2 * QK:(j + 1) * 2 * QK], bank[j][:R, 0:2 * QK], ACT.Square)
                        ins.then_inc(s("squares_ready"), 1)
                        e.wait_ge(s("ssq_done"), 2 * n + 1)
                        e.activation(RQH[:R], SQH[:R], ACT.Sqrt, scale=1.0 / QK, bias=eps[:R, :]).then_inc(s("q_rms"), 1)
                        e.wait_ge(s("k_ready"), n + 1)
                        e.activation(sqs[:R, 0:512], bank[2][:R, :], ACT.Square).then_inc(s("squares_ready"), 1)
                        e.wait_ge(s("ssq_done"), 2 * n + 2)
                        e.activation(RKH[:R], SKH[:R], ACT.Sqrt, scale=1.0 / QK, bias=eps[:R, :]).then_inc(s("k_rms"), 1)
                        if t == PT:
                            yield
                            continue
                        m = PHALVES[hh, t]
                        e.wait_ge(s("v_ready"), m + 1)
                        if m:
                            e.wait_ge(s("pv_done"), HH * m)
                        if g == 0 and hh and t == 0:
                            e.wait_ge(s("keys_parked"), 48)
                        e.copy(V[:, t, :], bank[3][:, :]).then_inc(s("v_sb"), 1)
                        e.wait_ge(s("qT_psum"), m + 1)
                        e.copy(QTn[:, :, :], four(bank[4]))
                        e.copy(QTr[:, :, :], four(bank[5])[:, 0:2]).then_inc(s("qT_sb"), 1)
                        nk = (t + 1) * P
                        for h in range(HH):
                            u = m * HH + h
                            e.wait_ge(s("neg_max"), u + 1)
                            if u >= 2:
                                e.wait_ge(s("pT_psum"), u - 1)
                            e.activation(pr[:, h % 2, 0:nk], bank[h % 2][:, 0:nk], ACT.Exp, scale=SCALE, bias=NMX[:, h:h + 1],
                                         accum_out=RSUM[:, h:h + 1]).then_inc(s("exp_done"), 1)
                            if h:
                                pT_copy(m, t, h - 1)
                        pT_copy(m, t, HH - 1)
                        yield
                if g:
                    for x in sample():
                        yield
                for t in tiles:
                    R = ROWS[t]
                    lv0 = 0 if t < PT else SAMPLE_LEVEL0
                    if t == tiles[0]:
                        e.wait_ge(s("gla_fills"), g + 1)
                    e.wait_ge(s("lrT_psum"), t + 1)
                    e.copy(alT[0:GATE_R, 0:R], bank[0][0:GATE_R, 0:R]).then_inc(s("lrT_sb"), 1)
                    e.wait_ge(s("gqkT_psum"), t + 1)
                    e.activation(heads(gqT, R), heads(bank[1], R), ACT.Copy, scale=float(GK) ** -0.5)
                    e.copy(heads(gkT, R), heads(bank[2], R)).then_inc(s("gqkT_sb"), 1)
                    e.wait_ge(s("gate_pre"), t + 1)
                    link(e.activation(gt1[:R, :], bank[3][:R, :], ACT.Abs))
                    link(e.activation(gt1[:R, :], gt1[:R, :], ACT.Exp, scale=-1.0))
                    e.activation(gt1[:R, :], gt1[:R, :], ACT.Ln, bias=1.0).then_inc(s("gate_ln"), 1)
                    for n in range(lv0, NLEV - 1):
                        v = level_count(t, n)
                        e.wait_ge(s("level_diff"), v + 1)
                        e.activation(heads(dlev[:, n % 2, :], R), heads(dlev[:, n % 2, :], R), ACT.Exp).then_inc(s("level_exp"), 1)
                    e.wait_ge(s("cum_sb"), t + 1)
                    e.activation(heads(eb, R), heads(gbT, R), ACT.Exp).then_inc(s("eb_ready"), 1)
                    e.wait_ge(s("kdiff"), t + 1)
                    e.activation(heads(kd, R), heads(kd, R), ACT.Exp).then_inc(s("kexp"), 1)
                    yield
                    e.wait_ge(s("kdr_psum"), t + 1)
                    e.copy(kdr[:R, :, :], bank[5][:R, :].rearrange("p (h n) -> p h n", h=H_GLA)).then_inc(s("kdr_sb"), 1)
                    if t != tiles[0]:
                        e.wait_ge(s("gla_o_ready"), t)
                    link(e.activation(gsil[:R, :], gz[:R, 2 * H_GLA * GK + 1024:2 * H_GLA * GK + 2048], ACT.Silu))
                    e.wait_ge(s("gla_o_sb"), t + 1)
                    for h in range(H_GLA):
                        mark(e.activation(gsq[:R, h * GV:(h + 1) * GV], go[:R, h * GV:(h + 1) * GV], ACT.Square,
                                          accum_out=GSS[:R, h:h + 1]))
                    e.wait_ge(s("act_own"), own[0])
                    e.activation(GRS[:R], GSS[:R], ACT.Sqrt, scale=1.0 / GV, bias=eps[:R, :]).then_inc(s("gla_rms"), 1)
                    e.sem_inc(s("gla_read"), 1)
                    yield
                norm_squares("mix", tiles, lambda t: e.wait_ge(s("rows_loaded"), 16 * (loaded + 2 * nt)))
                yield
                if g:
                    yield
                norm_squares("ffn", tiles, lambda t: e.wait_ge(s("rows_added"), ADDED[f"out{g}"] + (NBLK - 1) * nt + slot(t) + 1))
                e.wait_ge(s("h_stored"), 16 * (tiles[-1] + 1))
                e.dma_start(keysR[:, 0, :], a["peer_keys1"][0]).then_inc(s("keys_loaded"), 16)
                e.dma_start(keysR[:, 1, :], a["peer_keys2"][0]).then_inc(s("keys_loaded"), 16)
                e.wait_ge(s("keysT_psum"), g + 1)
                e.copy(keysT[:, :, :], four(bank[0])[:, 0:2]).then_inc(s("keysT_sb"), 1)
                yield
                ntok = sum(ROWS[t] for t in tiles)
                for n in range(2 * PH):
                    side = n % 2
                    m = 2 * PH * g + n
                    e.wait_ge(s("tiles_projected"), PASSES[f"query{g}"][1] + n + 1)
                    if n >= 2:
                        e.wait_ge(s("key_scores"), m - 1)
                    e.copy(qTm[:, side, 0:ntok], bank[side][:, 0:ntok]).then_inc(s("qT_evacuated"), 1)
                    if n % 4 == 3:
                        yield

            def sample():
                for j in range(4):
                    e.wait_ge(s("sprep_psum"), j + 1)
                    e.copy(w_ukT[:, 2 * j:2 * j + 2, :].rearrange("p h n -> p (h n)"), bank[0][:, :]).then_inc(s("sprep_act"), 1)
                e.wait_ge(s("sprep_psum"), 5)
                e.copy(krT[0:ROPE, :], bank[1][0:ROPE, 0:NS]).then_inc(s("sprep_act"), 1)
                e.copy(ikx[:NS, :].rearrange("p (h t) -> p h t", t=DEC_T), IKH(PT)[:NS, :].unsqueeze(2).to_broadcast([NS, H_MLA, DEC_T]))\
                    .then_inc(s("sprep_act"), 1)
                e.wait_ge(s("sprep_psum"), 6)
                for k in range(2):
                    ins = e.copy(by_batch(q_lat[k]), bank[4 + k][:, :].rearrange("p (h b t) -> p h b t", h=H_MLA, b=DEC_B))
                ins.then_inc(s("sprep_act"), 1)
                yield
                for b in range(DEC_B):
                    e.wait_ge(s(f"pages_landed{b % 2}"), 16 * 3 * N_PAGES * (b // 2 + 1))
                    if b:
                        e.wait_ge(s("ir_psum"), 4 * b)
                    e.copy(ire.rearrange("p g (h t) -> p (g h) t", t=DEC_T),
                           pages_sb[b % 2][2].rearrange("p g h -> p (g h)").unsqueeze(2).to_broadcast([P, N_PAGES * H_MLA, DEC_T]))\
                        .then_inc(s("ire_ready"), 1)
                    for g in range(4):
                        u = 4 * b + g
                        e.wait_ge(s("latT_psum"), u + 1)
                        if u:
                            e.wait_ge(s("sscore_psum"), u)
                        e.copy(latT[:, 0, :], bank[0][:, :])
                        e.copy(latT[:, 1, :], bank[1][:, :])
                        e.copy(latT[0:ROPE, 2, :], bank[2][0:ROPE, :]).then_inc(s("latT_sb"), 1)
                        e.wait_ge(s("ir_psum"), u + 1)
                        if u:
                            e.wait_ge(s("scaled"), u)
                        e.copy(irs[:NS, :], bank[3][:NS, :]).then_inc(s("ir_sb"), 1)
                    e.wait_ge(s("sneg_max"), b + 1)
                    e.activation(sc[:NS, :], sc[:NS, :], ACT.Exp, scale=SCALE, bias=NMX[:NS, 0:1], accum_out=RSUM[:NS, 0:1])\
                        .then_inc(s("sexp_done"), 1)
                    for q in range(3):
                        v = 3 * b + q
                        n = 8 if q < 2 else 1
                        R = P if q < 2 else NS
                        e.wait_ge(s("spT_psum"), v + 1)
                        if b and q == 0:
                            e.wait_ge(s("olat_psum"), b)
                        e.copy(pTs[:R, 8 * q:8 * q + n, :].rearrange("p a b -> p (a b)"), bank[6][:R, 0:n * NS]).then_inc(s("spT_sb"), 1)
                    e.wait_ge(s("olatT_psum"), b + 1)
                    for k in range(2):
                        ins = e.copy(oT[k][:, :, b * DEC_T:(b + 1) * DEC_T],
                                     bank[7][:, 256 + k * NS:256 + (k + 1) * NS].rearrange("p (h t) -> p h t", h=H_MLA))
                    ins.then_inc(s("olatT_sb"), 1)
                    yield

            def route(t):
                R = ROWS[t]
                e.wait_ge(s("gate_diff"), t + 1)
                e.activation(gtop[:R, :], gtop[:R, :], ACT.Exp).then_inc(s("gate_exp"), 1)

            def embedding(pg):
                tiles = PLE_GROUPS[pg]
                nt = len(tiles)
                if pg < 2:
                    norm_squares("ple", tiles, lambda t: e.wait_ge(s("rows_loaded"), 16 * (3 * T + tiles[-1] + 1)))
                else:
                    norm_squares("ple", tiles, lambda t: e.wait_ge(s("peer_done"), T))
                for t in tiles:
                    e.wait_ge(s("pT_ple_psum"), t + 1)
                    e.copy(pT_ple[:, :, (t % 2) * P:(t % 2) * P + ROWS[t]], four(bank[5], ROWS[t])[:, 0:2]).then_inc(s("pT_ple_sb"), 1)
                yield
                for i in pairs(e, 0, NBLK // 2, pg == 2):
                    for p in range(2):
                        for sl, t in enumerate(tiles):
                            R = ROWS[t]
                            u = (i * 2 + p) * nt + sl
                            x = (p * nt + sl) % 2
                            e.wait_ge(s("tiles_projected"), u + (PASSES[f"gate{pg}"][1] + 1))
                            e.wait_ge(s("rows_added"), u + (ADDED[f"gate{pg}"] - 1))
                            e.activation(sg[:R, x, :], out_bank(p, sl)[:R, 0:NC], ACT.Sigmoid).then_inc(s("sigmoid_ready"), 1)
                    if pg < 2:
                        yield

            def woven():
                route(1)
                yield
                for x in mixer(1):
                    yield
                route(2)
                yield
                route(3)
                yield
                route(4)
                yield
                for pg in range(2):
                    for x in embedding(pg):
                        yield

            e.wait_ge(s("fills_ready"), 2)
            e.sem_inc(s("z_read"), 4)
            e.sem_inc(s("z_stored0"), Z_BEFORE[0])
            e.sem_inc(s("z_stored1"), Z_BEFORE[0])
            for x in mixer(0):
                pass
            route(0)

            def load_x(t):
                e.wait_ge(s("xn_stored"), 16 * (t + 1))
                if t < PT:
                    e.dma_start(xrow[:, t % 2, :], xn_dram[rows(t), :]).then_inc(s(f"xrow_loaded{t % 2}"), 16)
                else:
                    for r in range(2):
                        e.dma_start(xrow[r * NS:(r + 1) * NS, t % 2, :], xn_dram[rows(t), :]).then_inc(s(f"xrow_loaded{t % 2}"), 16)

            load_x(0)
            load_x(1)
            weave = woven()
            for t in range(T):
                first, nu = t * PH, PH if t < PT else PH // 2
                if t == 2:
                    pass
                for j in range(nu):
                    u = first + j
                    for _ in range(SEGMENTS[u]):
                        next(weave)
                    if t == 2 and j == 0:
                        e.wait_ge(s("peer_done"), 1)
                    if j == 0 and t >= 1:
                        e.wait_ge(s("peer_done"), t)
                        e.dma_start(h2_dram[rows(t - 1), :], xrow[:, (t - 1) % 2, :]).then_inc(s("h2_stored"), 16)
                    e.wait_ge(s("dots_done"), (u + 1) * TOPK)
                    e.activation(gel[:, :], dots[:, :], ACT.Gelu).then_inc(s("gelu_ready"), 1)
                    if j == 1 and t in (2, 3):
                        e.wait_ge(s("h2_stored"), 16 * t)
                        load_x(t + 1)
                    if j == nu - 1:
                        e.wait_ge(s("h_stored"), 16 * (t + 1))
                        R = ROWS[t]
                        e.dma_start(xrow[:R, t % 2, :], h_dram[rows(t), :]).then_inc(s("h_loaded"), 16)
                if t == 1:
                    e.wait_ge(s("h2_stored"), 16)
                    load_x(2)
            e.wait_ge(s("sample_halves"), 1)
            e.dma_start(acc[0:NS, 1, :], acc[NS:P, 0, :]).then_inc(s("sample_back"), 16)
            for x in weave:
                pass
            for x in embedding(2):
                pass

        @block.vector
        def _(e):
            own = [0]

            def mark(ins):
                own[0] += 1
                ins.then_inc(s("dve_own"), 1)

            def link(ins):
                mark(ins)
                e.wait_ge(s("dve_own"), own[0])

            def norm_rows(use, tiles):
                for t in tiles:
                    R = ROWS[t]
                    n = NORMS[use, t]
                    sl = slot(t) if use != "ple" else t % 2
                    width = H_MLA * DV if use == "mix" else D
                    inv = st[:R, 2 * ns + n:2 * ns + n + 1]
                    e.wait_ge(s("rms_ready"), n + 1)
                    link(e.reciprocal(inv, st[:R, ns + n:ns + n + 1]))
                    if t == tiles[0]:
                        e.wait_ge(s("gain_loaded"), 16 * (GAINS.index((use, tiles[0])) + 1))
                    e.scalar_tensor_tensor(out=Y[:R, 0:width], in0=H[:R, sl, 0:width], scalar=inv, in1=G[:R, 0:width],
                                           op0=ALU.mult, op1=ALU.mult).then_inc(s("normed"), 1)
                    yield STEP

            def rotate(t, out, x, n):
                R = ROWS[t]
                cs, sn = cosT[:R, t, :], sinT[:R, t, :]
                hf = ROPE // 2
                if n > 1:
                    cb = cs.unsqueeze(1).to_broadcast([R, n, ROPE])
                    s0 = sn[:, 0:hf].unsqueeze(1).to_broadcast([R, n, hf])
                    s1 = sn[:, hf:ROPE].unsqueeze(1).to_broadcast([R, n, hf])
                    tmp = rtmp[:R]
                    xa, xb, ta, tb = x[:, :, hf:ROPE], x[:, :, 0:hf], tmp[:, :, 0:hf], tmp[:, :, hf:ROPE]
                else:
                    cb, s0, s1 = cs, sn[:, 0:hf], sn[:, hf:ROPE]
                    tmp = rtmp[:R, 0, :]
                    xa, xb, ta, tb = x[:, hf:ROPE], x[:, 0:hf], tmp[:, 0:hf], tmp[:, hf:ROPE]
                e.tensor_tensor(ta, xa, s0, ALU.mult)
                e.tensor_tensor(tb, xb, s1, ALU.mult)
                link(e.tensor_tensor(out, x, cb, ALU.mult))
                return e.tensor_tensor(out, out, tmp, ALU.add)

            def mixer(g):
                tiles = GROUPS[g]
                nt = len(tiles)
                yield from norm_rows("x", tiles)
                yield SEGMENT
                for seg in range(4 if g else 1):
                    yield SEGMENT
                e.wait_ge(s("mla_gains_loaded"), 64 * (g + 1))
                for t in tiles:
                    R = ROWS[t]
                    e.wait_ge(s("lat_rms"), t + 1)
                    mark(e.reciprocal(IQ[:R], RQ[:R]))
                    link(e.reciprocal(IC[:R], RC[:R]))
                    e.scalar_tensor_tensor(out=cqn[:R, :], in0=m_z[:R, 0:QR], scalar=IQ[:R], in1=g_q[:R, :], op0=ALU.mult, op1=ALU.mult)
                    if t:
                        e.wait_ge(s("lat_stored"), 16 * t)
                    e.scalar_tensor_tensor(out=c_rows[:R, :], in0=m_z[:R, QR:QR + KVR], scalar=IC[:R], in1=g_kv[:R, :],
                                           op0=ALU.mult, op1=ALU.mult).then_inc(s("mla_latents_normed"), 1)
                    yield STEP
                    link(e.tensor_tensor(kr_g[:R, :], m_z[:R, QR + KVR:MLA_COLS], g_k[:R, NOPE:QK], ALU.mult))
                    rotate(t, kr_o[:R, slot(t), :], kr_g[:R, :], 1).then_inc(s("rope_key_ready"), 1)
                    e.wait_ge(s("rope_key_ready"), t + 1)
                    e.wait_ge(s("lat_transposed"), t + 1)
                    yield STEP
                yield SEGMENT
                for hh in range(2):
                    for t in tiles:
                        R = ROWS[t]
                        n = HALVES[hh, t]
                        e.wait_ge(s("squares_ready"), 2 * n + 1)
                        e.tensor_reduce(SQH[:R], sqs[:R, :].rearrange("p (h n) -> p h n", h=HH), AX, ALU.add).then_inc(s("ssq_done"), 1)
                        yield STEP
                        e.wait_ge(s("q_rms"), n + 1)
                        link(e.reciprocal(IQH[:R], RQH[:R]))
                        for j in range(2):
                            ins = e.tensor_tensor(qrow[:R, 2 * j:2 * j + 2, :], bank[j][:R, 0:2 * QK].rearrange("p (h n) -> p h n", h=2),
                                                  IQH[:R, 2 * j:2 * j + 2].unsqueeze(2).to_broadcast([R, 2, QK]), ALU.mult)
                        link(ins)
                        yield STEP
                        link(e.tensor_tensor(qrow[:R], qrow[:R], g_qk[:R, :].unsqueeze(1).to_broadcast([R, HH, QK]), ALU.mult))
                        yield STEP
                        link(rotate(t, qro[:R], qrow[:R, :, NOPE:QK], HH))
                        if t == PT:
                            link(e.tensor_tensor(qrow[:R, :, 0:NOPE], qrow[:R, :, 0:NOPE],
                                                 g_k[:R, 0:NOPE].unsqueeze(1).to_broadcast([R, HH, NOPE]), ALU.mult))
                        e.sem_inc(s("q_rows_ready"), 1)
                        yield STEP
                        e.wait_ge(s("squares_ready"), 2 * n + 2)
                        link(e.tensor_reduce(SKH[:R], sqs[:R, 0:512].rearrange("p (h n) -> p h n", h=HH), AX, ALU.add))
                        e.tensor_scalar(SKH[:R], SKH[:R], SKR(t)[:R], None, ALU.add).then_inc(s("ssq_done"), 1)
                        yield STEP
                        e.wait_ge(s("k_rms"), n + 1)
                        ik = IKH(t)[:R, hh * HH:(hh + 1) * HH]
                        e.reciprocal(ik, RKH[:R]).then_inc(s("ikh_ready"), 1)
                        e.wait_ge(s("ikh_ready"), n + 1)
                        if t == PT:
                            e.sem_inc(s("k_rows_ready"), 1)
                            e.wait_ge(s("sample_qT_psum"), hh + 1)
                            e.tensor_copy(qgT[:, hh * HH:(hh + 1) * HH, :], bank[4][:, 0:HH * NS].rearrange("p (h n) -> p h n", h=HH))
                            e.tensor_copy(by_batch(qrT[0:ROPE], hh * HH, HH),
                                          bank[5][0:ROPE, 0:HH * NS].rearrange("p (h b t) -> p h b t", h=HH, b=DEC_B))\
                                .then_inc(s("sample_qT_sb"), 1)
                            yield SEGMENT
                            continue
                        link(e.tensor_tensor(krow[:, :, :], bank[2][:, :].rearrange("p (h n) -> p h n", h=HH),
                                             ik.unsqueeze(2).to_broadcast([P, HH, NOPE]), ALU.mult))
                        yield STEP
                        link(e.tensor_tensor(krow[:, :, :], krow[:, :, :], g_k[:, 0:NOPE].unsqueeze(1).to_broadcast([P, HH, NOPE]), ALU.mult))
                        e.tensor_tensor(kro[:, :, :], kr_o[:, slot(t), :].unsqueeze(1).to_broadcast([P, HH, ROPE]),
                                        ik.unsqueeze(2).to_broadcast([P, HH, ROPE]), ALU.mult).then_inc(s("k_rows_ready"), 1)
                        yield STEP
                        m = PHALVES[hh, t]
                        e.wait_ge(s("kT_psum"), m + 1)
                        if m:
                            e.wait_ge(s("pv_done"), HH * m)
                        if g == 0 and hh and t == 0:
                            e.wait_ge(s("keys_parked"), 48)
                        e.tensor_copy(KTn[:, :, t * P:(t + 1) * P], four(bank[6]))
                        e.tensor_copy(KTr[:, :, t * P:(t + 1) * P], four(bank[7])[:, 0:2]).then_inc(s("kT_sb"), 1)
                        yield STEP
                        for h in range(HH):
                            u = m * HH + h
                            e.wait_ge(s("scores_ready"), u + 1)
                            link(e.tensor_reduce(MXV[:, h:h + 1], bank[h % 2][:, 0:(t + 1) * P], AX, ALU.max))
                            e.tensor_scalar(NMX[:, h:h + 1], MXV[:, h:h + 1], -SCALE, None, ALU.mult).then_inc(s("neg_max"), 1)
                            yield STEP
                        e.wait_ge(s("exp_done"), (m + 1) * HH)
                        link(e.reciprocal(RINV[:, :], RSUM[:, :]))
                        e.wait_ge(s("pv_done"), (m + 1) * HH)
                        if m:
                            e.wait_ge(s("o_stored"), 16 * m)
                        e.tensor_tensor(orow.rearrange("p (h n) -> p h n", h=HH), bank[4][:, :].rearrange("p (h n) -> p h n", h=HH),
                                        RINV[:, :].unsqueeze(2).to_broadcast([P, HH, DV]), ALU.mult).then_inc(s("mla_o_rows"), 1)
                        yield SEGMENT
                if g:
                    yield from sample()
                if g:
                    e.wait_ge(s("o_stored"), 16 * 9)
                else:
                    e.wait_ge(s("o_stored"), 16 * 4)
                e.wait_ge(s("gla_w_loaded"), 48 if g == 0 else 48 + 64)
                mark(e.memset(alT[0:GATE_R + 1, :], 1.0))
                link(e.memset(qz, 0.0))
                e.sem_inc(s("gla_fills"), 1)
                for t in tiles:
                    yield from gla(t)
                yield from norm_rows("mix", tiles)
                yield SEGMENT
                e.wait_ge(s("rows_loaded"), 16 * ((0 if g == 0 else 6) + 3 * nt))
                for i in pairs(e, 0, NBLK // 2, g == 0):
                    for p in range(2):
                        for sl, t in enumerate(tiles):
                            R = ROWS[t]
                            u = (i * 2 + p) * nt + sl
                            hs = H[:R, sl, bass.ds((i * 2 + p) * NC, NC)]
                            e.wait_ge(s("tiles_projected"), u + (PASSES[f"out{g}"][1] + 1))
                            e.tensor_tensor(hs, hs, out_bank(p, sl)[:R, 0:NC], ALU.add).then_inc(s("rows_added"), 1)
                            if g:
                                yield STEP
                    if g and i == NBLK // 4 - 1:
                        yield SEGMENT
                yield from norm_rows("ffn", tiles)
                e.wait_ge(s("xn_stored"), 16 * (tiles[-1] + 1))
                e.wait_ge(s("keys_loaded"), 32 * (g + 1))
                yield SEGMENT
                for n in range(2 * PH):
                    side = n % 2
                    m = 2 * PH * g + n
                    e.wait_ge(s("key_scores"), m + 1)

                    def sco(sl):
                        return bank[2 + side][:ROWS[tiles[sl]], sl * P:(sl + 1) * P]

                    def top(sl):
                        return topv[:ROWS[tiles[sl]], sl, n, :]

                    for sl in range(nt):
                        ins = e.max(top(sl)[:, 0:8], sco(sl))
                    link(ins)
                    yield STEP
                    for sl in range(nt):
                        R = ROWS[tiles[sl]]
                        e.max_index(topu[:R, sl, 0:8], top(sl)[:, 0:8], sco(sl))
                        ins = e.match_replace(out=swork[:R, sl, :], in_to_replace=top(sl)[:, 0:8], in_values=sco(sl), imm_value=LOWEST)
                    link(ins)
                    yield STEP
                    for sl in range(nt):
                        ins = e.max(top(sl)[:, 8:16], swork[:ROWS[tiles[sl]], sl, :])
                    link(ins)
                    for sl in range(nt):
                        R = ROWS[tiles[sl]]
                        ins = e.max_index(topu[:R, sl, 8:16], top(sl)[:, 8:16], swork[:R, sl, :])
                    link(ins)
                    ins = e.tensor_copy(topi[:, 0:2, n, :], topu[:, 0:2, :])
                    if g:
                        ins = e.tensor_copy(topi[:NS, 2, n, :], topu[:NS, 2, :])
                    ins.then_inc(s("topk_done"), 1)
                    e.wait_ge(s("topk_done"), m + 1)
                    yield SEGMENT if n % 4 == 3 else STEP

            def sample():
                yield SEGMENT
                for b in range(DEC_B):
                    for g in range(4):
                        u = 4 * b + g
                        e.wait_ge(s("sscore_psum"), u + 1)
                        e.wait_ge(s("ir_sb"), u + 1)
                        if b and g == 0:
                            e.wait_ge(s("spT_psum"), 3 * b)
                        e.tensor_tensor(sc[:NS, g * 512:(g + 1) * 512], bank[4][:NS, :], irs[:NS, :], ALU.mult).then_inc(s("scaled"), 1)
                        yield STEP
                    e.wait_ge(s("snew_psum"), b + 1)
                    link(e.tensor_copy(sc[:NS, PAST:PAST + NS], bank[5][:NS, NS:2 * NS]))
                    link(e.tensor_tensor(sc[:NS, PAST:PAST + NS], sc[:NS, PAST:PAST + NS], bank[5][:NS, 0:NS], ALU.mult))
                    e.tensor_tensor(sc[:NS, PAST:PAST + NS], sc[:NS, PAST:PAST + NS], smask[:NS, b, :], ALU.add).then_inc(s("snew_done"), 1)
                    e.wait_ge(s("snew_done"), b + 1)
                    e.wait_ge(s("scaled"), 4 * b + 4)
                    link(e.tensor_reduce(MXV[:NS, 0:1], sc[:NS, :], AX, ALU.max))
                    e.tensor_scalar(NMX[:NS, 0:1], MXV[:NS, 0:1], -SCALE, None, ALU.mult).then_inc(s("sneg_max"), 1)
                    yield STEP
                    e.wait_ge(s("sexp_done"), b + 1)
                    link(e.reciprocal(RINV[:NS, 0:1], RSUM[:NS, 0:1]))
                    e.wait_ge(s("olat_psum"), b + 1)
                    e.tensor_scalar(olr[:NS, :], bank[7][:NS, 0:KVR], RINV[:NS, 0:1], None, ALU.mult).then_inc(s("olat_sb"), 1)
                    yield SEGMENT if b < DEC_B - 1 else STEP
                e.wait_ge(s("sprep_psum"), 7)
                for n in range(2):
                    ins = e.tensor_copy(so_rows[:NS, n * 512:(n + 1) * 512], bank[n][:NS, :])
                ins.then_inc(s("sample_o_rows"), 1)
                yield SEGMENT

            def gla(t):
                R = ROWS[t]
                lv0 = 0 if t < PT else SAMPLE_LEVEL0
                e.wait_ge(s("gate_ln"), t + 1)
                link(e.tensor_scalar(gt2[:R, :], bank[3][:R, :], 0.0, 1.0 / TAU, ALU.min, ALU.mult))
                e.scalar_tensor_tensor(out=gx[:R, :], in0=gt1[:R, :], scalar=-1.0 / TAU, in1=gt2[:R, :],
                                       op0=ALU.mult, op1=ALU.add).then_inc(s("gate_log"), 1)
                yield STEP
                e.wait_ge(s("cum_psum"), t + 1)
                e.tensor_copy(heads(gbT, R), heads(bank[4], R)).then_inc(s("cum_sb"), 1)
                e.wait_ge(s("cum_sb"), t + 1)
                e.wait_ge(s("gqkT_sb"), t + 1)
                if t not in (0, 2):
                    e.wait_ge(s("gla_out_psum"), t * H_GLA)
                yield STEP

                def halves(ap, n):
                    hf = LEVELS[n]
                    if R == P:
                        v = ap[:, 0:H_GLA * P].rearrange("p (g a b) -> p g a b", a=2, b=hf)
                        return v[:, :, 0, :], v[:, :, 1, :]
                    v = heads(ap, R).rearrange("p h (g a b) -> p h g a b", a=2, b=hf)
                    return v[:, :, :, 0, :], v[:, :, :, 1, :]

                def multiply(n):
                    v = level_count(t, n)
                    e.wait_ge(s("level_exp"), v + 1)
                    d0, d1 = halves(dlev[:, n % 2, :], n)
                    m0, m1 = halves(Mlev[:, n, :], n)
                    k0, _ = halves(gkT, n)
                    _, q1 = halves(gqT, n)
                    e.tensor_tensor(m0, d0, k0, ALU.mult)
                    e.tensor_tensor(m1, d1, q1, ALU.mult).then_inc(s("level_done"), 1)

                for n in range(lv0, NLEV - 1):
                    hf = LEVELS[n]
                    v = level_count(t, n)
                    if v >= 2:
                        e.wait_ge(s("level_done"), v - 1)
                    b0, b1 = halves(gbT, n)
                    d0, d1 = halves(dlev[:, n % 2, :], n)
                    rb = b0[..., hf - 1:hf].to_broadcast(list(b0.shape))
                    e.tensor_tensor(d0, rb, b0, ALU.subtract)
                    e.tensor_tensor(d1, b1, rb, ALU.subtract).then_inc(s("level_diff"), 1)
                    if n > lv0:
                        multiply(n - 1)
                    yield STEP
                multiply(NLEV - 2)
                e.wait_ge(s("level_done"), level_count(t, NLEV - 2) + 1)
                e.sem_inc(s("levels_ready"), 1)
                seg = P if t < PT else DEC_T
                gseg = heads(gbT, R).rearrange("p h (g n) -> p h g n", n=seg)
                kseg = heads(kd, R).rearrange("p h (g n) -> p h g n", n=seg)
                last = gseg[:, :, :, seg - 1:seg]
                e.tensor_tensor(kseg, last.to_broadcast(list(gseg.shape)), gseg, ALU.subtract).then_inc(s("kdiff"), 1)
                e.wait_ge(s("eb_ready"), t + 1)
                e.tensor_tensor(heads(qe, R), heads(gqT, R), heads(eb, R), ALU.mult)
                ebs = heads(eb, R).rearrange("p h (g n) -> p h g n", n=seg)[:, :, :, seg - 1]
                nseg = R // seg
                link(e.tensor_copy(eL[:, 0:H_GLA * nseg].rearrange("p (h g) -> p h g", h=H_GLA), ebs))
                yield STEP
                e.wait_ge(s("kexp"), t + 1)
                e.tensor_tensor(heads(kd, R), heads(kd, R), heads(gkT, R), ALU.mult).then_inc(s("kdec_ready"), 1)
                yield SEGMENT
                nl = NLEV - lv0
                for h in range(H_GLA):
                    u = t * H_GLA + h
                    e.wait_ge(s("level_products"), u + 1)
                    for half in range((nl + 3) // 4):
                        n4 = min(4, nl - 4 * half)
                        ins = e.tensor_tensor(am[:R, 4 * half:4 * half + n4, 0:R],
                                              bank[2 * (h % 2) + half][:R, :].rearrange("p (l n) -> p l n", n=P)[:, 0:n4, 0:R],
                                              lev[:R, lv0 + 4 * half:lv0 + 4 * half + n4, 0:R], ALU.mult)
                    ins.then_inc(s("levels_masked"), 1)
                    e.wait_ge(s("levels_masked"), u + 1)
                    link(e.tensor_reduce(AT[:R, h, 0:R], am[:R, 0:nl, 0:R].rearrange("p l n -> p n l"), AX, ALU.add))
                    e.sem_inc(s("AT_ready"), 1)
                    yield STEP
                for h in range(H_GLA):
                    u = t * H_GLA + h
                    if t < PT:
                        e.wait_ge(s("gla_out_psum"), u + 1)
                        upd = bank[(h % 2) * 4][:, 0:GV]
                        if t:
                            e.scalar_tensor_tensor(out=S0[:, h, :], in0=S0[:, h, :], scalar=eL[:, h:h + 1], in1=upd,
                                                   op0=ALU.mult, op1=ALU.add).then_inc(s("gla_state"), 1)
                        else:
                            e.tensor_copy(S0[:, h, :], upd).then_inc(s("gla_state"), 1)
                    else:
                        if h:
                            e.wait_ge(s("sample_state_psum"), h)
                            sample_state(h - 1)
                            yield STEP
                        for b in range(DEC_B):
                            ins = e.tensor_copy(qz[:, b, b * DEC_T:(b + 1) * DEC_T], qe[:, h * P + b * DEC_T:h * P + (b + 1) * DEC_T])
                        e.wait_ge(s("kdr_sb"), T)
                        e.tensor_tensor(kz[:R, :, :], kdr[:R, h, :].unsqueeze(1).to_broadcast([R, DEC_B, GK]),
                                        bmask[:R, :].unsqueeze(2).to_broadcast([R, DEC_B, GK]), ALU.mult).then_inc(s("qz_ready"), 1)
                    yield STEP
                if t == PT:
                    e.wait_ge(s("sample_state_psum"), H_GLA)
                    sample_state(H_GLA - 1)
                e.wait_ge(s("gla_out_psum"), (t + 1) * H_GLA)
                if t:
                    e.wait_ge(s("go_stored"), 16 * t)
                e.tensor_copy(go[:R, 0:512], bank[6][:R, :])
                e.tensor_copy(go[:R, 512:1024], bank[7][:R, :]).then_inc(s("gla_o_sb"), 1)
                yield STEP
                e.wait_ge(s("gla_rms"), t + 1)
                link(e.reciprocal(GIS[:R], GRS[:R]))
                gv = go[:R, :].rearrange("p (h n) -> p h n", h=H_GLA)
                link(e.tensor_tensor(gv, gv, GIS[:R].unsqueeze(2).to_broadcast([R, H_GLA, GV]), ALU.mult))
                link(e.tensor_tensor(gv, gv, g_go[:R, :].unsqueeze(1).to_broadcast([R, H_GLA, GV]), ALU.mult))
                e.tensor_tensor(go[:R, :], go[:R, :], gsil[:R, :], ALU.mult).then_inc(s("gla_o_ready"), 1)
                yield SEGMENT

            def sample_state(h):
                for b in range(DEC_B):
                    upd = bank[b // 2][:, (b % 2) * GV:(b % 2 + 1) * GV]
                    st_ = Ss[h % 2][:, b, :]
                    ins = e.scalar_tensor_tensor(out=st_, in0=st_, scalar=eL[:, h * DEC_B + b:h * DEC_B + b + 1], in1=upd,
                                                 op0=ALU.mult, op1=ALU.add)
                ins.then_inc(s("sample_state_head"), 1)

            def route(t):
                R = ROWS[t]
                sl = slot(t)
                tv = topv[:R, sl, :, :].rearrange("p (h w) k -> p h w k", w=2)
                ti = topi[:R, sl, :, :].rearrange("p (h w) k -> p h w k", w=2)
                cv = cand[:R, :].rearrange("p (h i j) -> p h i j", h=PH, i=TOPK)
                link(e.tensor_tensor(cv, tv[:, :, 0, :].unsqueeze(3).to_broadcast([R, PH, TOPK, TOPK]),
                                     tv[:, :, 1, :].unsqueeze(2).to_broadcast([R, PH, TOPK, TOPK]), ALU.add))
                yield STEP
                gv = gtop
                for h in range(PH):
                    ins = e.max(gv[:R, h * 16:h * 16 + 8], cand[:R, h * 256:(h + 1) * 256])
                link(ins)
                yield STEP
                for h in range(PH):
                    e.max_index(sela[:R, h * 16:h * 16 + 8], gv[:R, h * 16:h * 16 + 8], cand[:R, h * 256:(h + 1) * 256])
                    ins = e.match_replace(out=candw[:R, h * 256:(h + 1) * 256], in_to_replace=gv[:R, h * 16:h * 16 + 8],
                                          in_values=cand[:R, h * 256:(h + 1) * 256], imm_value=LOWEST)
                    if h % 4 == 3:
                        link(ins)
                        yield STEP
                for h in range(PH):
                    ins = e.max(gv[:R, h * 16 + 8:h * 16 + 16], candw[:R, h * 256:(h + 1) * 256])
                link(ins)
                yield STEP
                for h in range(PH):
                    ins = e.max_index(sela[:R, h * 16 + 8:h * 16 + 16], gv[:R, h * 16 + 8:h * 16 + 16], candw[:R, h * 256:(h + 1) * 256])
                link(ins)
                yield STEP
                link(e.tensor_copy(e1[:R, 0:8], gv[:R, :].rearrange("p (h k) -> p h k", h=PH)[:, :, 0]))
                g3 = gv[:R, :].rearrange("p (h k) -> p h k", h=PH)
                e.tensor_tensor(g3, g3, e1[:R, 0:8].unsqueeze(2).to_broadcast([R, PH, TOPK]), ALU.subtract).then_inc(s("gate_diff"), 1)
                mark(e.tensor_single_scalar(selh[:R, :], sela[:R, :], 4, ALU.logical_shift_right))
                link(e.tensor_single_scalar(sell[:R, :], sela[:R, :], 15, ALU.bitwise_and))
                mark(e.tensor_copy(selhf[:R, :], selh[:R, :]))
                link(e.tensor_copy(sellf[:R, :], sell[:R, :]))
                yield STEP
                for sel, w, out in ((selhf, 0, e1), (sellf, 1, e2)):
                    oh = oneh[:R, :].rearrange("p (h i j) -> p h i j", h=PH, i=TOPK)
                    o3 = oneh[:R, :].rearrange("p (n j) -> p n j", j=TOPK)
                    link(e.tensor_tensor(o3, sel[:R, :].unsqueeze(2).to_broadcast([R, P, TOPK]),
                                         iota16[:R, :].unsqueeze(1).to_broadcast([R, P, TOPK]), ALU.is_equal))
                    yield STEP
                    link(e.tensor_tensor(oh, oh, ti[:, :, w, :].unsqueeze(2).to_broadcast([R, PH, TOPK, TOPK]), ALU.mult))
                    yield STEP
                    link(e.tensor_reduce(out[:R, :], o3, AX, ALU.add))
                    yield STEP
                link(e.scalar_tensor_tensor(out=e1[:R, :], in0=e1[:R, :], scalar=float(NKEY), in1=e2[:R, :], op0=ALU.mult, op1=ALU.add))
                e.wait_ge(s("gate_exp"), t + 1)
                link(e.tensor_reduce(gsum[:R, :], g3, AX, ALU.add))
                link(e.reciprocal(gsum[:R, :], gsum[:R, :]))
                u0 = t * PH * TOPK
                if t < PT:
                    mark(e.tensor_copy(idx_all[:, u0:u0 + 128], e1[:, :]))
                    link(e.tensor_tensor(gate_all[:, u0:u0 + 128].rearrange("p (h k) -> p h k", h=PH), g3,
                                         gsum[:, :].unsqueeze(2).to_broadcast([P, PH, TOPK]), ALU.mult))
                else:
                    hf = PH // 2
                    mark(e.tensor_copy(idx_all[:R, u0:u0 + 64], e1[:R, 0:64]))
                    mark(e.tensor_copy(ixs_hi, e1[:R, 64:128]))
                    mark(e.tensor_tensor(gate_all[:R, u0:u0 + 64].rearrange("p (h k) -> p h k", h=hf), g3[:, 0:hf],
                                         gsum[:R, 0:hf].unsqueeze(2).to_broadcast([R, hf, TOPK]), ALU.mult))
                    link(e.tensor_tensor(gts_hi.rearrange("p (h k) -> p h k", h=hf), g3[:, hf:PH],
                                         gsum[:R, hf:PH].unsqueeze(2).to_broadcast([R, hf, TOPK]), ALU.mult))
                e.sem_inc(s("route_ready"), 1)
                yield SEGMENT

            def embedding(pg):
                tiles = PLE_GROUPS[pg]
                nt = len(tiles)
                yield from norm_rows("ple", tiles)
                yield SEGMENT
                for i in pairs(e, 0, NBLK // 2, pg == 2):
                    for p in range(2):
                        for sl, t in enumerate(tiles):
                            R = ROWS[t]
                            u = (i * 2 + p) * nt + sl
                            x = (p * nt + sl) % 2
                            e.wait_ge(s("sigmoid_ready"), u + (EMBEDDED[pg] + 1))
                            e.tensor_tensor(sg[:R, x, :], sg[:R, x, :], bank[6 + x][:R, 0:NC], ALU.mult).then_inc(s("embed_read"), 1)
                            e.wait_ge(s("embed_read"), u + (EMBEDDED[pg] + 3))
                            if pg < 2:
                                yield STEP
                            hs = H[:R, sl, bass.ds((i * 2 + p) * NC, NC)]
                            e.tensor_tensor(hs, hs, sg[:R, x, :], ALU.add).then_inc(s("rows_added"), 1)
                            if pg < 2:
                                yield STEP
                    if pg < 2:
                        yield SEGMENT

            def woven():
                yield from route(1)
                yield from mixer(1)
                for t in range(2, T):
                    yield from route(t)
                for pg in range(2):
                    yield from embedding(pg)

            e.memset(ones[:, :], 1.0).then_inc(s("fills_ready"), 1)
            e.memset(eps[:, :], EPS).then_inc(s("fills_ready"), 1)
            e.sem_inc(s("rows_added"), 4)
            e.sem_inc(s("embed_read"), 2)
            e.wait_ge(s("consts_loaded"), 16 * 11)
            for x in mixer(0):
                pass
            for x in route(0):
                pass

            e.sem_inc(s("buffers_free"), RING)
            e.sem_inc(s("summed"), 1)
            weave = woven()
            left = [0]

            def steps(n):
                while n and left[0]:
                    if next(weave) == SEGMENT:
                        left[0] -= 1
                    n -= 1

            for t in range(T):
                nu = PH if t < PT else PH // 2
                xb = t % 2
                for j in range(nu):
                    u = t * PH + j
                    if j == 0:
                        left[0] += SEGMENTS[u]
                        if t == 2:
                            steps(10 ** 6)
                        e.wait_ge(s(f"xrow_loaded{xb}"), 16 * (t // 2 + 1 if t < PT else T - 1))
                        if t == PT:
                            e.wait_ge(s("sample_spread"), 32)
                    for k in range(TOPK):
                        b = k % RING
                        e.wait_ge(s(f"rows_landed{b}"), u * 64 + 16 * (k // RING + 1))
                        e.tensor_tensor_reduce(out=ring[:, b, :], in0=ring[:, b, :], in1=xrow[:, xb, :], scale=1.0, scalar=0.0,
                                               op0=ALU.mult, op1=ALU.add, accum_out=dots[:, k:k + 1]).then_inc(s("dots_done"), 1)
                        e.wait_ge(s("dots_done"), u * TOPK + k + 1)
                        e.sem_inc(s("buffers_free"), 1)
                        steps(STEPS_PER_SLOT)
                    steps(10 ** 6)
                    e.wait_ge(s("gelu_ready"), u + 1)
                    e.tensor_tensor(coef[:, :], gel[:, :], gate_all[:, u * TOPK:(u + 1) * TOPK], ALU.mult).then_inc(s("coef_ready"), 1)
                    e.wait_ge(s("coef_ready"), u + 1)
                    if j + 1 < nu:
                        left[0] += SEGMENTS[u + 1]
                    for k in range(TOPK):
                        b = k % RING
                        e.wait_ge(s(f"rows_landed{b}"), u * 64 + 16 * ((TOPK + k) // RING + 1))
                        e.wait_ge(s("summed"), u * TOPK + max(k, 1))
                        if j == 0 and k < 2:
                            e.tensor_scalar(acc[:, k, :], ring[:, b, :], coef[:, k:k + 1], None, ALU.mult).then_inc(s("summed"), 1)
                        else:
                            e.scalar_tensor_tensor(out=acc[:, k % 2, :], in0=ring[:, b, :], scalar=coef[:, k:k + 1], in1=acc[:, k % 2, :],
                                                   op0=ALU.mult, op1=ALU.add).then_inc(s("summed"), 1)
                        e.wait_ge(s("summed"), u * TOPK + k + 2)
                        e.sem_inc(s("buffers_free"), 1)
                        steps(STEPS_PER_SLOT)
                R = ROWS[t]
                if t < PT:
                    e.wait_ge(s("h_loaded"), 16 * (t + 1))
                    link(e.tensor_tensor(xrow[:, xb, :], xrow[:, xb, :], acc[:, 0, :], ALU.add))
                    link(e.tensor_tensor(xrow[:, xb, :], xrow[:, xb, :], acc[:, 1, :], ALU.add))
                else:
                    link(e.tensor_tensor(acc[:, 0, :], acc[:, 0, :], acc[:, 1, :], ALU.add))
                    e.sem_inc(s("sample_halves"), 1)
                    for x in weave:
                        pass
                    e.wait_ge(s("h_loaded"), 16 * (t + 1))
                    e.wait_ge(s("sample_back"), 16)
                    e.wait_ge(s("y_out"), 16 * PT)
                    link(e.tensor_tensor(acc[0:R, 0, :], acc[0:R, 0, :], acc[0:R, 1, :], ALU.add))
                    link(e.tensor_tensor(H[:R, 0, :], xrow[:R, xb, :], acc[0:R, 0, :], ALU.add))
                e.sem_inc(s("peer_done"), 1)
            for x in embedding(2):
                pass

        @block.gpsimd
        def _(e):
            for t in range(T):
                nu = PH if t < PT else PH // 2
                e.wait_ge(s("route_ready"), t + 1)
                if t == PT:
                    e.wait_ge(s("sample_spread"), 32)
                with e.Fori(t * PH // 2, t * PH // 2 + nu // 2) as i:
                    for p in range(2):
                        u = i * 2 + p
                        e.wait_ge(s("buffers_free"), u * (2 * TOPK) + 1)
                        e.tensor_copy(idx_cur[:, p, :], idx_all[:, bass.ds(u * TOPK, TOPK)]).then_inc(s("idx_ready"), 1)
                        e.wait_ge(s("idx_ready"), u + 1)
                        for k in range(2 * TOPK):
                            e.wait_ge(s("buffers_free"), u * (2 * TOPK) + k + 1)
                            e.sem_inc(s("slots_granted"), 1)
                            e.indirect_dma_start(out=ring[:, k % RING, :], out_offset=None,
                                                 in_=(a["peer_u"] if k < TOPK else a["peer_v"])[0],
                                                 in_offset=bass.IndirectOffsetOnAxis(ap=idx_cur[:, p, k % TOPK:k % TOPK + 1], axis=0))\
                                .then_inc(s(f"rows_landed{k % RING}"), 16)


_OUTS = [("y_p", (1, SEQ, D)), ("y_s", (DEC_B, DEC_T, D)), ("lat_p", (1, 1, SEQ, KVR)), ("kr_p", (1, 1, SEQ, ROPE)),
         ("ir_p", (1, 1, SEQ, H_MLA)), ("gla_p", (1, 1, H_GLA, GK, GV)), ("lat_s", (1, DEC_B, DEC_T, KVR)),
         ("kr_s", (1, DEC_B, DEC_T, ROPE)), ("ir_s", (1, DEC_B, DEC_T, H_MLA)), ("gla_s", (1, DEC_B, H_GLA, GK, GV))]


def kernel(**inputs):
    import concourse.bacc as bacc
    from concourse.bass_utils import run_bass_kernel_spmd

    nc = bacc.Bacc("TRN2", target_bir_lowering=False, num_devices=1)
    arrays, a, o, c = {}, {}, {}, {}
    for name, value in inputs.items():
        v = np.ascontiguousarray(value)
        arrays[f"in_{name}"] = v
        a[name] = nc.dram_tensor(f"in_{name}", v.shape, mybir.dt.from_np(v.dtype), kind="ExternalInput").ap()
    for name, v in constants().items():
        arrays[f"const_{name}"] = v
        c[name] = nc.dram_tensor(f"const_{name}", v.shape, F32, kind="ExternalInput").ap()
    for name, shape in _OUTS:
        o[name] = nc.dram_tensor(f"out_{name}", shape, F32, kind="ExternalOutput").ap()
    build(nc, a, o, c)
    r = run_bass_kernel_spmd(nc, [arrays], core_ids=[0])
    return tuple(r.results[0][f"out_{name}"] for name, _ in _OUTS)
```

```python
from contextlib import ExitStack

import numpy as np

import concourse.bass as bass
import concourse.mybir as mybir

ALU = mybir.AluOpType
ACT = mybir.ActivationFunctionType
AX = mybir.AxisListType.X
F32 = mybir.dt.float32
U32 = mybir.dt.uint32
I32 = mybir.dt.int32

P = 128
D = 2048
KD = D // P
SEQ = 512
DEC_B, DEC_T = 8, 8
NS = DEC_B * DEC_T
NTOK = SEQ + NS
PT = SEQ // P
T = PT + 1
ROWS = [P] * PT + [NS]
PAGE = 128
N_PAGES = 16
N_POOL = 160
PAST = PAGE * N_PAGES
H_MLA, NOPE, ROPE, DV = 8, 128, 64, 128
QK = NOPE + ROPE
QR, KVR = 512, 256
SCALE = QK ** -0.5
THETA = 10000.0
H_GLA, GK, GV = 4, 128, 256
GATE_R = 16
TAU = 16.0
IN_SPLITS = (QR, KVR, ROPE, H_GLA * GK, H_GLA * GK, H_GLA * GV, H_GLA * GV, GATE_R)
IN_COLS = sum(IN_SPLITS)
MLA_COLS = QR + KVR + ROPE
GLA_COLS = IN_COLS - MLA_COLS
IN_BLOCKS = 16
IN_NC = IN_COLS // IN_BLOCKS
NC = 256
NBLK = D // NC
GROUPS = [[0], [1, 2], [3, 4]]
PLE_GROUPS = [[0, 1], [2, 3], [4]]
MT = 2
HH = H_MLA // 2
PH, NKEY, TOPK = 8, 128, 16
PLE = 256
EPS = 1e-6
NEG = -1e30
LOWEST = -3e38
LEVELS = [64, 32, 16, 8, 4, 2, 1]
NLEV = len(LEVELS) + 1
SAMPLE_LEVEL0 = LEVELS.index(DEC_T // 2)
UNITS = PH * PT + PH // 2
FIRST_UNITS = [t * PH for t in range(T)] + [UNITS]
LAST = len(GROUPS) - 1
O_STORED = [16 * (2 * min(tiles[-1] + 1, PT) + (PT in tiles)) for tiles in GROUPS]
ROUTES = [r for g in GROUPS for t in g for r in ([(t, h, h + 2) for h in range(0, PH, 2)] if t == g[0] else [(t, 0, PH)])]
PASSES = {}
_landed = _served = _firsts = 0
for _name, _nt, _nb in ([(f"{k}{g}", nt, nb) for g, tiles in enumerate(GROUPS)
                         for k, nt, nb in (("in", len(tiles), IN_BLOCKS), ("out", len(tiles), NBLK), ("query", 2, PH))]
                        + [(f"gate{g}", len(tiles), NBLK) for g, tiles in enumerate(PLE_GROUPS)]):
    PASSES[_name] = (_landed, _served, None if _name.startswith("query") else _firsts)
    _firsts += 0 if _name.startswith("query") else _nb
    _landed += _nb // 2
    _served += _nb * _nt
IN_READ = {f"in{g}": 4 + tiles[0] * IN_BLOCKS for g, tiles in enumerate(GROUPS)}
ADDED = {f"out{g}": 4 + tiles[0] * NBLK for g, tiles in enumerate(GROUPS)}
ADDED.update({f"gate{g}": 4 + (T + tiles[0]) * NBLK for g, tiles in enumerate(PLE_GROUPS)})
NORMS = {k: n for n, k in enumerate(
    [(use, t) for g in GROUPS for use in ("x", "mix", "ffn") for t in g] + [("ple", t) for t in range(T)])}
HALVES = {k: n for n, k in enumerate([(hh, t) for g in GROUPS for hh in range(2) for t in g])}
PHALVES = {k: n for n, k in enumerate([(hh, t) for g in GROUPS for hh in range(2) for t in g if t < PT])}
GAINS = [(use, g[0]) for g in GROUPS for use in ("x", "mix", "ffn")] + [("ple", g[0]) for g in PLE_GROUPS]
Z_BEFORE = [32 + 16 * tiles[0] * IN_BLOCKS // 2 for tiles in GROUPS]
Z_STORED = [32 + 16 * (tiles[-1] + 1) * IN_BLOCKS // 2 for tiles in GROUPS]
EMBEDDED = [0, 2 * NBLK, 4 * NBLK]
RING = 8
SEGMENT = 0
STEP, HALF_STEP = 1, 0.5
NORM_PACE = 2
IN_PACE, OUT_PACE = 4.2, 1.2
HEAD_PACE, HALF_PACE = 1, 2
PREP_PACE, PAGES_PACE, SOFTMAX_PACE = 33, 2, 4
KEY_PACE = 0.4
ROUTE_PACE, LATE_PACE = 1, 4
EMBED_PACE = 3
LEAD = 5


def constants():
    i = np.arange(P)
    c = {"ident": np.eye(P, dtype=np.float32)}
    c["tri"] = (i[:, None] <= i[None, :]).astype(np.float32)
    j = np.arange(NS)
    same = (j[:, None] // DEC_T) == (j[None, :] // DEC_T)
    tri_s = np.zeros((P, NS), np.float32)
    tri_s[:NS] = (j[:, None] <= j[None, :]) & same
    c["tri_s"] = tri_s
    lev = np.zeros((P, NLEV, P), np.float32)
    for n, half in enumerate(LEVELS):
        s, t = i[:, None], i[None, :]
        lev[:, n] = (s // (2 * half) == t // (2 * half)) & (s % (2 * half) < half) & (t % (2 * half) >= half)
    lev[:, NLEV - 1] = np.eye(P)
    c["lev"] = lev
    c["causal"] = np.where(i[None, :] <= i[:, None], 0.0, NEG).astype(np.float32)
    m = np.full((P, DEC_B, DEC_B, DEC_T), NEG, np.float32)
    for b in range(DEC_B):
        for h in range(H_MLA):
            for t in range(DEC_T):
                m[h * DEC_T + t, b, b, :t + 1] = 0.0
    c["smask"] = m.reshape(P, DEC_B * NS)
    bm = np.zeros((P, DEC_B), np.float32)
    bm[j, j // DEC_T] = 1.0
    c["bmask"] = bm
    half = ROPE // 2
    inv = np.float32(THETA) ** (-np.arange(half, dtype=np.float32) / np.float32(half))
    pos = np.zeros((P, T), np.float32)
    for t in range(PT):
        pos[:, t] = t * P + i
    pos[:NS, PT] = PAST + j % DEC_T
    ang = pos[:, :, None] * inv
    cos, sin = np.cos(ang), np.sin(ang)
    c["cos"] = np.concatenate([cos, cos], -1).astype(np.float32)
    c["sin"] = np.concatenate([-sin, sin], -1).astype(np.float32)
    c["iota16"] = np.tile(np.arange(TOPK, dtype=np.float32), (P, 1))
    return c


def build(nc, a, o, c):
    ctx = ExitStack()
    with ctx:
        sems = {}

        def s(name):
            if name not in sems:
                sems[name] = nc.alloc_semaphore(name)
            return sems[name]

        def sb(name, shape, dt=F32):
            return ctx.enter_context(nc.sbuf_tensor(name, shape, dt))

        ring = sb("ring", [P, RING, D])
        acc = sb("acc", [P, 2, D])
        keysT = sb("keysT", [P, 2, P])
        keysR = ring[:, 0, 0:2 * P].rearrange("p (a b) -> p a b", b=P)
        xrow = sb("xrow", [P, 2, D])
        ident = sb("ident", [P, P])
        tri, tri_s = sb("tri", [P, P]), sb("tri_s", [P, NS])
        lev = sb("lev", [P, NLEV, P])
        causal = sb("causal", [P, P])
        smask = sb("smask", [P, DEC_B, NS])
        bmask = sb("bmask", [P, DEC_B])
        cosT, sinT = sb("cosT", [P, T, ROPE]), sb("sinT", [P, T, ROPE])
        iota16 = sb("iota16", [P, TOPK])
        pages = sb("pages", [1, DEC_B * N_PAGES], I32)
        eps = sb("eps", [P, 1])
        idx_all = sb("idx_all", [P, UNITS * TOPK], U32)
        gate_all = sb("gate_all", [P, UNITS * TOPK])
        idx_cur = sb("idx_cur", [P, 3, TOPK], U32)
        dots, gel, coef = sb("dots", [P, 2, TOPK]), sb("gel", [P, 2, TOPK]), sb("coef", [P, TOPK])
        ns = len(NORMS)
        st = sb("st", [P, 3 * ns])
        ms = sb("ms", [P, 112])
        FW = 24048
        front = sb("front", [P, FW])
        used = [0]

        def carve(*shape, at=None):
            if at is not None:
                used[0] = at
            n = int(np.prod(shape))
            ap = front[:, used[0]:used[0] + n]
            used[0] += n
            assert used[0] <= FW, used[0]
            if len(shape) == 2:
                ap = ap.rearrange("p (a b) -> p a b", b=shape[1])
            if len(shape) == 3:
                ap = ap.rearrange("p (a b c) -> p a b c", b=shape[1], c=shape[2])
            return ap

        GT = MT * P
        XT = carve(KD, GT, at=0)
        W = [carve(KD * NC), carve(KD * NC)]
        h0 = used[0]
        H = carve(MT, D)
        y0 = used[0]
        Y = carve(D)
        G = carve(D)
        zst = carve(2 * MT, NC, at=h0)
        topv, topi = carve(MT, 16, TOPK, at=h0), carve(MT, 16, TOPK)
        swork = carve(MT, P)
        topu = carve(MT, TOPK).bitcast(U32)
        qTm = carve(2, GT)
        sela, selh, sell = [carve(P).bitcast(U32) for _ in range(3)]
        selhf, sellf, e1, e2, gtop = [carve(P) for _ in range(5)]
        gsum = carve(PH)
        ixs_hi, gts_hi = carve(64)[0:NS].bitcast(U32), carve(64)[0:NS]
        assert used[0] <= y0
        cand, candw = Y, G
        oneh = candw
        pT_ple = carve(PLE // P, 2 * P, at=y0 + 2 * D)
        p_row = carve(2, PLE)
        w_pp = [carve(PLE // P, NC), carve(PLE // P, NC)]
        sg = G.rearrange("p (a b) -> p a b", a=8)

        c_rows, cT = carve(KVR, at=0), carve(MT, KVR // P, P)
        kr_o = carve(MT, ROPE)
        qgT, qrT = carve(H_MLA, NS), carve(DEC_B, NS)
        low = used[0]
        m_z, cqn, cqT, kr_g = carve(MLA_COLS), carve(QR), carve(MT, QR // P, P), carve(ROPE)
        g_q, g_kv, g_k, g_qk = carve(QR), carve(KVR), carve(QK), carve(QK)
        half0 = max(used[0], low + PAST + NS + 3 * 512 + 2 * NS)
        used[0] = half0
        wq, wk, wv = carve(QR // P, HH * QK), carve(KVR // P, HH * NOPE), carve(KVR // P, HH * DV)
        KTn, KTr, V = carve(HH, SEQ), carve(HH // 2, SEQ), carve(PT, HH * DV)
        qrow, krow, sqs = carve(HH, QK), carve(HH, NOPE), carve(HH * QK)
        qro, kro, rtmp = carve(HH, ROPE), carve(HH, ROPE), carve(HH, ROPE)
        QTn, QTr = carve(HH, P), carve(HH // 2, P)
        pr, pT = carve(2, SEQ), carve(2, SEQ)
        orow = carve(HH * DV)
        sc = carve(PAST + NS, at=low)
        latT = carve(3, 512)
        krT, ikx = carve(NS), carve(NS)
        assert used[0] <= half0
        pages_sb = []
        used[0] = half0
        for _ in range(2):
            pages_sb.append((carve(N_PAGES, KVR), carve(N_PAGES, ROPE), carve(N_PAGES, H_MLA)))
        wuv_f = carve(KVR // P, H_MLA * DV)
        pTs = carve(N_PAGES + 1, NS)
        q_lat = [carve(DEC_B, NS), carve(DEC_B, NS)]
        oT = [carve(H_MLA, NS), carve(H_MLA, NS)]
        olr = carve(KVR)
        ire = carve(N_PAGES, NS)
        irs = carve(512)
        wuk_f, w_ukT = carve(KVR // P, H_MLA * NOPE, at=half0), carve(H_MLA, KVR)
        so_rows = carve(H_MLA * DV, at=half0)
        gz = carve(GLA_COLS, at=0)
        w_ga, g_go = carve(H_GLA * GK), carve(GV)
        S0 = carve(H_GLA, GV)
        Ss = [carve(DEC_B, GV), carve(DEC_B, GV)]
        gx, gt1, gt2 = carve(H_GLA * GK), carve(H_GLA * GK), carve(H_GLA * GK)
        alT = carve(P)
        gqT, gkT, gbT = carve(H_GLA * GK), carve(H_GLA * GK), carve(H_GLA * GK)
        Mlev = carve(NLEV - 1, H_GLA * P)
        dlev = carve(2, H_GLA * P)
        am = carve(NLEV, P)
        AT = carve(H_GLA, P)
        eb, qe, kd = carve(H_GLA * P), carve(H_GLA * P), carve(H_GLA * P)
        kdr = carve(H_GLA, GK)
        go, gsil = carve(H_GLA * GV), carve(H_GLA * GV)
        gsq = dlev.rearrange("p a b -> p (a b)")
        qz, kz = carve(DEC_B, NS), carve(DEC_B, GK)
        eL = carve(H_GLA * DEC_B)

        bank = [ctx.enter_context(nc.psum_tensor(f"bank{i}", [P, 512], F32)) for i in range(8)]

        def scratch(name, *shape):
            return nc.dram_tensor(name, list(shape), F32).ap()

        z_dram = scratch("z_dram", NTOK, IN_COLS)
        mix_dram = scratch("mix_dram", NTOK, D)
        h_dram = scratch("h_dram", NTOK, D)
        xn_dram = scratch("xn_dram", NTOK, D)
        h2_dram = scratch("h2_dram", NTOK, D)
        kt_dram = scratch("kt_dram", 2, P, HH, SEQ)
        ktr_dram = scratch("ktr_dram", 2, P, HH // 2, SEQ)
        v_dram = scratch("v_dram", 2, P, PT, HH * DV)
        s_dram = scratch("s_dram", P, H_GLA, GV)

        def rows(t):
            return slice(t * P, t * P + ROWS[t])

        def tile_of(prompt, sample, t):
            return prompt[rows(t), :] if t < PT else sample.rearrange("b t d -> (b t) d")

        def x_rows(t):
            return tile_of(a["x_prompt"][0], a["x_sample"], t)

        def down(dram_row, n=P):
            return dram_row.partition_broadcast(n)

        def slot(t):
            return next(t - tiles[0] for tiles in GROUPS if t in tiles)

        def first_slot(u, side):
            if side == 0:
                return (2 * u - 1) * TOPK if u else 0
            return (2 * u + 2) * TOPK if u < UNITS - 1 else (2 * u + 1) * TOPK

        def pairs(e, lo, hi, looped):
            if looped:
                with e.Fori(lo, hi) as i:
                    yield i
            else:
                for i in range(lo, hi):
                    yield i

        SSQ, RQ, IQ = ms[:, 0:1], ms[:, 1:2], ms[:, 2:3]
        SSC, RC, IC = ms[:, 3:4], ms[:, 4:5], ms[:, 5:6]
        SQH, RQH, IQH = ms[:, 8:12], ms[:, 12:16], ms[:, 16:20]
        SKH, RKH = ms[:, 20:24], ms[:, 24:28]
        MXV, NMX, RSUM, RINV = ms[:, 28:32], ms[:, 32:36], ms[:, 36:40], ms[:, 40:44]
        GSS, GRS, GIS = ms[:, 44:48], ms[:, 48:52], ms[:, 52:56]

        def SKR(t):
            return ms[:, 56 + slot(t):57 + slot(t)]

        def IKH(t):
            return ms[:, 64 + 8 * slot(t):72 + 8 * slot(t)]

        def heads(ap, R):
            return ap[:, 0:H_GLA * P].rearrange("p (h n) -> p h n", h=H_GLA)[:, :, 0:R]

        def level_count(t, n):
            per = NLEV - 1
            return t * per + n if t < PT else PT * per + n - SAMPLE_LEVEL0

        def by_batch(ap, h0_=0, n=H_MLA):
            return ap.rearrange("p b (h t) -> p h b t", h=H_MLA)[:, h0_:h0_ + n]

        def four(ap, R=P):
            return ap[:, :].rearrange("p (j n) -> p j n", j=4)[:, :, 0:R]

        def out_bank(p, sl):
            return bank[3 * p + sl]

        segments_before, segments_after = [], []
        segments_summed = []

        block = ctx.enter_context(nc.Block())

        @block.sync
        def _(e):
            def weight_blocks(name, w, ncol, nblk, nt, extra=None, between=None):
                served, firsts = PASSES[name][1:]

                def load(i, p, half):
                    col = bass.ds((i * 2 + p) * ncol, ncol)
                    k = slice(half * KD // 2, (half + 1) * KD // 2)
                    e.dma_start(W[p][:, 0:KD * ncol].rearrange("p (k n) -> p k n", k=KD)[:, k, :],
                                w[k.start * P:k.stop * P, col].rearrange("(k p) n -> p k n", p=P)).then_inc(s(f"w_landed{p}_{half}"), 16)
                    if extra is not None and half == 0:
                        e.dma_start(w_pp[p], extra[:, col].rearrange("(k p) n -> p k n", p=P))\
                            .then_inc(s(f"w_landed{p}_0"), 16)
                for p in range(2):
                    for half in range(2):
                        load(0, p, half)
                if between is not None:
                    between()
                with e.Fori(1, nblk // 2) as i:
                    for p in range(2):
                        early = firsts is not None and extra is None
                        if early:
                            e.wait_ge(s("first_halves_used"), (i * 2 + p - 1) + firsts)
                            load(i, p, 0)
                        e.wait_ge(s("tiles_projected"), (i * 2 + p - 1) * nt + served)
                        if not early:
                            load(i, p, 0)
                        load(i, p, 1)

            for name, dst in (("ident", ident), ("tri", tri), ("tri_s", tri_s), ("lev", lev), ("causal", causal),
                              ("bmask", bmask), ("cos", cosT), ("sin", sinT), ("iota16", iota16)):
                v = dst[:, :] if name not in ("lev", "cos", "sin") else dst[:, :, :]
                e.dma_start(v, c[name]).then_inc(s("consts_loaded"), 16)
            e.dma_start(smask[:, :, :].rearrange("p a b -> p (a b)"), c["smask"]).then_inc(s("consts_loaded"), 16)
            for side in range(2):
                e.dma_start(keysR[:, side, :], a[("peer_keys1", "peer_keys2")[side]][0]).then_inc(s("consts_loaded"), 16)
            e.dma_start(pages[:, :], a["page_table"].rearrange("b n -> (b n)").rearrange("(o n) -> o n", o=1))\
                .then_inc(s("consts_loaded"), 16)

            def mixer_loads(g):
                tiles = GROUPS[g]
                nt = len(tiles)
                if g:
                    e.wait_ge(s("route_ready"), sum(1 for t, _, _ in ROUTES if t < tiles[0]))
                for t in tiles:
                    e.dma_start(H[:ROWS[t], slot(t), :], x_rows(t)).then_inc(s("rows_loaded"), 16)
                e.dma_start(G, down(a["norm_mix"][0])).then_inc(s("gain_loaded"), 16)
                weight_blocks(f"in{g}", a["w_in"][0], IN_NC, IN_BLOCKS, nt)

                e.wait_ge(s("tiles_projected"), PASSES[f"out{g}"][1])
                e.wait_ge(s("z_stored0"), Z_STORED[g])
                e.wait_ge(s("z_stored1"), Z_STORED[g])
                for dst, src in ((g_q, down(a["norm_q_lat"][0])), (g_kv, down(a["norm_kv_lat"][0])),
                                 (g_k, down(a["qk_gain_k"][0])), (g_qk, down(a["qk_gain_q"][0]))):
                    e.dma_start(dst, src).then_inc(s("mla_gains_loaded"), 16)
                for t in tiles:
                    R = ROWS[t]
                    if t:
                        e.wait_ge(s("rope_key_ready"), t)
                    e.dma_start(m_z[:R, :], z_dram[rows(t), 0:MLA_COLS]).then_inc(s("mla_z_loaded"), 16)
                    if t == tiles[0]:
                        half_weights(g, 0)
                        if g:
                            old_keys(g, 0)
                    e.wait_ge(s("mla_latents_normed"), t + 1)
                    e.dma_start(tile_of(o["lat_p"][0, 0], o["lat_s"][0], t), c_rows[:R, :]).then_inc(s("lat_stored"), 16)
                    e.wait_ge(s("rope_key_ready"), t + 1)
                    e.dma_start(tile_of(o["kr_p"][0, 0], o["kr_s"][0], t), kr_o[:R, slot(t), :]).then_inc(s("mla_outputs"), 16)
                for hh in range(2):
                    for t in tiles:
                        if hh == 0 and t == tiles[-1]:
                            half_weights(g, 1)
                        if t < PT:
                            n = PHALVES[hh, t]
                            e.wait_ge(s("mla_o_rows"), n + 1)
                            e.dma_start(mix_dram[rows(t), hh * HH * DV:(hh + 1) * HH * DV], orow).then_inc(s("o_stored"), 16)
                    if g and hh == 0:
                        old_keys(g, 1)
                    if g < LAST:
                        n = PHALVES[hh, tiles[-1]] + 1
                        e.wait_ge(s("kT_sb"), n)
                        e.wait_ge(s("v_sb"), n)
                        new = slice(tiles[0] * P, (tiles[-1] + 1) * P)
                        e.dma_start(kt_dram[hh][:, :, new], KTn[:, :, new]).then_inc(s("keys_parked"), 16)
                        e.dma_start(ktr_dram[hh][:, :, new], KTr[:, :, new]).then_inc(s("keys_parked"), 16)
                        e.dma_start(v_dram[hh][:, tiles[0]:tiles[-1] + 1, :], V[:, tiles[0]:tiles[-1] + 1, :])\
                            .then_inc(s("keys_parked"), 16)
                for t in tiles:
                    e.wait_ge(s("ikh_ready"), HALVES[1, t] + 1)
                    e.dma_start(tile_of(o["ir_p"][0, 0], o["ir_s"][0], t), IKH(t)[:ROWS[t], :]).then_inc(s("mla_outputs"), 16)

                if PT in tiles:
                    e.wait_ge(s("pv_done"), HH * len(PHALVES))
                    e.wait_ge(s("o_stored"), 16 * len(PHALVES))
                    e.wait_ge(s("q_rows_ready"), len(HALVES))
                    e.wait_ge(s("k_rows_ready"), len(HALVES))
                    e.wait_ge(s("sample_qT_psum"), 2)
                    e.dma_start(wuk_f, a["w_uk"][0].rearrange("(k p) h d -> p k (h d)", p=P)).then_inc(s("sample_w_loaded"), 16)
                    e.dma_start(wuv_f, a["w_uv"][0].rearrange("(k p) h d -> p k (h d)", p=P)).then_inc(s("sample_w_loaded"), 16)
                    e.wait_ge(s("sprep_psum"), 6)
                    for b in range(DEC_B):
                        if b >= 2:
                            e.wait_ge(s("olat_psum"), b - 1)
                        for q in range(N_PAGES):
                            i = b * N_PAGES + q
                            pg = e.value_load(pages[0:1, i:i + 1], min_val=0, max_val=N_POOL - 1)
                            for dst, pool in zip(pages_sb[b % 2], ("cache_kv_latent", "cache_k_rope", "cache_k_inv_rms")):
                                e.dma_start(dst[:, q, :], a[pool][0, bass.ds(pg, 1), :, :].rearrange("o p d -> (o p) d"))\
                                    .then_inc(s(f"pages_landed{b % 2}"), 16)
                    e.wait_ge(s("sample_o_rows"), 1)
                    e.dma_start(mix_dram[rows(PT), 0:H_MLA * DV], so_rows[:NS, :]).then_inc(s("o_stored"), 16)

                e.wait_ge(s("o_stored"), O_STORED[g])
                e.wait_ge(s("mla_outputs"), 16 * 2 * (tiles[-1] + 1))
                e.wait_ge(s("lat_stored"), 16 * (tiles[-1] + 1))
                if g < LAST:
                    e.wait_ge(s("keys_parked"), 16 * 6 * (g + 1))
                e.dma_start(w_ga[0:GATE_R, :], a["w_gla_a"][0]).then_inc(s("gla_w_loaded"), 16)
                e.dma_start(w_ga[GATE_R:GATE_R + 1, :], a["b_gla_a"][0].rearrange("(o n) -> o n", o=1)).then_inc(s("gla_w_loaded"), 16)
                e.dma_start(g_go, down(a["norm_gla_out"][0])).then_inc(s("gla_w_loaded"), 16)
                if g:
                    e.dma_start(S0, s_dram).then_inc(s("gla_w_loaded"), 16)

                def head_state(h):
                    e.dma_start(Ss[h % 2], a["state_gla"][0, :, h].rearrange("b k v -> k b v")).then_inc(s(f"state_loaded{h % 2}"), 16)

                for t in tiles:
                    if t != tiles[0]:
                        e.wait_ge(s("gla_read"), t)
                    e.dma_start(gz[:ROWS[t], :], z_dram[rows(t), MLA_COLS:IN_COLS]).then_inc(s("gla_z_loaded"), 16)
                    if t == PT:
                        head_state(0)
                        head_state(1)
                        for h in range(H_GLA):
                            e.wait_ge(s("sample_state_head"), h + 1)
                            e.dma_start(o["gla_s"][0, :, h].rearrange("b k v -> k b v"), Ss[h % 2]).then_inc(s("state_out"), 16)
                            if h < 2:
                                e.wait_ge(s("state_out"), 16 * (LAST + 2 + h))
                                head_state(h + 2)
                    e.wait_ge(s("gla_o_ready"), t + 1)
                    e.dma_start(mix_dram[rows(t), H_MLA * DV:D], go[:ROWS[t], :]).then_inc(s("go_stored"), 16)
                    if t == tiles[-1] and g < LAST:
                        e.wait_ge(s("gla_state"), H_GLA * (t + 1))
                        e.dma_start(s_dram, S0).then_inc(s("state_out"), 16)
                        e.wait_ge(s("state_out"), 16 * (g + 1))
                    if t == PT - 1:
                        e.wait_ge(s("gla_state"), H_GLA * PT)
                        e.dma_start(o["gla_p"][0, 0].rearrange("h k v -> k h v"), S0).then_inc(s("state_out"), 16)
                        e.wait_ge(s("state_out"), 16 * (LAST + 1))

                e.wait_ge(s("go_stored"), 16 * (tiles[-1] + 1))
                if PT in tiles:
                    e.wait_ge(s("state_out"), 16 * (LAST + 1 + H_GLA))
                for t in tiles:
                    e.dma_start(H[:ROWS[t], slot(t), :], mix_dram[rows(t), :]).then_inc(s("rows_loaded"), 16)
                e.dma_start(G[:, 0:H_MLA * DV], down(a["norm_mla_out"][0])).then_inc(s("gain_loaded"), 16)

                def residual_rows():
                    for t in tiles:
                        e.wait_ge(s("nt_transposed"), 4 * (NORMS["mix", t] + 1))
                        e.dma_start(H[:ROWS[t], slot(t), :], x_rows(t)).then_inc(s("rows_loaded"), 16)
                    e.wait_ge(s("normed"), NORMS["mix", tiles[-1]] + 1)
                    e.dma_start(G, down(a["norm_ffn"][0])).then_inc(s("gain_loaded"), 16)

                weight_blocks(f"out{g}", a["w_out"][0], NC, NBLK, nt, between=residual_rows)

                def store_rows():
                    for t in tiles:
                        e.wait_ge(s("normed"), NORMS["ffn", t] + 1)
                        e.dma_start(xn_dram[rows(t), :], Y[:ROWS[t], :]).then_inc(s("xn_stored"), 16)
                    for t in tiles:
                        e.wait_ge(s("rows_added"), ADDED[f"out{g}"] + (NBLK - 1) * nt + slot(t) + 1)
                        e.dma_start(h_dram[rows(t), :], H[:ROWS[t], slot(t), :]).then_inc(s("h_stored"), 16)

                e.wait_ge(s("tiles_projected"), PASSES[f"query{g}"][1])
                weight_blocks(f"query{g}", a["peer_w_q"][0], NC, PH, 2, between=store_rows)

            def half_weights(g, hh):
                if hh:
                    e.wait_ge(s("k_ready"), HALVES[1, GROUPS[g][0]])
                    e.wait_ge(s("v_ready"), PHALVES[1, GROUPS[g][0]])
                e.dma_start(wq, a["w_uq"][0][:, hh * HH * QK:(hh + 1) * HH * QK].rearrange("(k p) n -> p k n", p=P))\
                    .then_inc(s("half_w_loaded"), 16)
                e.dma_start(wk, a["w_uk"][0][:, hh * HH:(hh + 1) * HH, :].rearrange("(k p) h d -> p k (h d)", p=P))\
                    .then_inc(s("half_w_loaded"), 16)
                e.dma_start(wv, a["w_uv"][0][:, hh * HH:(hh + 1) * HH, :].rearrange("(k p) h d -> p k (h d)", p=P))\
                    .then_inc(s("half_w_loaded"), 16)

            def old_keys(g, hh):
                n = GROUPS[g][0]
                if hh:
                    e.wait_ge(s("pv_done"), HH * PHALVES[1, n])
                e.dma_start(KTn[:, :, 0:n * P], kt_dram[hh][:, :, 0:n * P]).then_inc(s("old_keys_loaded"), 16)
                e.dma_start(KTr[:, :, 0:n * P], ktr_dram[hh][:, :, 0:n * P]).then_inc(s("old_keys_loaded"), 16)
                e.dma_start(V[:, 0:n, :], v_dram[hh][:, 0:n, :]).then_inc(s("old_keys_loaded"), 16)

            def embedding_loads(pg):
                tiles = PLE_GROUPS[pg]
                nt = len(tiles)
                if pg == 0:
                    e.wait_ge(s("route_ready"), len(ROUTES))
                else:
                    e.wait_ge(s("y_out"), 16 * PLE_GROUPS[pg][0])
                for t in tiles:
                    if t < PT:
                        e.wait_ge(s("h2_stored"), 16 * (t + 1))
                        e.dma_start(H[:ROWS[t], t % 2, :], h2_dram[rows(t), :]).then_inc(s("rows_loaded"), 16)
                if pg:
                    e.wait_ge(s("rows_added"), ADDED[f"gate{pg}"])
                e.dma_start(G, down(a["norm_ple"][0])).then_inc(s("gain_loaded"), 16)
                e.wait_ge(s("tiles_projected"), PASSES[f"gate{pg}"][1])
                for t in tiles:
                    e.dma_start(p_row[:ROWS[t], t % 2, :], tile_of(a["p_prompt"][0, 0], a["p_sample"][0], t))\
                        .then_inc(s("p_loaded"), 16)
                weight_blocks(f"gate{pg}", a["w_ple_gate"][0], NC, NBLK, nt, extra=a["w_ple_proj"][0])
                for t in tiles:
                    e.wait_ge(s("rows_added"), ADDED[f"gate{pg}"] + (NBLK - 1) * nt + t % 2 + 1)
                    e.dma_start(tile_of(o["y_p"][0], o["y_s"], t), H[:ROWS[t], t % 2, :]).then_inc(s("y_out"), 16)

            for g in range(len(GROUPS)):
                mixer_loads(g)
            e.wait_ge(s("route_ready"), len(ROUTES))
            lo = slice(PH * PT * TOPK, UNITS * TOPK)
            e.dma_start(idx_all[NS:P, lo], ixs_hi).then_inc(s("sample_spread"), 16)
            e.dma_start(gate_all[NS:P, lo], gts_hi).then_inc(s("sample_spread"), 16)
            e.wait_ge(s("sample_spread"), 32)
            for pg in range(len(PLE_GROUPS)):
                embedding_loads(pg)
            e.wait_ge(s("y_out"), 16 * T)

        @block.tensor
        def _(e):
            def norm_transposes(use, tiles):
                for t in tiles:
                    R = ROWS[t]
                    n = NORMS[use, t]
                    sl = slot(t) if use != "ple" else t % 2
                    e.wait_ge(s("normed"), n + 1)
                    for q in range(4):
                        m = 4 * n + q
                        if m >= 2:
                            e.wait_ge(s("nt_evacuated"), m - 1)
                        for j in range(4):
                            k = 4 * q + j
                            src = H[:R, sl, k * P:(k + 1) * P] if use == "mix" and k >= 8 else Y[:R, k * P:(k + 1) * P]
                            mm = e.transpose(bank[6 + m % 2][:, j * P:j * P + R], src, ident[:R, :R])
                        mm.then_inc(s("nt_transposed"), 1)

            def project(name, tiles, ncol, nblk, free, free0, embed=False):
                nt = len(tiles)
                landed = PASSES[name][0]
                pg = int(name[-1])
                with e.Fori(0, nblk // 2) as i:
                    for p in range(2):
                        w = W[p][:, 0:KD * ncol].rearrange("p (k n) -> p k n", k=KD)
                        if embed:
                            e.wait_ge(s(f"w_landed{p}_0"), i * 32 + (16 * landed + 16 * (landed - PASSES["gate0"][0]) + 32))
                        else:
                            e.wait_ge(s(f"w_landed{p}_0"), (i + landed + 1) * 16)
                        for sl, t in enumerate(tiles):
                            R = ROWS[t]
                            u = (i * 2 + p) * nt + sl
                            if embed:
                                x = (p * nt + sl) % 2
                                e.wait_ge(s("embed_read"), u + EMBEDDED[pg] + 1)
                                for k in range(PLE // P):
                                    e.matmul(bank[6 + x][:R, 0:NC], pT_ple[:, k, sl * P:sl * P + R], w_pp[p][:, k, :],
                                             start=(k == 0), stop=(k == 1))
                            e.wait_ge(s(free), u + (free0 - 2 * nt + 1))
                            for k in range(KD // 2):
                                mm = e.matmul(out_bank(p, sl)[:R, 0:ncol], XT[:, k, sl * P:sl * P + R], w[:, k, :],
                                              start=(k == 0), stop=False)
                        mm.then_inc(s("first_halves_used"), 1)
                        e.wait_ge(s(f"w_landed{p}_1"), (i + landed + 1) * 16)
                        for sl, t in enumerate(tiles):
                            R = ROWS[t]
                            for k in range(KD // 2, KD):
                                mm = e.matmul(out_bank(p, sl)[:R, 0:ncol], XT[:, k, sl * P:sl * P + R], w[:, k, :],
                                              start=False, stop=(k == KD - 1))
                            mm.then_inc(s("tiles_projected"), 1)

            def latent_attention(g):
                tiles = GROUPS[g]
                for t in tiles:
                    R = ROWS[t]
                    e.wait_ge(s("mla_latents_normed"), t + 1)
                    if t:
                        e.wait_ge(s("latT_ready"), t)
                    for k in range(4):
                        e.transpose(bank[0][:, k * P:k * P + R], cqn[:R, k * P:(k + 1) * P], ident[:R, :R])
                    for k in range(2):
                        mm = e.transpose(bank[1][:, k * P:k * P + R], c_rows[:R, k * P:(k + 1) * P], ident[:R, :R])
                    mm.then_inc(s("lat_transposed"), 1)
                e.wait_ge(s("latT_ready"), tiles[-1] + 1)
                for hh in range(2):
                    e.wait_ge(s("half_w_loaded"), 48 * (2 * g + hh + 1))
                    for t in tiles:
                        R = ROWS[t]
                        n = HALVES[hh, t]
                        m = PHALVES[hh, t] if t < PT else len(PHALVES)
                        before = sum(1 for k, v in HALVES.items() if v < n and k[1] < PT)
                        if n:
                            e.wait_ge(s("q_rows_ready"), n)
                            e.wait_ge(s("k_rows_ready"), n)
                        if before:
                            e.wait_ge(s("exp_done"), HH * before)
                            e.wait_ge(s("pT_sb"), HH * before)
                            e.wait_ge(s("v_sb"), before)
                        for j in range(2):
                            for k in range(4):
                                mm = e.matmul(bank[j][:R, 0:2 * QK], cqT[:, slot(t), k, 0:R], wq[:, k, j * 2 * QK:(j + 1) * 2 * QK],
                                              start=(k == 0), stop=(k == 3))
                        mm.then_inc(s("q_ready"), 1)
                        for k in range(2):
                            mm = e.matmul(bank[2][:R, :], cT[:, slot(t), k, 0:R], wk[:, k, :], start=(k == 0), stop=(k == 1))
                        mm.then_inc(s("k_ready"), 1)
                        if t < PT:
                            for k in range(2):
                                mm = e.matmul(bank[3][:R, :], cT[:, slot(t), k, 0:R], wv[:, k, :], start=(k == 0), stop=(k == 1))
                            mm.then_inc(s("v_ready"), 1)
                        e.wait_ge(s("q_rows_ready"), n + 1)
                        if t == PT:
                            if before:
                                e.wait_ge(s("mla_o_rows"), before)
                            if hh:
                                e.wait_ge(s("sample_qT_sb"), 1)
                            for h in range(HH):
                                e.transpose(bank[4][:, h * NS:(h + 1) * NS], qrow[:NS, h, 0:NOPE], ident[:NS, :NS])
                            for h in range(HH):
                                mm = e.transpose(bank[5][0:ROPE, h * NS:(h + 1) * NS], qro[:NS, h, :], ident[:NS, :NS])
                            mm.then_inc(s("sample_qT_psum"), 1)
                            continue
                        if before:
                            e.wait_ge(s("mla_o_rows"), before)
                        if hh and PT in tiles:
                            e.wait_ge(s("sample_qT_sb"), 1)
                        for h in range(HH):
                            e.transpose(bank[4][:, h * P:(h + 1) * P], qrow[:, h, 0:NOPE], ident[:, :])
                        for j in range(2):
                            mm = e.transpose(bank[5][:, j * P:(j + 1) * P],
                                             qro[:, 2 * j:2 * j + 2, :].rearrange("p a b -> p (a b)"), ident[:, :])
                        mm.then_inc(s("qT_psum"), 1)
                        e.wait_ge(s("k_rows_ready"), n + 1)
                        for h in range(HH):
                            e.transpose(bank[6][:, h * P:(h + 1) * P], krow[:, h, :], ident[:, :])
                        for j in range(2):
                            mm = e.transpose(bank[7][:, j * P:(j + 1) * P],
                                             kro[:, 2 * j:2 * j + 2, :].rearrange("p a b -> p (a b)"), ident[:, :])
                        mm.then_inc(s("kT_psum"), 1)
                        e.wait_ge(s("qT_sb"), m + 1)
                        e.wait_ge(s("kT_sb"), m + 1)
                        e.wait_ge(s("v_sb"), m + 1)
                        if g:
                            e.wait_ge(s("old_keys_loaded"), 48 * (2 * (g - 1) + hh + 1))
                        nk = (t + 1) * P

                        def scores(h):
                            if h >= 2:
                                e.wait_ge(s("exp_done"), m * HH + h - 1)
                            S = bank[h % 2]
                            r = slice((h % 2) * ROPE, (h % 2 + 1) * ROPE)
                            e.matmul(S[:, 0:nk], QTn[:, h, :], KTn[:, h, 0:nk], start=True, stop=False)
                            e.matmul(S[:, 0:nk], QTr[r, h // 2, :], KTr[r, h // 2, 0:nk], start=False, stop=False)
                            e.matmul(S[:, t * P:nk], ident[:, :], causal[:, :], start=False, stop=True)\
                                .then_inc(s("scores_ready"), 1)

                        scores(0)
                        for h in range(HH):
                            u = m * HH + h
                            if h + 1 < HH:
                                scores(h + 1)
                            e.wait_ge(s("exp_done"), u + 1)
                            if h >= 2:
                                e.wait_ge(s("pT_sb"), u - 1)
                            for kt in range(t + 1):
                                mm = e.transpose(bank[2 + h % 2][:, kt * P:(kt + 1) * P], pr[:, h % 2, kt * P:(kt + 1) * P], ident[:, :])
                            mm.then_inc(s("pT_psum"), 1)
                            e.wait_ge(s("pT_sb"), u + 1)
                            for kt in range(t + 1):
                                mm = e.matmul(bank[4][:, h * DV:(h + 1) * DV], pT[:, h % 2, kt * P:(kt + 1) * P],
                                              V[:, kt, h * DV:(h + 1) * DV], start=(kt == 0), stop=(kt == t))
                            mm.then_inc(s("pv_done"), 1)

            def sample_attention():
                e.wait_ge(s("sample_w_loaded"), 32)
                for h in range(H_MLA):
                    for k in range(2):
                        j = h * 2 + k
                        if j % 4 == 0 and j >= 4:
                            e.wait_ge(s("sprep_act"), j // 4)
                        mm = e.transpose(bank[0][:, (j % 4) * P:(j % 4 + 1) * P], wuk_f[:, k, h * NOPE:(h + 1) * NOPE], ident[:, :])
                        if j % 4 == 3:
                            mm.then_inc(s("sprep_psum"), 1)
                e.wait_ge(s("rope_key_ready"), T)
                e.transpose(bank[1][0:ROPE, 0:NS], kr_o[:NS, slot(PT), :], ident[:NS, :NS]).then_inc(s("sprep_psum"), 1)
                e.wait_ge(s("sample_qT_sb"), 2)
                e.wait_ge(s("sprep_act"), 4)
                e.wait_ge(s("mla_o_rows"), len(PHALVES))
                for k in range(2):
                    for h in range(H_MLA):
                        mm = e.matmul(bank[4 + k][:, h * NS:(h + 1) * NS], w_ukT[:, h, k * P:(k + 1) * P], qgT[:, h, :],
                                      start=True, stop=True)
                mm.then_inc(s("sprep_psum"), 1)
                e.wait_ge(s("sprep_act"), 7)
                for b in range(DEC_B):
                    latb, krb, _ = pages_sb[b % 2]
                    e.wait_ge(s(f"pages_landed{b % 2}"), 16 * 3 * N_PAGES * (b // 2 + 1))
                    for g in range(4):
                        u = 4 * b + g
                        if u:
                            e.wait_ge(s("latT_sb"), u)
                        for j in range(4):
                            pg = 4 * g + j
                            for k in range(2):
                                e.transpose(bank[k][:, j * P:(j + 1) * P], latb[:, pg, k * P:(k + 1) * P], ident[:, :])
                            mm = e.transpose(bank[2][0:ROPE, j * P:(j + 1) * P], krb[:, pg, :], ident[:, :])
                        mm.then_inc(s("latT_psum"), 1)
                        if u:
                            e.wait_ge(s("ir_sb"), u)
                        if g == 0:
                            e.wait_ge(s("ire_ready"), b + 1)
                        for j in range(4):
                            mm = e.matmul(bank[3][0:NS, j * P:(j + 1) * P], ire[:, 4 * g + j, :], ident[:, :], start=True, stop=True)
                        mm.then_inc(s("ir_psum"), 1)
                        e.wait_ge(s("latT_sb"), u + 1)
                        if u:
                            e.wait_ge(s("scaled"), u)
                        e.matmul(bank[4][0:NS, :], q_lat[0][:, b, :], latT[:, 0, :], start=True, stop=False)
                        e.matmul(bank[4][0:NS, :], q_lat[1][:, b, :], latT[:, 1, :], start=False, stop=False)
                        e.matmul(bank[4][0:NS, :], qrT[0:ROPE, b, :], latT[0:ROPE, 2, :], start=False, stop=True)\
                            .then_inc(s("sscore_psum"), 1)
                    if b:
                        e.wait_ge(s("snew_done"), b)
                    cs = cT[:, slot(PT)]
                    e.matmul(bank[5][0:NS, 0:NS], q_lat[0][:, b, :], cs[:, 0, 0:NS], start=True, stop=False)
                    e.matmul(bank[5][0:NS, 0:NS], q_lat[1][:, b, :], cs[:, 1, 0:NS], start=False, stop=False)
                    e.matmul(bank[5][0:NS, 0:NS], qrT[0:ROPE, b, :], krT[0:ROPE, :], start=False, stop=True)
                    e.matmul(bank[5][0:NS, NS:2 * NS], ikx[:NS, :], ident[:NS, :NS], start=True, stop=True).then_inc(s("snew_psum"), 1)
                    e.wait_ge(s("sexp_done"), b + 1)
                    for q in range(3):
                        v = 3 * b + q
                        if v:
                            e.wait_ge(s("spT_sb"), v)
                        for pg in range(8 * q, min(8 * q + 8, N_PAGES + 1)):
                            w = P if pg < N_PAGES else NS
                            mm = e.transpose(bank[6][:w, (pg % 8) * NS:(pg % 8 + 1) * NS], sc[:NS, pg * P:pg * P + w], ident[:NS, :NS])
                        mm.then_inc(s("spT_psum"), 1)
                    e.wait_ge(s("spT_sb"), 3 * b + 3)
                    if b:
                        e.wait_ge(s("olatT_sb"), b)
                    for pg in range(N_PAGES):
                        e.matmul(bank[7][0:NS, 0:KVR], pTs[:, pg, :], latb[:, pg, :], start=(pg == 0), stop=False)
                    e.matmul(bank[7][0:NS, 0:KVR], pTs[:NS, N_PAGES, :], c_rows[:NS, :], start=False, stop=True)\
                        .then_inc(s("olat_psum"), 1)
                    e.wait_ge(s("olat_sb"), b + 1)
                    for k in range(2):
                        mm = e.transpose(bank[7][:, 256 + k * NS:256 + (k + 1) * NS], olr[:NS, k * P:(k + 1) * P], ident[:NS, :NS])
                    mm.then_inc(s("olatT_psum"), 1)
                e.wait_ge(s("olatT_sb"), DEC_B)
                for h in range(H_MLA):
                    for k in range(2):
                        mm = e.matmul(bank[h // 4][:NS, (h % 4) * DV:(h % 4 + 1) * DV], oT[k][:, h, :],
                                      wuv_f[:, k, h * DV:(h + 1) * DV], start=(k == 0), stop=(k == 1))
                mm.then_inc(s("sprep_psum"), 1)

            def linear_attention(g):
                tiles = GROUPS[g]
                e.wait_ge(s("gla_w_loaded"), 48 * (g + 1) + 16 * g)
                for t in tiles:
                    R = ROWS[t]
                    lv0 = 0 if t < PT else SAMPLE_LEVEL0
                    e.wait_ge(s("gla_z_loaded"), 16 * (t + 1))
                    if t:
                        e.wait_ge(s("gla_read"), t)
                    e.transpose(bank[0][0:GATE_R, 0:R], gz[:R, GLA_COLS - GATE_R:GLA_COLS], ident[:R, :R]).then_inc(s("lrT_psum"), 1)
                    for h in range(H_GLA):
                        e.transpose(bank[1][:, h * P:h * P + R], gz[:R, h * GK:(h + 1) * GK], ident[:R, :R])
                    for h in range(H_GLA):
                        mm = e.transpose(bank[2][:, h * P:h * P + R], gz[:R, (H_GLA + h) * GK:(H_GLA + h + 1) * GK], ident[:R, :R])
                    mm.then_inc(s("gqkT_psum"), 1)
                    e.wait_ge(s("lrT_sb"), t + 1)
                    e.matmul(bank[3][:R, :], alT[0:GATE_R + 1, 0:R], w_ga[0:GATE_R + 1, :], start=True, stop=True)\
                        .then_inc(s("gate_pre"), 1)
                    e.wait_ge(s("gate_log"), t + 1)
                    for h in range(H_GLA):
                        mm = e.matmul(bank[4][:, h * P:h * P + R], gx[:R, h * GK:(h + 1) * GK],
                                      tri[:, :] if t < PT else tri_s[0:R, :], start=True, stop=True)
                    mm.then_inc(s("cum_psum"), 1)
                    e.wait_ge(s("levels_ready"), t + 1)
                    for h in range(H_GLA):
                        u = t * H_GLA + h
                        if h >= 2:
                            e.wait_ge(s("levels_masked"), u - 1)
                        for n in range(lv0, NLEV):
                            B = bank[2 * (h % 2) + (n - lv0) // 4]
                            dst = B[:R, ((n - lv0) % 4) * P:((n - lv0) % 4) * P + R]
                            l = Mlev[:, n, h * P:h * P + R] if n < NLEV - 1 else gkT[:, h * P:h * P + R]
                            r = l if n < NLEV - 1 else gqT[:, h * P:h * P + R]
                            mm = e.matmul(dst, l, r, start=True, stop=True)
                        mm.then_inc(s("level_products"), 1)
                    e.wait_ge(s("kdec_ready"), t + 1)
                    for h in range(H_GLA):
                        mm = e.transpose(bank[5][:R, h * GK:(h + 1) * GK], kd[:, h * P:h * P + R], ident[:, :])
                    mm.then_inc(s("kdr_psum"), 1)
                    e.wait_ge(s("kdr_sb"), t + 1)
                    for h in range(H_GLA):
                        u = t * H_GLA + h
                        e.wait_ge(s("AT_ready"), (t + 1) * H_GLA)
                        vg = gz[:R, 2 * H_GLA * GK + h * GV:2 * H_GLA * GK + (h + 1) * GV]
                        ob = bank[6 + h // 2][:R, (h % 2) * GV:(h % 2 + 1) * GV]
                        if t < PT:
                            e.matmul(ob, AT[:R, h, 0:R], vg, start=True, stop=(t == 0))
                            if t:
                                e.matmul(ob, qe[:, h * P:h * P + R], S0[:, h, :], start=False, stop=True)
                            if h >= 2:
                                e.wait_ge(s("gla_state"), u - 1)
                            e.matmul(bank[(h % 2) * 4][:, 0:GV], kdr[:R, h, :], vg, start=True, stop=True)\
                                .then_inc(s("gla_out_psum"), 1)
                        else:
                            e.wait_ge(s("qz_ready"), h + 1)
                            e.wait_ge(s(f"state_loaded{h % 2}"), 16 * (h // 2 + 1))
                            e.matmul(ob, AT[:R, h, 0:R], vg, start=True, stop=False)
                            for b in range(DEC_B):
                                mm = e.matmul(ob, qz[:, b, :], Ss[h % 2][:, b, :], start=False, stop=(b == DEC_B - 1))
                            mm.then_inc(s("gla_out_psum"), 1)
                            for b in range(DEC_B):
                                mm = e.matmul(bank[b // 2][:, (b % 2) * GV:(b % 2 + 1) * GV], kz[:R, b, :], vg,
                                              start=True, stop=True)
                            mm.then_inc(s("sample_state_psum"), 1)
                            e.wait_ge(s("sample_state_head"), h + 1)

            def queries(g):
                tiles = GROUPS[g]
                ntok = sum(ROWS[t] for t in tiles)
                landed = PASSES[f"query{g}"][0]
                e.wait_ge(s("nt_evacuated"), 4 * (NORMS["ffn", tiles[-1]] + 1))

                def query(n):
                    h, side = n // 2, n % 2
                    m = 2 * PH * g + n
                    w = W[h % 2].rearrange("p (k n) -> p k n", k=KD)
                    for half in range(2):
                        e.wait_ge(s(f"w_landed{h % 2}_{half}"), 16 * (landed + h // 2 + 1))
                    if n >= 2:
                        e.wait_ge(s("qT_evacuated"), m - 1)
                    for k in range(KD):
                        mm = e.matmul(bank[side][:, 0:ntok], w[:, k, side * P:(side + 1) * P], XT[:, k, 0:ntok],
                                      start=(k == 0), stop=(k == KD - 1))
                    mm.then_inc(s("tiles_projected"), 1)

                def key_scores(n):
                    side = n % 2
                    m = 2 * PH * g + n
                    e.wait_ge(s("qT_evacuated"), m + 1)
                    if n >= 2:
                        e.wait_ge(s("topk_done"), m - 1)
                    for sl, t in enumerate(tiles):
                        R = ROWS[t]
                        mm = e.matmul(bank[2 + side][:R, sl * P:(sl + 1) * P], qTm[:, side, sl * P:sl * P + R], keysT[:, side, :],
                                      start=True, stop=True)
                    mm.then_inc(s("key_scores"), 1)

                for n in range(2 * PH + 1):
                    if n < 2 * PH:
                        query(n)
                    if n:
                        key_scores(n - 1)

            e.wait_ge(s("consts_loaded"), 16 * 13)
            for side in range(2):
                mm = e.transpose(bank[0][:, side * P:(side + 1) * P], keysR[:, side, :], ident[:, :])
            mm.then_inc(s("keysT_psum"), 1)
            e.wait_ge(s("keysT_sb"), 1)
            for g, tiles in enumerate(GROUPS):
                norm_transposes("x", tiles)
                e.wait_ge(s("nt_evacuated"), 4 * (NORMS["x", tiles[-1]] + 1))
                if g:
                    e.wait_ge(s("topk_done"), 2 * PH * g)
                    e.wait_ge(s("qT_evacuated"), 2 * PH * g)
                project(f"in{g}", tiles, IN_NC, IN_BLOCKS, "z_read", IN_READ[f"in{g}"])
                e.wait_ge(s("z_read"), IN_READ[f"in{g}"] + IN_BLOCKS * len(tiles))
                latent_attention(g)
                if PT in tiles:
                    sample_attention()
                linear_attention(g)
                norm_transposes("mix", tiles)
                e.wait_ge(s("nt_evacuated"), 4 * (NORMS["mix", tiles[-1]] + 1))
                e.wait_ge(s("gla_o_sb"), tiles[-1] + 1)
                project(f"out{g}", tiles, NC, NBLK, "rows_added", ADDED[f"out{g}"])
                norm_transposes("ffn", tiles)
                queries(g)
            for pg, tiles in enumerate(PLE_GROUPS):
                if pg == 0:
                    e.wait_ge(s("topk_done"), 2 * PH * len(GROUPS))
                norm_transposes("ple", tiles)
                e.wait_ge(s("p_loaded"), 16 * (tiles[-1] + 1))
                for t in tiles:
                    R = ROWS[t]
                    if t:
                        e.wait_ge(s("pT_ple_sb"), t)
                    for k in range(2):
                        mm = e.transpose(bank[5][:, k * P:k * P + R], p_row[:R, t % 2, k * P:(k + 1) * P], ident[:R, :R])
                    mm.then_inc(s("pT_ple_psum"), 1)
                e.wait_ge(s("pT_ple_sb"), tiles[-1] + 1)
                e.wait_ge(s("nt_evacuated"), 4 * (NORMS["ple", tiles[-1]] + 1))
                project(f"gate{pg}", tiles, NC, NBLK, "rows_added", ADDED[f"gate{pg}"], embed=True)

        @block.vector
        def _(e):
            own = [0]

            def mark(ins):
                own[0] += 1
                ins.then_inc(s("dve_own"), 1)

            def link(ins):
                mark(ins)
                e.wait_ge(s("dve_own"), own[0])

            def norm_rows(use, tiles):
                for t in tiles:
                    R = ROWS[t]
                    n = NORMS[use, t]
                    sl = slot(t) if use != "ple" else t % 2
                    width = H_MLA * DV if use == "mix" else D
                    inv = st[:R, 2 * ns + n:2 * ns + n + 1]
                    e.wait_ge(s("rms_ready"), n + 1)
                    link(e.reciprocal(inv, st[:R, ns + n:ns + n + 1]))
                    if t == tiles[0]:
                        e.wait_ge(s("gain_loaded"), 16 * (GAINS.index((use, tiles[0])) + 1))
                    e.scalar_tensor_tensor(out=Y[:R, 0:width], in0=H[:R, sl, 0:width], scalar=inv, in1=G[:R, 0:width],
                                           op0=ALU.mult, op1=ALU.mult).then_inc(s("normed"), 1)
                    yield NORM_PACE

            def rotate(t, out, x, n):
                R = ROWS[t]
                cs, sn = cosT[:R, t, :], sinT[:R, t, :]
                hf = ROPE // 2
                if n > 1:
                    cb = cs.unsqueeze(1).to_broadcast([R, n, ROPE])
                    s0 = sn[:, 0:hf].unsqueeze(1).to_broadcast([R, n, hf])
                    s1 = sn[:, hf:ROPE].unsqueeze(1).to_broadcast([R, n, hf])
                    tmp = rtmp[:R]
                    xa, xb, ta, tb = x[:, :, hf:ROPE], x[:, :, 0:hf], tmp[:, :, 0:hf], tmp[:, :, hf:ROPE]
                else:
                    cb, s0, s1 = cs, sn[:, 0:hf], sn[:, hf:ROPE]
                    tmp = rtmp[:R, 0, :]
                    xa, xb, ta, tb = x[:, hf:ROPE], x[:, 0:hf], tmp[:, 0:hf], tmp[:, hf:ROPE]
                e.tensor_tensor(ta, xa, s0, ALU.mult)
                e.tensor_tensor(tb, xb, s1, ALU.mult)
                link(e.tensor_tensor(out, x, cb, ALU.mult))
                return e.tensor_tensor(out, out, tmp, ALU.add)

            def mixer(g):
                tiles = GROUPS[g]
                nt = len(tiles)
                yield LEAD
                yield from norm_rows("x", tiles)
                yield SEGMENT
                for seg in range(IN_BLOCKS // 2 if g else 1):
                    yield IN_PACE * nt
                    yield SEGMENT
                e.wait_ge(s("mla_gains_loaded"), 64 * (g + 1))
                for t in tiles:
                    R = ROWS[t]
                    e.wait_ge(s("lat_rms"), t + 1)
                    mark(e.reciprocal(IQ[:R], RQ[:R]))
                    link(e.reciprocal(IC[:R], RC[:R]))
                    e.scalar_tensor_tensor(out=cqn[:R, :], in0=m_z[:R, 0:QR], scalar=IQ[:R], in1=g_q[:R, :], op0=ALU.mult, op1=ALU.mult)
                    if t:
                        e.wait_ge(s("lat_stored"), 16 * t)
                    e.scalar_tensor_tensor(out=c_rows[:R, :], in0=m_z[:R, QR:QR + KVR], scalar=IC[:R], in1=g_kv[:R, :],
                                           op0=ALU.mult, op1=ALU.mult).then_inc(s("mla_latents_normed"), 1)
                    yield STEP
                    link(e.tensor_tensor(kr_g[:R, :], m_z[:R, QR + KVR:MLA_COLS], g_k[:R, NOPE:QK], ALU.mult))
                    rotate(t, kr_o[:R, slot(t), :], kr_g[:R, :], 1).then_inc(s("rope_key_ready"), 1)
                    e.wait_ge(s("rope_key_ready"), t + 1)
                    e.wait_ge(s("lat_transposed"), t + 1)
                    yield STEP
                yield SEGMENT
                for hh in range(2):
                    for t in tiles:
                        R = ROWS[t]
                        n = HALVES[hh, t]
                        e.wait_ge(s("squares_ready"), 2 * n + 1)
                        e.tensor_reduce(SQH[:R], sqs[:R, :].rearrange("p (h n) -> p h n", h=HH), AX, ALU.add).then_inc(s("ssq_done"), 1)
                        yield STEP
                        e.wait_ge(s("q_rms"), n + 1)
                        link(e.reciprocal(IQH[:R], RQH[:R]))
                        for j in range(2):
                            ins = e.tensor_tensor(qrow[:R, 2 * j:2 * j + 2, :], bank[j][:R, 0:2 * QK].rearrange("p (h n) -> p h n", h=2),
                                                  IQH[:R, 2 * j:2 * j + 2].unsqueeze(2).to_broadcast([R, 2, QK]), ALU.mult)
                        link(ins)
                        yield HALF_STEP
                        link(e.tensor_tensor(qrow[:R], qrow[:R], g_qk[:R, :].unsqueeze(1).to_broadcast([R, HH, QK]), ALU.mult))
                        yield HALF_STEP
                        link(rotate(t, qro[:R], qrow[:R, :, NOPE:QK], HH))
                        if t == PT:
                            link(e.tensor_tensor(qrow[:R, :, 0:NOPE], qrow[:R, :, 0:NOPE],
                                                 g_k[:R, 0:NOPE].unsqueeze(1).to_broadcast([R, HH, NOPE]), ALU.mult))
                        e.sem_inc(s("q_rows_ready"), 1)
                        yield STEP
                        e.wait_ge(s("squares_ready"), 2 * n + 2)
                        link(e.tensor_reduce(SKH[:R], sqs[:R, 0:512].rearrange("p (h n) -> p h n", h=HH), AX, ALU.add))
                        e.tensor_scalar(SKH[:R], SKH[:R], SKR(t)[:R], None, ALU.add).then_inc(s("ssq_done"), 1)
                        yield STEP
                        e.wait_ge(s("k_rms"), n + 1)
                        ik = IKH(t)[:R, hh * HH:(hh + 1) * HH]
                        e.reciprocal(ik, RKH[:R]).then_inc(s("ikh_ready"), 1)
                        e.wait_ge(s("ikh_ready"), n + 1)
                        if t == PT:
                            e.sem_inc(s("k_rows_ready"), 1)
                            e.wait_ge(s("sample_qT_psum"), hh + 1)
                            e.tensor_copy(qgT[:, hh * HH:(hh + 1) * HH, :], bank[4][:, 0:HH * NS].rearrange("p (h n) -> p h n", h=HH))
                            e.tensor_copy(by_batch(qrT[0:ROPE], hh * HH, HH),
                                          bank[5][0:ROPE, 0:HH * NS].rearrange("p (h b t) -> p h b t", h=HH, b=DEC_B))\
                                .then_inc(s("sample_qT_sb"), 1)
                            yield SEGMENT
                            continue
                        link(e.tensor_tensor(krow[:, :, :], bank[2][:, :].rearrange("p (h n) -> p h n", h=HH),
                                             ik.unsqueeze(2).to_broadcast([P, HH, NOPE]), ALU.mult))
                        yield HALF_STEP
                        link(e.tensor_tensor(krow[:, :, :], krow[:, :, :], g_k[:, 0:NOPE].unsqueeze(1).to_broadcast([P, HH, NOPE]), ALU.mult))
                        e.tensor_tensor(kro[:, :, :], kr_o[:, slot(t), :].unsqueeze(1).to_broadcast([P, HH, ROPE]),
                                        ik.unsqueeze(2).to_broadcast([P, HH, ROPE]), ALU.mult).then_inc(s("k_rows_ready"), 1)
                        yield STEP
                        m = PHALVES[hh, t]
                        e.wait_ge(s("kT_psum"), m + 1)
                        if m:
                            e.wait_ge(s("pv_done"), HH * m)
                        if g < LAST and hh and t == tiles[0]:
                            e.wait_ge(s("keys_parked"), 48 * (2 * g + 1))
                        e.tensor_copy(KTn[:, :, t * P:(t + 1) * P], four(bank[6]))
                        e.tensor_copy(KTr[:, :, t * P:(t + 1) * P], four(bank[7])[:, 0:2]).then_inc(s("kT_sb"), 1)
                        yield STEP
                        for h in range(HH):
                            u = m * HH + h
                            e.wait_ge(s("scores_ready"), u + 1)
                            link(e.tensor_reduce(MXV[:, h:h + 1], bank[h % 2][:, 0:(t + 1) * P], AX, ALU.max))
                            e.tensor_scalar(NMX[:, h:h + 1], MXV[:, h:h + 1], -SCALE, None, ALU.mult).then_inc(s("neg_max"), 1)
                            yield HEAD_PACE
                        e.wait_ge(s("exp_done"), (m + 1) * HH)
                        link(e.reciprocal(RINV[:, :], RSUM[:, :]))
                        e.wait_ge(s("pv_done"), (m + 1) * HH)
                        if m:
                            e.wait_ge(s("o_stored"), 16 * m)
                        e.tensor_tensor(orow.rearrange("p (h n) -> p h n", h=HH), bank[4][:, :].rearrange("p (h n) -> p h n", h=HH),
                                        RINV[:, :].unsqueeze(2).to_broadcast([P, HH, DV]), ALU.mult).then_inc(s("mla_o_rows"), 1)
                        yield HALF_PACE
                        yield SEGMENT
                if PT in tiles:
                    yield from sample()
                e.wait_ge(s("o_stored"), O_STORED[g])
                e.wait_ge(s("gla_w_loaded"), 48 * (g + 1) + 16 * g)
                mark(e.memset(alT[0:GATE_R + 1, :], 1.0))
                link(e.memset(qz, 0.0))
                e.sem_inc(s("gla_fills"), 1)
                for t in tiles:
                    yield from gla(t)
                yield from norm_rows("mix", tiles)
                yield SEGMENT
                yield LEAD
                e.wait_ge(s("rows_loaded"), 16 * 3 * (tiles[0] + nt))
                for i in pairs(e, 0, NBLK // 2, g == 0):
                    for p in range(2):
                        for sl, t in enumerate(tiles):
                            R = ROWS[t]
                            u = (i * 2 + p) * nt + sl
                            hs = H[:R, sl, bass.ds((i * 2 + p) * NC, NC)]
                            e.wait_ge(s("tiles_projected"), u + (PASSES[f"out{g}"][1] + 1))
                            e.tensor_tensor(hs, hs, out_bank(p, sl)[:R, 0:NC], ALU.add).then_inc(s("rows_added"), 1)
                            if g:
                                yield OUT_PACE
                    if g and i == NBLK // 4 - 1:
                        yield SEGMENT
                yield LEAD
                yield from norm_rows("ffn", tiles)
                e.wait_ge(s("xn_stored"), 16 * (tiles[-1] + 1))
                e.wait_ge(s("h_stored"), 16 * (tiles[-1] + 1))
                yield SEGMENT
                yield 2 * LEAD
                yield from best_keys(g, 0, 2)

            def best_keys(g, lo, hi):
                tiles = GROUPS[g]
                nt = len(tiles)
                for n in range(2 * lo, 2 * hi):
                    side = n % 2
                    m = 2 * PH * g + n
                    e.wait_ge(s("key_scores"), m + 1)

                    def sco(sl):
                        return bank[2 + side][:ROWS[tiles[sl]], sl * P:(sl + 1) * P]

                    def top(sl):
                        return topv[:ROWS[tiles[sl]], sl, n, :]

                    for sl in range(nt):
                        ins = e.max(top(sl)[:, 0:8], sco(sl))
                    link(ins)
                    yield KEY_PACE * nt
                    for sl in range(nt):
                        R = ROWS[tiles[sl]]
                        e.max_index(topu[:R, sl, 0:8], top(sl)[:, 0:8], sco(sl))
                        ins = e.match_replace(out=swork[:R, sl, :], in_to_replace=top(sl)[:, 0:8], in_values=sco(sl), imm_value=LOWEST)
                    link(ins)
                    yield KEY_PACE * nt
                    for sl in range(nt):
                        ins = e.max(top(sl)[:, 8:16], swork[:ROWS[tiles[sl]], sl, :])
                    link(ins)
                    for sl in range(nt):
                        R = ROWS[tiles[sl]]
                        ins = e.max_index(topu[:R, sl, 8:16], top(sl)[:, 8:16], swork[:R, sl, :])
                    link(ins)
                    full = sum(1 for t in tiles if t < PT)
                    ins = e.tensor_copy(topi[:, 0:full, n, :], topu[:, 0:full, :])
                    if PT in tiles:
                        ins = e.tensor_copy(topi[:NS, full, n, :], topu[:NS, full, :])
                    ins.then_inc(s("topk_done"), 1)
                    e.wait_ge(s("topk_done"), m + 1)
                    yield KEY_PACE * nt
                    if n % 4 == 3:
                        yield SEGMENT

            def sample():
                yield PREP_PACE
                yield SEGMENT
                for b in range(DEC_B):
                    for g in range(4):
                        u = 4 * b + g
                        e.wait_ge(s("sscore_psum"), u + 1)
                        e.wait_ge(s("ir_sb"), u + 1)
                        if b and g == 0:
                            e.wait_ge(s("spT_psum"), 3 * b)
                        e.tensor_tensor(sc[:NS, g * 512:(g + 1) * 512], bank[4][:NS, :], irs[:NS, :], ALU.mult).then_inc(s("scaled"), 1)
                        yield PAGES_PACE
                    e.wait_ge(s("snew_psum"), b + 1)
                    link(e.tensor_copy(sc[:NS, PAST:PAST + NS], bank[5][:NS, NS:2 * NS]))
                    link(e.tensor_tensor(sc[:NS, PAST:PAST + NS], sc[:NS, PAST:PAST + NS], bank[5][:NS, 0:NS], ALU.mult))
                    e.tensor_tensor(sc[:NS, PAST:PAST + NS], sc[:NS, PAST:PAST + NS], smask[:NS, b, :], ALU.add).then_inc(s("snew_done"), 1)
                    e.wait_ge(s("snew_done"), b + 1)
                    e.wait_ge(s("scaled"), 4 * b + 4)
                    link(e.tensor_reduce(MXV[:NS, 0:1], sc[:NS, :], AX, ALU.max))
                    e.tensor_scalar(NMX[:NS, 0:1], MXV[:NS, 0:1], -SCALE, None, ALU.mult).then_inc(s("sneg_max"), 1)
                    yield SOFTMAX_PACE
                    e.wait_ge(s("sexp_done"), b + 1)
                    link(e.reciprocal(RINV[:NS, 0:1], RSUM[:NS, 0:1]))
                    e.wait_ge(s("olat_psum"), b + 1)
                    e.tensor_scalar(olr[:NS, :], bank[7][:NS, 0:KVR], RINV[:NS, 0:1], None, ALU.mult).then_inc(s("olat_sb"), 1)
                    yield STEP
                    if b < DEC_B - 1:
                        yield SEGMENT
                e.wait_ge(s("sprep_psum"), 7)
                for n in range(2):
                    ins = e.tensor_copy(so_rows[:NS, n * 512:(n + 1) * 512], bank[n][:NS, :])
                ins.then_inc(s("sample_o_rows"), 1)
                yield SEGMENT

            def gla(t):
                R = ROWS[t]
                lv0 = 0 if t < PT else SAMPLE_LEVEL0
                yield LEAD
                e.wait_ge(s("gate_ln"), t + 1)
                link(e.tensor_scalar(gt2[:R, :], bank[3][:R, :], 0.0, 1.0 / TAU, ALU.min, ALU.mult))
                e.scalar_tensor_tensor(out=gx[:R, :], in0=gt1[:R, :], scalar=-1.0 / TAU, in1=gt2[:R, :],
                                       op0=ALU.mult, op1=ALU.add).then_inc(s("gate_log"), 1)
                yield STEP
                e.wait_ge(s("cum_psum"), t + 1)
                e.tensor_copy(heads(gbT, R), heads(bank[4], R)).then_inc(s("cum_sb"), 1)
                e.wait_ge(s("cum_sb"), t + 1)
                e.wait_ge(s("gqkT_sb"), t + 1)
                if slot(t):
                    e.wait_ge(s("gla_out_psum"), t * H_GLA)
                yield STEP

                def halves(ap, n):
                    hf = LEVELS[n]
                    if R == P:
                        v = ap[:, 0:H_GLA * P].rearrange("p (g a b) -> p g a b", a=2, b=hf)
                        return v[:, :, 0, :], v[:, :, 1, :]
                    v = heads(ap, R).rearrange("p h (g a b) -> p h g a b", a=2, b=hf)
                    return v[:, :, :, 0, :], v[:, :, :, 1, :]

                def multiply(n):
                    v = level_count(t, n)
                    e.wait_ge(s("level_exp"), v + 1)
                    d0, d1 = halves(dlev[:, n % 2, :], n)
                    m0, m1 = halves(Mlev[:, n, :], n)
                    k0, _ = halves(gkT, n)
                    _, q1 = halves(gqT, n)
                    e.tensor_tensor(m0, d0, k0, ALU.mult)
                    e.tensor_tensor(m1, d1, q1, ALU.mult).then_inc(s("level_done"), 1)

                for n in range(lv0, NLEV - 1):
                    hf = LEVELS[n]
                    v = level_count(t, n)
                    if v >= 2:
                        e.wait_ge(s("level_done"), v - 1)
                    b0, b1 = halves(gbT, n)
                    d0, d1 = halves(dlev[:, n % 2, :], n)
                    rb = b0[..., hf - 1:hf].to_broadcast(list(b0.shape))
                    e.tensor_tensor(d0, rb, b0, ALU.subtract)
                    e.tensor_tensor(d1, b1, rb, ALU.subtract).then_inc(s("level_diff"), 1)
                    if n > lv0:
                        multiply(n - 1)
                    yield STEP
                multiply(NLEV - 2)
                e.wait_ge(s("level_done"), level_count(t, NLEV - 2) + 1)
                e.sem_inc(s("levels_ready"), 1)
                seg = P if t < PT else DEC_T
                gseg = heads(gbT, R).rearrange("p h (g n) -> p h g n", n=seg)
                kseg = heads(kd, R).rearrange("p h (g n) -> p h g n", n=seg)
                last = gseg[:, :, :, seg - 1:seg]
                e.tensor_tensor(kseg, last.to_broadcast(list(gseg.shape)), gseg, ALU.subtract).then_inc(s("kdiff"), 1)
                e.wait_ge(s("eb_ready"), t + 1)
                e.tensor_tensor(heads(qe, R), heads(gqT, R), heads(eb, R), ALU.mult)
                ebs = heads(eb, R).rearrange("p h (g n) -> p h g n", n=seg)[:, :, :, seg - 1]
                nseg = R // seg
                link(e.tensor_copy(eL[:, 0:H_GLA * nseg].rearrange("p (h g) -> p h g", h=H_GLA), ebs))
                yield STEP
                e.wait_ge(s("kexp"), t + 1)
                e.tensor_tensor(heads(kd, R), heads(kd, R), heads(gkT, R), ALU.mult).then_inc(s("kdec_ready"), 1)
                yield SEGMENT
                nl = NLEV - lv0
                for h in range(H_GLA):
                    u = t * H_GLA + h
                    e.wait_ge(s("level_products"), u + 1)
                    for half in range((nl + 3) // 4):
                        n4 = min(4, nl - 4 * half)
                        ins = e.tensor_tensor(am[:R, 4 * half:4 * half + n4, 0:R],
                                              bank[2 * (h % 2) + half][:R, :].rearrange("p (l n) -> p l n", n=P)[:, 0:n4, 0:R],
                                              lev[:R, lv0 + 4 * half:lv0 + 4 * half + n4, 0:R], ALU.mult)
                    ins.then_inc(s("levels_masked"), 1)
                    e.wait_ge(s("levels_masked"), u + 1)
                    link(e.tensor_reduce(AT[:R, h, 0:R], am[:R, 0:nl, 0:R].rearrange("p l n -> p n l"), AX, ALU.add))
                    e.sem_inc(s("AT_ready"), 1)
                    yield STEP
                for h in range(H_GLA):
                    u = t * H_GLA + h
                    if t < PT:
                        e.wait_ge(s("gla_out_psum"), u + 1)
                        upd = bank[(h % 2) * 4][:, 0:GV]
                        if t:
                            e.scalar_tensor_tensor(out=S0[:, h, :], in0=S0[:, h, :], scalar=eL[:, h:h + 1], in1=upd,
                                                   op0=ALU.mult, op1=ALU.add).then_inc(s("gla_state"), 1)
                        else:
                            e.tensor_copy(S0[:, h, :], upd).then_inc(s("gla_state"), 1)
                    else:
                        if h:
                            e.wait_ge(s("sample_state_psum"), h)
                            sample_state(h - 1)
                            yield STEP
                        for b in range(DEC_B):
                            ins = e.tensor_copy(qz[:, b, b * DEC_T:(b + 1) * DEC_T], qe[:, h * P + b * DEC_T:h * P + (b + 1) * DEC_T])
                        e.wait_ge(s("kdr_sb"), T)
                        e.tensor_tensor(kz[:R, :, :], kdr[:R, h, :].unsqueeze(1).to_broadcast([R, DEC_B, GK]),
                                        bmask[:R, :].unsqueeze(2).to_broadcast([R, DEC_B, GK]), ALU.mult).then_inc(s("qz_ready"), 1)
                    yield STEP
                if t == PT:
                    e.wait_ge(s("sample_state_psum"), H_GLA)
                    sample_state(H_GLA - 1)
                e.wait_ge(s("gla_out_psum"), (t + 1) * H_GLA)
                if t:
                    e.wait_ge(s("go_stored"), 16 * t)
                e.tensor_copy(go[:R, 0:512], bank[6][:R, :])
                e.tensor_copy(go[:R, 512:1024], bank[7][:R, :]).then_inc(s("gla_o_sb"), 1)
                yield STEP
                e.wait_ge(s("gla_rms"), t + 1)
                link(e.reciprocal(GIS[:R], GRS[:R]))
                gv = go[:R, :].rearrange("p (h n) -> p h n", h=H_GLA)
                link(e.tensor_tensor(gv, gv, GIS[:R].unsqueeze(2).to_broadcast([R, H_GLA, GV]), ALU.mult))
                link(e.tensor_tensor(gv, gv, g_go[:R, :].unsqueeze(1).to_broadcast([R, H_GLA, GV]), ALU.mult))
                e.tensor_tensor(go[:R, :], go[:R, :], gsil[:R, :], ALU.mult).then_inc(s("gla_o_ready"), 1)
                yield SEGMENT

            def sample_state(h):
                for b in range(DEC_B):
                    upd = bank[b // 2][:, (b % 2) * GV:(b % 2 + 1) * GV]
                    st_ = Ss[h % 2][:, b, :]
                    ins = e.scalar_tensor_tensor(out=st_, in0=st_, scalar=eL[:, h * DEC_B + b:h * DEC_B + b + 1], in1=upd,
                                                 op0=ALU.mult, op1=ALU.add)
                ins.then_inc(s("sample_state_head"), 1)

            def route(t, lo, hi):
                nh = hi - lo
                nk = nh * TOPK
                pace = (LATE_PACE if t == PT else ROUTE_PACE) if nh == PH else HALF_STEP
                R = ROWS[t]
                sl = slot(t)
                tv = topv[:R, sl, 2 * lo:2 * hi, :].rearrange("p (h w) k -> p h w k", w=2)
                ti = topi[:R, sl, 2 * lo:2 * hi, :].rearrange("p (h w) k -> p h w k", w=2)
                cv = cand[:R, 0:nk * TOPK].rearrange("p (h i j) -> p h i j", h=nh, i=TOPK)
                link(e.tensor_tensor(cv, tv[:, :, 0, :].unsqueeze(3).to_broadcast([R, nh, TOPK, TOPK]),
                                     tv[:, :, 1, :].unsqueeze(2).to_broadcast([R, nh, TOPK, TOPK]), ALU.add))
                yield pace
                gv = gtop
                for h in range(nh):
                    ins = e.max(gv[:R, h * 16:h * 16 + 8], cand[:R, h * 256:(h + 1) * 256])
                link(ins)
                yield pace
                for h in range(nh):
                    e.max_index(sela[:R, h * 16:h * 16 + 8], gv[:R, h * 16:h * 16 + 8], cand[:R, h * 256:(h + 1) * 256])
                    ins = e.match_replace(out=candw[:R, h * 256:(h + 1) * 256], in_to_replace=gv[:R, h * 16:h * 16 + 8],
                                          in_values=cand[:R, h * 256:(h + 1) * 256], imm_value=LOWEST)
                    if h % 4 == 3 or h == nh - 1:
                        link(ins)
                        yield pace
                for h in range(nh):
                    ins = e.max(gv[:R, h * 16 + 8:h * 16 + 16], candw[:R, h * 256:(h + 1) * 256])
                link(ins)
                yield pace
                for h in range(nh):
                    ins = e.max_index(sela[:R, h * 16 + 8:h * 16 + 16], gv[:R, h * 16 + 8:h * 16 + 16], candw[:R, h * 256:(h + 1) * 256])
                link(ins)
                yield pace
                link(e.tensor_copy(e1[:R, 0:nh], gv[:R, 0:nk].rearrange("p (h k) -> p h k", h=nh)[:, :, 0]))
                g3 = gv[:R, 0:nk].rearrange("p (h k) -> p h k", h=nh)
                e.tensor_tensor(g3, g3, e1[:R, 0:nh].unsqueeze(2).to_broadcast([R, nh, TOPK]), ALU.subtract).then_inc(s("gate_diff"), 1)
                mark(e.tensor_single_scalar(selh[:R, 0:nk], sela[:R, 0:nk], 4, ALU.logical_shift_right))
                link(e.tensor_single_scalar(sell[:R, 0:nk], sela[:R, 0:nk], 15, ALU.bitwise_and))
                mark(e.tensor_copy(selhf[:R, 0:nk], selh[:R, 0:nk]))
                link(e.tensor_copy(sellf[:R, 0:nk], sell[:R, 0:nk]))
                yield pace
                for sel, w, out in ((selhf, 0, e1), (sellf, 1, e2)):
                    oh = oneh[:R, 0:nk * TOPK].rearrange("p (h i j) -> p h i j", h=nh, i=TOPK)
                    o3 = oneh[:R, 0:nk * TOPK].rearrange("p (n j) -> p n j", j=TOPK)
                    link(e.tensor_tensor(o3, sel[:R, 0:nk].unsqueeze(2).to_broadcast([R, nk, TOPK]),
                                         iota16[:R, :].unsqueeze(1).to_broadcast([R, nk, TOPK]), ALU.is_equal))
                    yield pace
                    link(e.tensor_tensor(oh, oh, ti[:, :, w, :].unsqueeze(2).to_broadcast([R, nh, TOPK, TOPK]), ALU.mult))
                    yield pace
                    link(e.tensor_reduce(out[:R, 0:nk], o3, AX, ALU.add))
                    yield pace
                link(e.scalar_tensor_tensor(out=e1[:R, 0:nk], in0=e1[:R, 0:nk], scalar=float(NKEY), in1=e2[:R, 0:nk], op0=ALU.mult, op1=ALU.add))
                e.wait_ge(s("gate_exp"), ROUTES.index((t, lo, hi)) + 1)
                link(e.tensor_reduce(gsum[:R, 0:nh], g3, AX, ALU.add))
                link(e.reciprocal(gsum[:R, 0:nh], gsum[:R, 0:nh]))
                u0 = (FIRST_UNITS[t] + lo) * TOPK
                if t < PT:
                    mark(e.tensor_copy(idx_all[:, u0:u0 + nk], e1[:, 0:nk]))
                    link(e.tensor_tensor(gate_all[:, u0:u0 + nk].rearrange("p (h k) -> p h k", h=nh), g3,
                                         gsum[:, 0:nh].unsqueeze(2).to_broadcast([P, nh, TOPK]), ALU.mult))
                else:
                    hf = PH // 2
                    mark(e.tensor_copy(idx_all[:R, u0:u0 + 64], e1[:R, 0:64]))
                    mark(e.tensor_copy(ixs_hi, e1[:R, 64:128]))
                    mark(e.tensor_tensor(gate_all[:R, u0:u0 + 64].rearrange("p (h k) -> p h k", h=hf), g3[:, 0:hf],
                                         gsum[:R, 0:hf].unsqueeze(2).to_broadcast([R, hf, TOPK]), ALU.mult))
                    link(e.tensor_tensor(gts_hi.rearrange("p (h k) -> p h k", h=hf), g3[:, hf:PH],
                                         gsum[:R, hf:PH].unsqueeze(2).to_broadcast([R, hf, TOPK]), ALU.mult))
                e.sem_inc(s("route_ready"), 1)
                routed[t] = hi
                yield SEGMENT

            def embedding(pg):
                tiles = PLE_GROUPS[pg]
                nt = len(tiles)
                yield 2 * LEAD
                yield from norm_rows("ple", tiles)
                yield LEAD
                yield SEGMENT
                for i in pairs(e, 0, NBLK // 2, pg == 2):
                    for p in range(2):
                        for sl, t in enumerate(tiles):
                            R = ROWS[t]
                            u = (i * 2 + p) * nt + sl
                            x = (p * nt + sl) % 2
                            e.wait_ge(s("sigmoid_ready"), u + (EMBEDDED[pg] + 1))
                            e.tensor_tensor(sg[:R, x, :], sg[:R, x, :], bank[6 + x][:R, 0:NC], ALU.mult).then_inc(s("embed_read"), 1)
                            e.wait_ge(s("embed_read"), u + (EMBEDDED[pg] + 3))
                            hs = H[:R, sl, bass.ds((i * 2 + p) * NC, NC)]
                            e.tensor_tensor(hs, hs, sg[:R, x, :], ALU.add).then_inc(s("rows_added"), 1)
                            if pg < 2:
                                yield EMBED_PACE
                    if pg < 2:
                        yield SEGMENT

            def other_heads(g):
                for h in range(2, PH, 2):
                    yield from best_keys(g, h, h + 2)
                    yield from route(GROUPS[g][0], h, h + 2)

            def woven():
                yield from other_heads(0)
                for g in range(1, len(GROUPS)):
                    first = GROUPS[g][0]
                    yield from mixer(g)
                    yield from route(first, 0, 2)
                    yield from other_heads(g)
                    for t in GROUPS[g][1:]:
                        yield from route(t, 0, PH)
                for pg in range(2):
                    yield -(FIRST_UNITS[PLE_GROUPS[pg][-1] + 1] + 1)
                    yield from embedding(pg)


            e.memset(eps[:, :], EPS).then_inc(s("fills_ready"), 1)
            e.sem_inc(s("rows_added"), 4)
            e.sem_inc(s("embed_read"), 2)
            e.wait_ge(s("consts_loaded"), 16 * 13)
            routed = {}
            for x in mixer(0):
                pass
            for x in route(0, 0, 2):
                pass

            e.sem_inc(s("buffers_free"), RING)
            e.sem_inc(s("summed"), 1)
            weave = woven()
            state = {"credit": 0, "hold": 0, "segments": 0, "inside": False}

            def step():
                pace = next(weave, -UNITS - 1)
                state["inside"] = pace > 0
                if pace == SEGMENT:
                    state["segments"] += 1
                elif pace > 0:
                    state["credit"] -= pace
                else:
                    state["hold"] = -pace

            def steps(u):
                if u >= state["hold"]:
                    state["credit"] += 1
                while state["credit"] > 0 and u >= state["hold"]:
                    step()

            def dot_products(u, xb):
                segments_before.append(state["segments"])
                for k in range(TOPK):
                    b, n = k % RING, first_slot(u, 0) + k
                    e.wait_ge(s(f"rows_landed{b}"), 16 * (n // RING + 1))
                    e.tensor_tensor_reduce(out=ring[:, b, :], in0=ring[:, b, :], in1=xrow[:, xb, :], scale=1.0, scalar=0.0,
                                           op0=ALU.mult, op1=ALU.add, accum_out=dots[:, u % 2, k:k + 1]).then_inc(s("dots_done"), 1)
                    e.wait_ge(s("dots_done"), u * TOPK + k + 1)
                    e.sem_inc(s("buffers_free"), 1)
                    steps(u)
                segments_after.append(state["segments"] + state["inside"])

            def weighted_sum(u):
                while state["segments"] < segments_after[u]:
                    step()
                e.wait_ge(s("gelu_ready"), u + 1)
                link(e.tensor_tensor(coef[:, :], gel[:, u % 2, :], gate_all[:, u * TOPK:(u + 1) * TOPK], ALU.mult))
                for k in range(TOPK):
                    b, n = k % RING, first_slot(u, 1) + k
                    e.wait_ge(s(f"rows_landed{b}"), 16 * (n // RING + 1))
                    e.wait_ge(s("summed"), u * TOPK + max(k, 1))
                    if u in FIRST_UNITS and k < 2:
                        e.tensor_scalar(acc[:, k, :], ring[:, b, :], coef[:, k:k + 1], None, ALU.mult).then_inc(s("summed"), 1)
                    else:
                        e.scalar_tensor_tensor(out=acc[:, k % 2, :], in0=ring[:, b, :], scalar=coef[:, k:k + 1], in1=acc[:, k % 2, :],
                                               op0=ALU.mult, op1=ALU.add).then_inc(s("summed"), 1)
                    e.wait_ge(s("summed"), u * TOPK + k + 2)
                    e.sem_inc(s("buffers_free"), 1)
                    steps(u)

            def prompt_rows_done(t):
                xr = xrow[:, t % 2, :]
                e.wait_ge(s("h_loaded"), 16 * (t + 1))
                segments_summed.append(state["segments"] + state["inside"])
                link(e.tensor_tensor(xr, xr, acc[:, 0, :], ALU.add))
                e.tensor_tensor(xr, xr, acc[:, 1, :], ALU.add).then_inc(s("peer_done"), 1)

            for t in range(T):
                for u in range(FIRST_UNITS[t], FIRST_UNITS[t + 1]):
                    while routed.get(t, 0) <= u - FIRST_UNITS[t]:
                        step()
                    if u == FIRST_UNITS[t]:
                        e.wait_ge(s(f"xrow_loaded{t % 2}"), 16 * (t // 2 + 1 if t < PT else T - 1))
                        if t == PT:
                            e.wait_ge(s("sample_spread"), 32)
                    dot_products(u, t % 2)
                    if u:
                        weighted_sum(u - 1)
                    if u and u == FIRST_UNITS[t]:
                        prompt_rows_done(t - 1)
            weighted_sum(UNITS - 1)
            for x in weave:
                pass
            link(e.tensor_tensor(acc[:, 0, :], acc[:, 0, :], acc[:, 1, :], ALU.add))
            e.sem_inc(s("sample_halves"), 1)
            e.wait_ge(s("h_loaded"), 16 * T)
            e.wait_ge(s("sample_back"), 16)
            e.wait_ge(s("y_out"), 16 * PT)
            link(e.tensor_tensor(acc[0:NS, 0, :], acc[0:NS, 0, :], acc[0:NS, 1, :], ALU.add))
            e.tensor_tensor(H[:NS, 0, :], xrow[:NS, PT % 2, :], acc[0:NS, 0, :], ALU.add).then_inc(s("peer_done"), 1)
            for x in embedding(2):
                pass

        @block.scalar
        def _(e):
            own = [0]

            def mark(ins):
                own[0] += 1
                ins.then_inc(s("act_own"), 1)

            def link(ins):
                mark(ins)
                e.wait_ge(s("act_own"), own[0])

            def norm_squares(use, tiles, ready):
                for t in tiles:
                    R = ROWS[t]
                    n = NORMS[use, t]
                    sl = slot(t) if use != "ple" else t % 2
                    width = H_MLA * DV if use == "mix" else D
                    ready(t)
                    if n:
                        e.wait_ge(s("nt_transposed"), 4 * n)
                    if use == "ffn" and t != tiles[0]:
                        e.wait_ge(s("xn_stored"), 16 * t)
                    link(e.activation(Y[:R, 0:width], H[:R, sl, 0:width], ACT.Square, accum_out=st[:R, n:n + 1]))
                    e.activation(st[:R, ns + n:ns + n + 1], st[:R, n:n + 1], ACT.Sqrt, scale=1.0 / width, bias=eps[:R, :])\
                        .then_inc(s("rms_ready"), 1)
                    for q in range(4):
                        m = 4 * n + q
                        e.wait_ge(s("nt_transposed"), m + 1)
                        e.copy(XT[:, 4 * q:4 * q + 4, sl * P:sl * P + R], four(bank[6 + m % 2], R)).then_inc(s("nt_evacuated"), 1)

            def rms(out, ssq, width, R):
                return e.activation(out[:R], ssq[:R], ACT.Sqrt, scale=1.0 / width, bias=eps[:R, :])

            def pT_copy(m, t, h):
                u = m * HH + h
                e.wait_ge(s("pT_psum"), u + 1)
                if h >= 2:
                    e.wait_ge(s("pv_done"), u - 1)
                e.copy(pT[:, h % 2, 0:(t + 1) * P], bank[2 + h % 2][:, 0:(t + 1) * P]).then_inc(s("pT_sb"), 1)

            def mixer(g):
                tiles = GROUPS[g]
                nt = len(tiles)
                loaded = 3 * tiles[0]
                if g:
                    e.wait_ge(s("route_ready"), sum(1 for t, _, _ in ROUTES if t < tiles[0]))
                norm_squares("x", tiles, lambda t: e.wait_ge(s("rows_loaded"), 16 * (loaded + nt)))
                e.wait_ge(s("normed"), NORMS["x", tiles[-1]] + 1)
                yield
                for seg in range(IN_BLOCKS // 2 if g else 1):
                    for i in pairs(e, seg, seg + 1 if g else IN_BLOCKS // 2, g == 0):
                        for p in range(2):
                            e.wait_ge(s(f"z_stored{p}"), (i * (16 * nt)) + Z_BEFORE[g])
                            for sl, t in enumerate(tiles):
                                R = ROWS[t]
                                u = (i * 2 + p) * nt + sl
                                e.wait_ge(s("tiles_projected"), u + (PASSES[f"in{g}"][1] + 1))
                                zs = zst[:R, p * MT + sl, 0:IN_NC]
                                e.copy(zs, out_bank(p, sl)[:R, 0:IN_NC]).then_inc(s("z_read"), 1)
                                e.wait_ge(s("z_read"), u + (IN_READ[f"in{g}"] + 1))
                                e.dma_start(z_dram[rows(t), bass.ds((i * 2 + p) * IN_NC, IN_NC)], zs).then_inc(s(f"z_stored{p}"), 16)
                    yield
                for t in tiles:
                    R = ROWS[t]
                    e.wait_ge(s("mla_z_loaded"), 16 * (t + 1))
                    if t != tiles[0]:
                        e.wait_ge(s("rope_key_ready"), t)
                    mark(e.activation(sqs[:R, 0:QR], m_z[:R, 0:QR], ACT.Square, accum_out=SSQ[:R]))
                    mark(e.activation(QTn[:R, 0:2, :].rearrange("p a b -> p (a b)"), m_z[:R, QR:QR + KVR], ACT.Square, accum_out=SSC[:R]))
                    link(e.activation(QTr[:R, 0, 0:ROPE], m_z[:R, QR + KVR:MLA_COLS], ACT.Square, accum_out=SKR(t)[:R]))
                    rms(RQ, SSQ, QR, R)
                    rms(RC, SSC, KVR, R).then_inc(s("lat_rms"), 1)
                    e.wait_ge(s("lat_transposed"), t + 1)
                    e.copy(cqT[:, slot(t), :, 0:R], four(bank[0], R))
                    e.copy(cT[:, slot(t), :, 0:R], four(bank[1], R)[:, 0:2]).then_inc(s("latT_ready"), 1)
                yield
                for hh in range(2):
                    for t in tiles:
                        R = ROWS[t]
                        n = HALVES[hh, t]
                        e.wait_ge(s("q_ready"), n + 1)
                        if n:
                            e.wait_ge(s("ssq_done"), 2 * n)
                        for j in range(2):
                            ins = e.activation(sqs[:R, j * 2 * QK:(j + 1) * 2 * QK], bank[j][:R, 0:2 * QK], ACT.Square)
                        ins.then_inc(s("squares_ready"), 1)
                        e.wait_ge(s("ssq_done"), 2 * n + 1)
                        e.activation(RQH[:R], SQH[:R], ACT.Sqrt, scale=1.0 / QK, bias=eps[:R, :]).then_inc(s("q_rms"), 1)
                        e.wait_ge(s("k_ready"), n + 1)
                        e.activation(sqs[:R, 0:512], bank[2][:R, :], ACT.Square).then_inc(s("squares_ready"), 1)
                        e.wait_ge(s("ssq_done"), 2 * n + 2)
                        e.activation(RKH[:R], SKH[:R], ACT.Sqrt, scale=1.0 / QK, bias=eps[:R, :]).then_inc(s("k_rms"), 1)
                        if t == PT:
                            yield
                            continue
                        m = PHALVES[hh, t]
                        e.wait_ge(s("v_ready"), m + 1)
                        if m:
                            e.wait_ge(s("pv_done"), HH * m)
                        if g < LAST and hh and t == tiles[0]:
                            e.wait_ge(s("keys_parked"), 48 * (2 * g + 1))
                        e.copy(V[:, t, :], bank[3][:, :]).then_inc(s("v_sb"), 1)
                        e.wait_ge(s("qT_psum"), m + 1)
                        e.copy(QTn[:, :, :], four(bank[4]))
                        e.copy(QTr[:, :, :], four(bank[5])[:, 0:2]).then_inc(s("qT_sb"), 1)
                        nk = (t + 1) * P
                        for h in range(HH):
                            u = m * HH + h
                            e.wait_ge(s("neg_max"), u + 1)
                            if u >= 2:
                                e.wait_ge(s("pT_psum"), u - 1)
                            e.activation(pr[:, h % 2, 0:nk], bank[h % 2][:, 0:nk], ACT.Exp, scale=SCALE, bias=NMX[:, h:h + 1],
                                         accum_out=RSUM[:, h:h + 1]).then_inc(s("exp_done"), 1)
                            if h:
                                pT_copy(m, t, h - 1)
                        pT_copy(m, t, HH - 1)
                        yield
                if PT in tiles:
                    yield from sample()
                for t in tiles:
                    R = ROWS[t]
                    lv0 = 0 if t < PT else SAMPLE_LEVEL0
                    if t == tiles[0]:
                        e.wait_ge(s("gla_fills"), g + 1)
                    e.wait_ge(s("lrT_psum"), t + 1)
                    e.copy(alT[0:GATE_R, 0:R], bank[0][0:GATE_R, 0:R]).then_inc(s("lrT_sb"), 1)
                    e.wait_ge(s("gqkT_psum"), t + 1)
                    e.activation(heads(gqT, R), heads(bank[1], R), ACT.Copy, scale=float(GK) ** -0.5)
                    e.copy(heads(gkT, R), heads(bank[2], R)).then_inc(s("gqkT_sb"), 1)
                    e.wait_ge(s("gate_pre"), t + 1)
                    link(e.activation(gt1[:R, :], bank[3][:R, :], ACT.Abs))
                    link(e.activation(gt1[:R, :], gt1[:R, :], ACT.Exp, scale=-1.0))
                    e.activation(gt1[:R, :], gt1[:R, :], ACT.Ln, bias=1.0).then_inc(s("gate_ln"), 1)
                    for n in range(lv0, NLEV - 1):
                        v = level_count(t, n)
                        e.wait_ge(s("level_diff"), v + 1)
                        e.activation(heads(dlev[:, n % 2, :], R), heads(dlev[:, n % 2, :], R), ACT.Exp).then_inc(s("level_exp"), 1)
                    e.wait_ge(s("cum_sb"), t + 1)
                    e.activation(heads(eb, R), heads(gbT, R), ACT.Exp).then_inc(s("eb_ready"), 1)
                    e.wait_ge(s("kdiff"), t + 1)
                    e.activation(heads(kd, R), heads(kd, R), ACT.Exp).then_inc(s("kexp"), 1)
                    yield
                    e.wait_ge(s("kdr_psum"), t + 1)
                    e.copy(kdr[:R, :, :], bank[5][:R, :].rearrange("p (h n) -> p h n", h=H_GLA)).then_inc(s("kdr_sb"), 1)
                    if t != tiles[0]:
                        e.wait_ge(s("gla_o_ready"), t)
                    link(e.activation(gsil[:R, :], gz[:R, 2 * H_GLA * GK + 1024:2 * H_GLA * GK + 2048], ACT.Silu))
                    e.wait_ge(s("gla_o_sb"), t + 1)
                    for h in range(H_GLA):
                        mark(e.activation(gsq[:R, h * GV:(h + 1) * GV], go[:R, h * GV:(h + 1) * GV], ACT.Square,
                                          accum_out=GSS[:R, h:h + 1]))
                    e.wait_ge(s("act_own"), own[0])
                    e.activation(GRS[:R], GSS[:R], ACT.Sqrt, scale=1.0 / GV, bias=eps[:R, :]).then_inc(s("gla_rms"), 1)
                    e.sem_inc(s("gla_read"), 1)
                    yield
                norm_squares("mix", tiles, lambda t: e.wait_ge(s("rows_loaded"), 16 * (loaded + 2 * nt)))
                yield
                if g:
                    yield
                norm_squares("ffn", tiles, lambda t: e.wait_ge(s("rows_added"), ADDED[f"out{g}"] + (NBLK - 1) * nt + slot(t) + 1))
                e.wait_ge(s("h_stored"), 16 * (tiles[-1] + 1))
                yield
                yield from query_copies(g, 0, 2)

            def query_copies(g, lo, hi):
                ntok = sum(ROWS[t] for t in GROUPS[g])
                for n in range(2 * lo, 2 * hi):
                    side = n % 2
                    m = 2 * PH * g + n
                    e.wait_ge(s("tiles_projected"), PASSES[f"query{g}"][1] + n + 1)
                    if n >= 2:
                        e.wait_ge(s("key_scores"), m - 1)
                    e.copy(qTm[:, side, 0:ntok], bank[side][:, 0:ntok]).then_inc(s("qT_evacuated"), 1)
                    if n % 4 == 3:
                        yield

            def sample():
                for j in range(4):
                    e.wait_ge(s("sprep_psum"), j + 1)
                    e.copy(w_ukT[:, 2 * j:2 * j + 2, :].rearrange("p h n -> p (h n)"), bank[0][:, :]).then_inc(s("sprep_act"), 1)
                e.wait_ge(s("sprep_psum"), 5)
                e.copy(krT[0:ROPE, :], bank[1][0:ROPE, 0:NS]).then_inc(s("sprep_act"), 1)
                e.copy(ikx[:NS, :].rearrange("p (h t) -> p h t", t=DEC_T), IKH(PT)[:NS, :].unsqueeze(2).to_broadcast([NS, H_MLA, DEC_T]))\
                    .then_inc(s("sprep_act"), 1)
                e.wait_ge(s("sprep_psum"), 6)
                for k in range(2):
                    ins = e.copy(by_batch(q_lat[k]), bank[4 + k][:, :].rearrange("p (h b t) -> p h b t", h=H_MLA, b=DEC_B))
                ins.then_inc(s("sprep_act"), 1)
                yield
                for b in range(DEC_B):
                    e.wait_ge(s(f"pages_landed{b % 2}"), 16 * 3 * N_PAGES * (b // 2 + 1))
                    if b:
                        e.wait_ge(s("ir_psum"), 4 * b)
                    e.copy(ire.rearrange("p g (h t) -> p (g h) t", t=DEC_T),
                           pages_sb[b % 2][2].rearrange("p g h -> p (g h)").unsqueeze(2).to_broadcast([P, N_PAGES * H_MLA, DEC_T]))\
                        .then_inc(s("ire_ready"), 1)
                    for g in range(4):
                        u = 4 * b + g
                        e.wait_ge(s("latT_psum"), u + 1)
                        if u:
                            e.wait_ge(s("sscore_psum"), u)
                        e.copy(latT[:, 0, :], bank[0][:, :])
                        e.copy(latT[:, 1, :], bank[1][:, :])
                        e.copy(latT[0:ROPE, 2, :], bank[2][0:ROPE, :]).then_inc(s("latT_sb"), 1)
                        e.wait_ge(s("ir_psum"), u + 1)
                        if u:
                            e.wait_ge(s("scaled"), u)
                        e.copy(irs[:NS, :], bank[3][:NS, :]).then_inc(s("ir_sb"), 1)
                    e.wait_ge(s("sneg_max"), b + 1)
                    e.activation(sc[:NS, :], sc[:NS, :], ACT.Exp, scale=SCALE, bias=NMX[:NS, 0:1], accum_out=RSUM[:NS, 0:1])\
                        .then_inc(s("sexp_done"), 1)
                    for q in range(3):
                        v = 3 * b + q
                        n = 8 if q < 2 else 1
                        R = P if q < 2 else NS
                        e.wait_ge(s("spT_psum"), v + 1)
                        if b and q == 0:
                            e.wait_ge(s("olat_psum"), b)
                        e.copy(pTs[:R, 8 * q:8 * q + n, :].rearrange("p a b -> p (a b)"), bank[6][:R, 0:n * NS]).then_inc(s("spT_sb"), 1)
                    e.wait_ge(s("olatT_psum"), b + 1)
                    for k in range(2):
                        ins = e.copy(oT[k][:, :, b * DEC_T:(b + 1) * DEC_T],
                                     bank[7][:, 256 + k * NS:256 + (k + 1) * NS].rearrange("p (h t) -> p h t", h=H_MLA))
                    ins.then_inc(s("olatT_sb"), 1)
                    yield

            def route(t, lo, hi):
                R, nk = ROWS[t], (hi - lo) * TOPK
                e.wait_ge(s("gate_diff"), ROUTES.index((t, lo, hi)) + 1)
                e.activation(gtop[:R, 0:nk], gtop[:R, 0:nk], ACT.Exp).then_inc(s("gate_exp"), 1)
                yield

            def embedding(pg):
                tiles = PLE_GROUPS[pg]
                nt = len(tiles)
                if pg < 2:
                    norm_squares("ple", tiles, lambda t: e.wait_ge(s("rows_loaded"), 16 * (3 * T + tiles[-1] + 1)))
                else:
                    norm_squares("ple", tiles, lambda t: e.wait_ge(s("peer_done"), T))
                for t in tiles:
                    e.wait_ge(s("pT_ple_psum"), t + 1)
                    e.copy(pT_ple[:, :, (t % 2) * P:(t % 2) * P + ROWS[t]], four(bank[5], ROWS[t])[:, 0:2]).then_inc(s("pT_ple_sb"), 1)
                yield
                for i in pairs(e, 0, NBLK // 2, pg == 2):
                    for p in range(2):
                        for sl, t in enumerate(tiles):
                            R = ROWS[t]
                            u = (i * 2 + p) * nt + sl
                            x = (p * nt + sl) % 2
                            e.wait_ge(s("tiles_projected"), u + (PASSES[f"gate{pg}"][1] + 1))
                            e.wait_ge(s("rows_added"), u + (ADDED[f"gate{pg}"] - 1))
                            e.activation(sg[:R, x, :], out_bank(p, sl)[:R, 0:NC], ACT.Sigmoid).then_inc(s("sigmoid_ready"), 1)
                    if pg < 2:
                        yield

            def other_heads(g):
                for h in range(2, PH, 2):
                    yield from query_copies(g, h, h + 2)
                    yield from route(GROUPS[g][0], h, h + 2)

            def woven():
                yield from other_heads(0)
                for g in range(1, len(GROUPS)):
                    first = GROUPS[g][0]
                    yield from mixer(g)
                    yield from route(first, 0, 2)
                    yield from other_heads(g)
                    for t in GROUPS[g][1:]:
                        yield from route(t, 0, PH)
                for pg in range(2):
                    for x in embedding(pg):
                        yield

            e.wait_ge(s("fills_ready"), 1)
            e.sem_inc(s("z_read"), 4)
            e.sem_inc(s("z_stored0"), Z_BEFORE[0])
            e.sem_inc(s("z_stored1"), Z_BEFORE[0])
            e.wait_ge(s("keysT_psum"), 1)
            e.copy(keysT[:, :, :], four(bank[0])[:, 0:2]).then_inc(s("keysT_sb"), 1)
            for x in mixer(0):
                pass
            for x in route(0, 0, 2):
                pass

            def load_x(t):
                e.wait_ge(s("xn_stored"), 16 * (t + 1))
                if t < PT:
                    e.dma_start(xrow[:, t % 2, :], xn_dram[rows(t), :]).then_inc(s(f"xrow_loaded{t % 2}"), 16)
                else:
                    for r in range(2):
                        e.dma_start(xrow[r * NS:(r + 1) * NS, t % 2, :], xn_dram[rows(t), :]).then_inc(s(f"xrow_loaded{t % 2}"), 16)

            load_x(0)
            weave = woven()
            passed = [0]
            firsts = [tiles[0] for tiles in GROUPS]

            def segments_to(n):
                while passed[0] < n:
                    next(weave, None)
                    passed[0] += 1

            for t in range(T):
                for j, u in enumerate(range(FIRST_UNITS[t], FIRST_UNITS[t + 1])):
                    segments_to(segments_before[u])
                    if j == 0 and t and t in firsts:
                        load_x(t)
                    if j == 1 and t:
                        segments_to(segments_summed[t - 1])
                        e.wait_ge(s("peer_done"), t)
                        e.dma_start(h2_dram[rows(t - 1), :], xrow[:, (t - 1) % 2, :]).then_inc(s("h2_stored"), 16)
                    segments_to(segments_after[u])
                    e.wait_ge(s("dots_done"), (u + 1) * TOPK)
                    e.activation(gel[:, u % 2, :], dots[:, u % 2, :], ACT.Gelu).then_inc(s("gelu_ready"), 1)
                    if j == 1 and t:
                        e.wait_ge(s("h2_stored"), 16 * t)
                        if t + 1 < T and t + 1 not in firsts:
                            load_x(t + 1)
                    if u + 1 == FIRST_UNITS[t + 1]:
                        e.wait_ge(s("h_stored"), 16 * (t + 1))
                        e.dma_start(xrow[:ROWS[t], t % 2, :], h_dram[rows(t), :]).then_inc(s("h_loaded"), 16)
            for x in weave:
                pass
            e.wait_ge(s("sample_halves"), 1)
            e.dma_start(acc[0:NS, 1, :], acc[NS:P, 0, :]).then_inc(s("sample_back"), 16)
            for x in embedding(2):
                pass

        @block.gpsimd
        def _(e):
            def gathers(u, side, slot0, n, own=None):
                cur = idx_cur[:, side if own is None else own, :]
                e.wait_ge(s("buffers_free"), slot0 + 1)
                e.tensor_copy(cur, idx_all[:, bass.ds(u * TOPK, TOPK)]).then_inc(s("idx_ready"), 1)
                e.wait_ge(s("idx_ready"), n + 1)
                for k in range(TOPK):
                    e.wait_ge(s("buffers_free"), slot0 + (k + 1))
                    e.sem_inc(s("slots_granted"), 1)
                    e.indirect_dma_start(out=ring[:, k % RING, :], out_offset=None, in_=a[("peer_u", "peer_v")[side]][0],
                                         in_offset=bass.IndirectOffsetOnAxis(ap=cur[:, k:k + 1], axis=0))\
                        .then_inc(s(f"rows_landed{k % RING}"), 16)

            for n, (t, lo, hi) in enumerate(ROUTES):
                e.wait_ge(s("route_ready"), n + 1)
                if n == 0:
                    gathers(0, 0, first_slot(0, 0), 0, own=2)
                if t == PT:
                    e.wait_ge(s("sample_spread"), 32)
                with e.Fori(max(FIRST_UNITS[t] + lo, 1), min(FIRST_UNITS[t] + hi, UNITS)) as u:
                    gathers(u, 0, u * (2 * TOPK) - TOPK, u * 2 - 1)
                    gathers(u - 1, 1, u * (2 * TOPK), u * 2)
            gathers(UNITS - 1, 1, first_slot(UNITS - 1, 1), 2 * UNITS - 1, own=2)


_OUTS = [("y_p", (1, SEQ, D)), ("y_s", (DEC_B, DEC_T, D)), ("lat_p", (1, 1, SEQ, KVR)), ("kr_p", (1, 1, SEQ, ROPE)),
         ("ir_p", (1, 1, SEQ, H_MLA)), ("gla_p", (1, 1, H_GLA, GK, GV)), ("lat_s", (1, DEC_B, DEC_T, KVR)),
         ("kr_s", (1, DEC_B, DEC_T, ROPE)), ("ir_s", (1, DEC_B, DEC_T, H_MLA)), ("gla_s", (1, DEC_B, H_GLA, GK, GV))]


def kernel(**inputs):
    import concourse.bacc as bacc
    from concourse.bass_utils import run_bass_kernel_spmd

    nc = bacc.Bacc("TRN2", target_bir_lowering=False, num_devices=1)
    arrays, a, o, c = {}, {}, {}, {}
    for name, value in inputs.items():
        v = np.ascontiguousarray(value)
        arrays[f"in_{name}"] = v
        a[name] = nc.dram_tensor(f"in_{name}", v.shape, mybir.dt.from_np(v.dtype), kind="ExternalInput").ap()
    for name, v in constants().items():
        arrays[f"const_{name}"] = v
        c[name] = nc.dram_tensor(f"const_{name}", v.shape, F32, kind="ExternalInput").ap()
    for name, shape in _OUTS:
        o[name] = nc.dram_tensor(f"out_{name}", shape, F32, kind="ExternalOutput").ap()
    build(nc, a, o, c)
    r = run_bass_kernel_spmd(nc, [arrays], core_ids=[0])
    return tuple(r.results[0][f"out_{name}"] for name, _ in _OUTS)
```
